# Optimizing a Trainium2 kernel written in Bass

```python
import math
import jax, jax.numpy as jnp
from jax import lax
import numpy as np

D_MODEL = 1024
BATCH = 1
SEQ = 1024
DEPTH = 1
DEC_BATCH = 8
DEC_SEQ = 4
PAST_LEN = 256
PAGE_SIZE = 128

MIX_WIDTH = D_MODEL
ATTN_WIDTH = MIX_WIDTH // 2
REC_WIDTH = MIX_WIDTH - ATTN_WIDTH
A_HEADS = 4
A_HD = ATTN_WIDTH // (2 * A_HEADS)
A_VD = 2 * A_HD
R_HEADS = 4
R_DK = REC_WIDTH // R_HEADS
R_DV = REC_WIDTH // R_HEADS
REC_CHUNK = 64
N_BUCKETS = 32
MAX_DISTANCE = 128
D_FF = ((8 * D_MODEL // 3 + 127) // 128) * 128
CONV_W = 3
Q_BLOCK = 128
EPS = 1e-6
IN_COLS = 3 * ATTN_WIDTH + 4 * REC_WIDTH
SPLITS = [ATTN_WIDTH, 2 * ATTN_WIDTH, 3 * ATTN_WIDTH,
          3 * ATTN_WIDTH + REC_WIDTH, 3 * ATTN_WIDTH + 2 * REC_WIDTH, 3 * ATTN_WIDTH + 3 * REC_WIDTH]

kernel_name = 'hymba_diffattn_hgrn2_convglu_step'

def rms_norm(x, g):
    xf = x.astype(jnp.float32)
    y = xf * lax.rsqrt(jnp.mean(xf * xf, axis=-1, keepdims=True) + EPS)
    return (y * g.astype(jnp.float32)).astype(x.dtype)

def rel_bucket(q_pos, k_pos):
    n = jnp.maximum(q_pos[:, None] - k_pos[None, :], 0)
    max_exact = N_BUCKETS // 2
    nf = jnp.maximum(n, 1).astype(jnp.float32)
    large = max_exact + (jnp.log(nf / max_exact) / math.log(MAX_DISTANCE / max_exact)
                         * (N_BUCKETS - max_exact)).astype(jnp.int32)
    large = jnp.minimum(large, N_BUCKETS - 1)
    return jnp.where(n < max_exact, n, large)

def diff_attn_block(q, k, v, q_pos, k_pos, rel_bias, lam):
    s = jnp.einsum('bqhmd,bkhmd->bhmqk', q, k).astype(jnp.float32) * (A_HD ** -0.5)
    bias = jnp.transpose(rel_bias.astype(jnp.float32)[rel_bucket(q_pos, k_pos)], (2, 0, 1))
    mask = k_pos[None, :] <= q_pos[:, None]
    s = jnp.where(mask, s + bias[None, :, None], -jnp.inf)
    p = jax.nn.softmax(s, axis=-1)
    a = p[:, :, 0] - lam * p[:, :, 1]
    return jnp.einsum('bhqk,bkhv->bqhv', a.astype(v.dtype), v)

def attn_prompt(q, k, v, rel_bias, lam):
    B, T = q.shape[0], q.shape[1]
    nqb = T // Q_BLOCK
    pos = jnp.arange(T, dtype=jnp.int32)
    qb = jnp.moveaxis(q.reshape(B, nqb, Q_BLOCK, A_HEADS, 2, A_HD), 1, 0)
    pb = pos.reshape(nqb, Q_BLOCK)
    ob = lax.map(lambda a: diff_attn_block(a[0], k, v, a[1], pos, rel_bias, lam), (qb, pb))
    return jnp.moveaxis(ob, 0, 1).reshape(B, T, A_HEADS, A_VD)

def hgrn_chunk(S, q, logf, kk, v):
    L = q.shape[2]
    b = jnp.cumsum(logf, axis=2)
    causal = jnp.tril(jnp.ones((L, L), dtype=bool))
    diff = b[:, :, :, None, :] - b[:, :, None, :, :]
    dec = jnp.exp(jnp.where(causal[None, None, :, :, None], diff, -jnp.inf))
    A = jnp.einsum('bhtk,bhsk,bhtsk->bhts', q, kk, dec)
    o = jnp.einsum('bhts,bhsv->bhtv', A, v) + jnp.einsum('bhtk,bhkv->bhtv', q * jnp.exp(b), S)
    b_last = b[:, :, -1:, :]
    S_new = jnp.exp(b_last[:, :, 0, :])[..., None] * S + jnp.einsum('bhsk,bhsv->bhkv', kk * jnp.exp(b_last - b), v)
    return S_new, o

def hgrn_mixer(rq, rf, ri, rg, S0, lb, g_norm, chunk):
    B, T = rq.shape[0], rq.shape[1]
    f = lb + (1.0 - lb) * jax.nn.sigmoid(rf.astype(jnp.float32))
    logf = jnp.log(f)
    kk = 1.0 - f
    heads = lambda t: t.astype(jnp.float32).reshape(B, T, R_HEADS, -1).transpose(0, 2, 1, 3)
    nC = T // chunk
    to_chunks = lambda t: jnp.moveaxis(t.reshape(B, R_HEADS, nC, chunk, t.shape[-1]), 2, 0)
    xs = (to_chunks(heads(rq)), to_chunks(heads(logf)), to_chunks(heads(kk)), to_chunks(heads(ri)))
    S_fin, o = lax.scan(lambda S, a: hgrn_chunk(S, *a), S0.astype(jnp.float32), xs)
    o = jnp.moveaxis(o, 0, 2).reshape(B, R_HEADS, T, R_DV).transpose(0, 2, 1, 3)
    o = rms_norm(o, g_norm) * jax.nn.silu(rg.astype(jnp.float32).reshape(B, T, R_HEADS, R_DV))
    return o.reshape(B, T, REC_WIDTH).astype(rq.dtype), S_fin.astype(S0.dtype)

def project(h, w, qk_g):
    B, T = h.shape[0], h.shape[1]
    z = h @ w
    aq, ak, av, rq, rf, ri, rg = jnp.split(z, SPLITS, axis=-1)
    aq = rms_norm(aq.reshape(B, T, A_HEADS, 2, A_HD), qk_g[0])
    ak = rms_norm(ak.reshape(B, T, A_HEADS, 2, A_HD), qk_g[1])
    av = av.reshape(B, T, A_HEADS, A_VD)
    return aq, ak, av, rq, rf, ri, rg

def mixer_out(o_attn, o_rec, subln, lam_init, w_out):
    B, T = o_attn.shape[0], o_attn.shape[1]
    oa = (rms_norm(o_attn, subln) * (1.0 - lam_init)).reshape(B, T, ATTN_WIDTH)
    return jnp.concatenate([oa, o_rec.astype(oa.dtype)], axis=-1) @ w_out

def conv_ffn(h, buf, w_gate, w_up, conv_w, conv_b, w_down):
    T = h.shape[1]
    a = h @ w_gate
    ext = jnp.concatenate([buf.astype(a.dtype), a], axis=1)
    c = conv_b + sum(conv_w[j] * ext[:, j:j + T] for j in range(CONV_W))
    y = (jax.nn.silu(c) * (h @ w_up)) @ w_down
    return y, ext[:, -(CONV_W - 1):]

def setup_inputs(seed: int = 0) -> dict:
    key = jax.random.key(seed)
    ks = jax.random.split(key, 24)
    n_pages = PAST_LEN // PAGE_SIZE
    used = DEC_BATCH * n_pages
    n_phys = used + max(1, used // 4)
    nrm = lambda k, s, sc: jax.random.normal(k, s, jnp.float32) * sc
    page_table = jax.random.permutation(ks[0], n_phys)[:used].reshape(DEC_BATCH, n_pages).astype(jnp.int32)
    return {
        'x_prompt': nrm(ks[1], (BATCH, SEQ, D_MODEL), 1.0),
        'x_sample': nrm(ks[2], (DEC_BATCH, DEC_SEQ, D_MODEL), 1.0),
        'cache_k': nrm(ks[3], (DEPTH, n_phys, PAGE_SIZE, A_HEADS, 2, A_HD), 1.0),
        'cache_v': nrm(ks[4], (DEPTH, n_phys, PAGE_SIZE, A_HEADS, A_VD), 1.0),
        'page_table': page_table,
        'state_hgrn': nrm(ks[5], (DEPTH, DEC_BATCH, R_HEADS, R_DK, R_DV), 0.3),
        'state_conv': nrm(ks[6], (DEPTH, DEC_BATCH, CONV_W - 1, D_FF), 1.0),
        'rel_bias': nrm(ks[7], (N_BUCKETS, A_HEADS), 0.5),
        'norm1_g': 1.0 + nrm(ks[8], (DEPTH, D_MODEL), 0.02),
        'w_in': nrm(ks[9], (DEPTH, D_MODEL, IN_COLS), D_MODEL ** -0.5),
        'qk_norm_g': 1.0 + nrm(ks[10], (DEPTH, 2, 2, A_HD), 0.02),
        'lambda_qk': nrm(ks[11], (DEPTH, 4, A_HD), 0.1),
        'subln_g': 1.0 + nrm(ks[12], (DEPTH, A_VD), 0.02),
        'hgrn_lb': nrm(ks[13], (DEPTH + 1, REC_WIDTH), 0.1),
        'hgrn_onorm_g': 1.0 + nrm(ks[14], (DEPTH, R_DV), 0.02),
        'w_out': nrm(ks[15], (DEPTH, MIX_WIDTH, D_MODEL), MIX_WIDTH ** -0.5),
        'norm2_g': 1.0 + nrm(ks[16], (DEPTH, D_MODEL), 0.02),
        'w_gate': nrm(ks[17], (DEPTH, D_MODEL, D_FF), D_MODEL ** -0.5),
        'w_up': nrm(ks[18], (DEPTH, D_MODEL, D_FF), D_MODEL ** -0.5),
        'conv_w': nrm(ks[19], (DEPTH, CONV_W, D_FF), CONV_W ** -0.5),
        'conv_b': nrm(ks[20], (DEPTH, D_FF), 0.01),
        'w_down': nrm(ks[21], (DEPTH, D_FF, D_MODEL), D_FF ** -0.5),
    }

def reference(x_prompt, x_sample, cache_k, cache_v, page_table, state_hgrn, state_conv, rel_bias,
              norm1_g, w_in, qk_norm_g, lambda_qk, subln_g, hgrn_lb, hgrn_onorm_g, w_out,
              norm2_g, w_gate, w_up, conv_w, conv_b, w_down):
    xp, xs = x_prompt, x_sample
    Bp, Tp = xp.shape[0], xp.shape[1]
    Bs, Ts = xs.shape[0], xs.shape[1]
    past_len = page_table.shape[1] * cache_k.shape[2]
    lb_all = jnp.cumsum(jax.nn.softmax(hgrn_lb.astype(jnp.float32), axis=0), axis=0)
    kp_l, vp_l, hp_l, cp_l, ks_l, vs_l, hs_l, cs_l = [], [], [], [], [], [], [], []
    for l in range(DEPTH):
        lam_init = 0.8 - 0.6 * math.exp(-0.3 * l)
        lp = lambda_qk[l].astype(jnp.float32)
        lam = jnp.exp(jnp.sum(lp[0] * lp[1])) - jnp.exp(jnp.sum(lp[2] * lp[3])) + lam_init
        lb = lb_all[l]
        h = rms_norm(xp, norm1_g[l])
        aq, ak, av, rq, rf, ri, rg = project(h, w_in[l], qk_norm_g[l])
        o_att = attn_prompt(aq, ak, av, rel_bias, lam)
        s0 = jnp.zeros((Bp, R_HEADS, R_DK, R_DV), xp.dtype)
        o_rec, S_p = hgrn_mixer(rq, rf, ri, rg, s0, lb, hgrn_onorm_g[l], REC_CHUNK)
        xp = xp + mixer_out(o_att, o_rec, subln_g[l], lam_init, w_out[l])
        buf0 = jnp.zeros((Bp, CONV_W - 1, D_FF), xp.dtype)
        y, cbuf_p = conv_ffn(rms_norm(xp, norm2_g[l]), buf0, w_gate[l], w_up[l], conv_w[l], conv_b[l], w_down[l])
        xp = xp + y
        kp_l.append(ak); vp_l.append(av); hp_l.append(S_p); cp_l.append(cbuf_p)
        h = rms_norm(xs, norm1_g[l])
        aq, ak, av, rq, rf, ri, rg = project(h, w_in[l], qk_norm_g[l])
        past_k = cache_k[l][page_table].reshape(Bs, past_len, A_HEADS, 2, A_HD)
        past_v = cache_v[l][page_table].reshape(Bs, past_len, A_HEADS, A_VD)
        k_all = jnp.concatenate([past_k.astype(ak.dtype), ak], axis=1)
        v_all = jnp.concatenate([past_v.astype(av.dtype), av], axis=1)
        q_pos = past_len + jnp.arange(Ts, dtype=jnp.int32)
        k_pos = jnp.arange(past_len + Ts, dtype=jnp.int32)
        o_att = diff_attn_block(aq, k_all, v_all, q_pos, k_pos, rel_bias, lam)
        o_rec, S_s = hgrn_mixer(rq, rf, ri, rg, state_hgrn[l], lb, hgrn_onorm_g[l], Ts)
        xs = xs + mixer_out(o_att, o_rec, subln_g[l], lam_init, w_out[l])
        y, cbuf_s = conv_ffn(rms_norm(xs, norm2_g[l]), state_conv[l], w_gate[l], w_up[l], conv_w[l], conv_b[l], w_down[l])
        xs = xs + y
        ks_l.append(ak); vs_l.append(av); hs_l.append(S_s); cs_l.append(cbuf_s)
    return (xp, xs, jnp.stack(kp_l), jnp.stack(vp_l), jnp.stack(hp_l), jnp.stack(cp_l),
            jnp.stack(ks_l), jnp.stack(vs_l), jnp.stack(hs_l), jnp.stack(cs_l))


_drawn_inputs = setup_inputs


def setup_inputs(seed=0):
    import zlib

    import numpy as np

    out = dict(_drawn_inputs(seed))
    spreads = {}
    factors = {'qk_norm_g': 2.815,
     'subln_g': 5.941,
     'hgrn_onorm_g': 7.491,
     'norm2_g': 2.835,
     'conv_b': 8.0}
    for name, (base, spread) in spreads.items():
        noise = np.random.default_rng([zlib.crc32(name.encode()), seed]).standard_normal(out[name].shape)
        drawn = base * np.exp(spread * noise) if base else spread * noise
        out[name] = __import__('jax').numpy.asarray(drawn.astype(out[name].dtype))
    for name, factor in factors.items():
        out[name] = (out[name] * factor).astype(out[name].dtype)
    return out
```

```python
import math
from contextlib import ExitStack

import numpy as np
import concourse.bass as bass
from concourse import mybir

F32 = mybir.dt.float32
F32R = mybir.dt.float32r
I32 = mybir.dt.int32
ALU = mybir.AluOpType
ACT = mybir.ActivationFunctionType
AX = mybir.AxisListType

P = 128
D = 1024
KC = D // P
T = 1024
NB = 8
TS = 4
NS = NB * TS
TT = T + NS
NT = T // P
NPC = 3
PW = TT // NPC
H = 4
HD = 64
FW = H * P
PARTS = 7
FF = 2816
FC = FF // P
PAGE = 128
PAST = 256
EPS = 1e-6
MASKED = -1.0e30
LEVELS = 8
SLEVELS = 3
LAM_INIT = 0.8 - 0.6 * math.exp(0.0)
N_BUCKETS, MAX_DISTANCE = 32, 128
BW = 3 * P
NK = PAST + NS

W_SLOT = [0, 1, 0, 1, 0, 1, 2]
W_USES = [3, 3, 1]
W_NTH = [0, 0, 1, 1, 2, 2, 0]
W_BACK = [3, 3, 2, 2, 2, 2, 7]


VECTORS = {"norm1_g": (0, KC), "norm2_g": (8, KC), "conv_w": (16, 3 * FC), "conv_b": (82, FC), "qk_norm_g": (104, 2),
           "subln_g": (106, 1), "hgrn_onorm_g": (107, 1), "hgrn_lb": (108, 2 * H)}
NVEC = 116
TABLES = 18


def vector(keep, name):
    first, rows = VECTORS[name]
    return keep["vec"][:, first:first + rows]


def piece(n):
    return slice(n * PW, (n + 1) * PW)


class Chain:

    def __init__(self, sem):
        self.sem, self.n = sem, 0

    def of(self, eng):
        self.eng = eng
        return self

    def __call__(self, ins):
        ins.then_inc(self.sem, 1)
        self.n = self.n + 1
        self.eng.wait_ge(self.sem, self.n)

    def loop(self, count, per):
        return _ChainLoop(self, count, per)


class _ChainLoop:
    def __init__(self, chain, count, per):
        self.chain, self.count, self.per = chain, count, per

    def __enter__(self):
        self.start = self.chain.n
        self.fori = self.chain.eng.Fori(0, self.count)
        i = self.fori.__enter__()
        self.chain.n = 0
        self.base = i * self.per + self.start
        self.chain.n = self.base
        self.i = i
        return i

    def __exit__(self, *a):
        self.chain.n = self.start + self.count * self.per
        return self.fori.__exit__(*a)


def open_memory(nc, ctx):
    def sb(name, shape, dt=F32):
        return ctx.enter_context(nc.sbuf_tensor(name, shape, dt))

    def ps(name, shape):
        return ctx.enter_context(nc.psum_tensor(name, shape, F32))

    def sem(name):
        return ctx.enter_context(nc.semaphore(name))

    return sb, ps, sem


def prepare(nc, io, keep):
    with ExitStack() as ctx:
        sb, ps, sem = open_memory(nc, ctx)
        rel = sb("rel", [33, H])
        dist = sb("dist", [33, BW])
        sdist = sb("sdist", [33, TS, NK])
        relrow = sb("relrow", [33, H, P])
        selrow = sb("selrow", [33, TS, P])
        smask = sb("smask", [P, 2, NK])
        skew = sb("skew_rows", [P, H, BW])
        lq = sb("lq", [P, 4, HD])
        lprod = sb("lprod", [P, 2, HD])
        lsum = sb("lsum", [P, 2])
        lexp = sb("lexp", [P, 2])
        vrows = sb("vrows", [NVEC, P])
        lbm = sb("lbm", [P, H])
        lbe = sb("lbe", [P, 2, H])
        lbs = sb("lbs", [P, H])
        pb = ps("pb", [P, H, 512])
        psb = ps("psb", [P, 512])
        pvec = ps("pvec", [P, 512])
        lbr = keep["vec"][:, VECTORS["hgrn_lb"][0]:NVEC].rearrange("p (a h) -> p a h", a=2)
        gqk = vector(keep, "qk_norm_g")
        gsub = vector(keep, "subln_g")
        tables_in = sem("tables_in")
        rel_ready = sem("rel_ready")
        bias_ready = sem("bias_ready")
        vec_ready = sem("vec_ready")
        skew_ready = sem("skew_ready")
        skewed = sem("skewed")
        exp_ready = sem("exp_ready")
        exp_wanted = sem("exp_wanted")

        with nc.Block() as block:
            @block.sync
            def _(sp):
                sp.dma_start(rel[0:32, :], io["rel_bias"]).then_inc(tables_in, 16)
                sp.dma_start(dist[:, :], io["c_dist"]).then_inc(tables_in, 16)
                sp.dma_start(sdist[:, :, :], io["c_sdist"]).then_inc(tables_in, 16)
                sp.dma_start(smask[:, :, :], io["c_smask"]).then_inc(tables_in, 16)
                sp.dma_start(lq[:, :, :], io["lambda_qk"].broadcast_to([P, 4, HD])).then_inc(tables_in, 16)
                sp.dma_start(keep["ident"][:, :], io["c_ident"]).then_inc(tables_in, 16)
                sp.dma_start(keep["blk"][:, :], io["c_blk"]).then_inc(tables_in, 16)
                sp.dma_start(keep["lmask"][:, :, :], io["c_lmask"]).then_inc(tables_in, 16)
                sp.dma_start(keep["rowmask"][:, :], io["c_rowmask"]).then_inc(tables_in, 16)
                sp.dma_start(keep["rowsel"][:, :], io["c_rowsel"]).then_inc(tables_in, 16)
                for name, view in (("norm1_g", "o (k p) -> (o k) p"), ("norm2_g", "o (k p) -> (o k) p"), ("conv_w", "o j (c p) -> (o j c) p"),
                                   ("conv_b", "o (c p) -> (o c) p"), ("qk_norm_g", "o a m d -> (o a) (m d)"), ("subln_g", "o p -> o p"),
                                   ("hgrn_onorm_g", "o p -> o p"), ("hgrn_lb", "a (h p) -> (a h) p")):
                    first, rows = VECTORS[name]
                    src = io[name] if view == "o p -> o p" else io[name].rearrange(view, **({"p": P} if "(k p)" in view or "(c p)" in view or "(h p)" in view else {}))
                    sp.dma_start(vrows[first:first + rows, :], src).then_inc(tables_in, 16)
                sp.wait_ge(skew_ready, H)
                sp.dma_start(io["skew"].rearrange("h p w -> p h w"), skew[:, :, :]).then_inc(skewed, 16)
                sp.wait_ge(skewed, 16)
                for h in range(H):
                    flat = io["skew"][h].rearrange("p w -> (p w)")
                    shifted = flat[P - 1:P - 1 + P * (BW - 1)].rearrange("(p w) -> p w", w=BW - 1)
                    sp.dma_start(keep["bias"][:, h, :], shifted[:, 0:2 * P]).then_inc(skewed, 16)
                sp.wait_ge(skewed, 16 * (H + 1))

            @block.vector
            def _(dve):
                link = keep["dve_chain"].of(dve)
                v = nc.vector
                v.memset(keep["ones"][:, :], 1.0)
                v.memset(keep["eps"][:, :], EPS)
                v.memset(selrow[:, :, :], 0.0)
                link(v.memset(rel[32:33, :], MASKED))
                dve.wait_ge(tables_in, 16 * TABLES)
                v.tensor_copy(relrow[:, :, :], rel[:, :].rearrange("p (h o) -> p h o", o=1).broadcast_to([33, H, P])).then_inc(rel_ready, 1)
                for t in range(TS):
                    for b in range(4):
                        out = selrow[:, t, 32 * b:32 * b + 32].rearrange("p (h m t) -> p h m t", h=H, m=2)[:, :, :, t]
                        src = rel[:, :].rearrange("p (h o) -> p h o", o=1).broadcast_to([33, H, 2])
                        v.tensor_copy(out, src).then_inc(rel_ready, 1)
                dve.wait_ge(vec_ready, 1)
                link(v.tensor_copy(keep["vec"][:, :], pvec[:, 0:NVEC]))
                link(v.tensor_tensor(lprod[:, :, :], lq[:, 0:4:2, :], lq[:, 1:4:2, :], ALU.mult))
                v.tensor_reduce(lsum[:, :], lprod[:, :, :], AX.X, ALU.add).then_inc(exp_wanted, 1)
                link(v.tensor_tensor(lbm[:, :], lbr[:, 0, :], lbr[:, 1, :], ALU.max))
                for a in range(2):
                    last = v.tensor_tensor(lbr[:, a, :], lbr[:, a, :], lbm[:, :], ALU.subtract)
                last.then_inc(exp_wanted, 1)
                dve.wait_ge(exp_ready, 1)
                link(v.tensor_tensor(lsum[:, 0:1], lexp[:, 0:1], lexp[:, 1:2], ALU.subtract))
                link(v.tensor_scalar(keep["lam"][:, 0:1], lsum[:, 0:1], LAM_INIT, None, ALU.add))
                link(v.tensor_scalar(keep["lam"][:, 1:2], keep["lam"][:, 0:1], -1.0, None, ALU.mult))
                dve.wait_ge(exp_ready, 2)
                link(v.tensor_tensor(lbs[:, :], lbe[:, 0, :], lbe[:, 1, :], ALU.add))
                link(v.reciprocal(lbm[:, :], lbs[:, :]))
                link(v.tensor_tensor(keep["lb0"][:, :], lbe[:, 0, :], lbm[:, :], ALU.mult))
                link(v.tensor_scalar(keep["lb1"][:, :], keep["lb0"][:, :], -1.0, 1.0, ALU.mult, ALU.add))
                link(v.tensor_scalar(gqk[:, 0:1], gqk[:, 0:1], HD ** -0.5, None, ALU.mult))
                link(v.tensor_scalar(gsub, gsub, 1.0 - LAM_INIT, None, ALU.mult))
                for h in range(H):
                    dve.wait_ge(bias_ready, h + 1)
                    v.tensor_copy(skew[:, h, :], pb[:, h, 0:BW]).then_inc(skew_ready, 1)
                    link(v.tensor_copy(keep["far"][:, h:h + 1], pb[:, h, 0:1]))
                dve.wait_ge(bias_ready, H + 1)
                for g in range(2):
                    link(v.tensor_tensor(keep["sbias"][:, g, :], psb[:, 0:NK], smask[:, g, :], ALU.add))

            @block.scalar
            def _(act):
                act.wait_ge(exp_wanted, 1)
                nc.scalar.activation(lexp[:, :], lsum[:, :], ACT.Exp).then_inc(exp_ready, 1)
                act.wait_ge(exp_wanted, 2)
                nc.scalar.activation(lbe[:, :, :], lbr[:, :, :], ACT.Exp).then_inc(exp_ready, 1)

            @block.tensor
            def _(pe):
                pe.wait_ge(tables_in, 16 * TABLES)
                nc.tensor.transpose(pvec[:, 0:NVEC], vrows[:, :], keep["ident"][0:NVEC, 0:NVEC]).then_inc(vec_ready, 1)
                pe.wait_ge(rel_ready, 1)
                for h in range(H):
                    nc.tensor.matmul(pb[:, h, 0:BW], relrow[:, h, :], dist[:, :], start=True, stop=True).then_inc(bias_ready, 1)
                pe.wait_ge(rel_ready, 1 + 4 * TS)
                for t in range(TS):
                    last = nc.tensor.matmul(psb[:, 0:NK], selrow[:, t, :], sdist[:, t, :], start=(t == 0), stop=(t == TS - 1))
                last.then_inc(bias_ready, 1)


def split_weights(nc, ones, raw, hi, lo, link):
    link(nc.gpsimd.tensor_tensor(hi, raw, ones.rearrange("p (o c) -> p o c", o=1).broadcast_to(list(raw.shape)), ALU.mult))
    return nc.gpsimd.tensor_tensor(lo, raw, hi.bitcast(F32), ALU.subtract)


def split_product(nc, out, whi, wlo, hi, lo):
    chunks = hi.shape[1]
    for k in range(chunks):
        nc.tensor.matmul(out, whi[:, k, :], hi[:, k, :], start=(k == 0), stop=False)
        nc.tensor.matmul(out, whi[:, k, :], lo[:, k, :], start=False, stop=False)
        last = nc.tensor.matmul(out, wlo[:, k, :], hi[:, k, :], start=False, stop=(k == chunks - 1))
    return last



def norm_squares(nc, act, src, sq, sq_ready, sq_used):
    for k in range(KC):
        if k >= 2:
            act.wait_ge(sq_used, k - 1)
        nc.scalar.activation(sq[:, k % 2, :], src[:, k, :], ACT.Square).then_inc(sq_ready, 1)


def norm_sums(nc, pe, ones, sq, ms, sq_ready, sq_used, ms_ready):
    for k in range(KC):
        pe.wait_ge(sq_ready, k + 1)
        for n in range(NPC):
            last = nc.tensor.matmul(ms[n][:, 0:PW], ones[:, :], sq[:, k % 2, piece(n)], start=(k == 0), stop=(k == KC - 1))
            if k == KC - 1:
                last.then_inc(ms_ready, 1)
        if k < KC - 1:
            last.then_inc(sq_used, 1)


def norm_inverse(nc, act, eps, ms, rb, lnb, ms_ready, rb_ready, link):
    for n in range(NPC):
        if n:
            act.wait_ge(rb_ready, n)
        act.wait_ge(ms_ready, n + 1)
        link(nc.scalar.activation(lnb[:, :], ms[n][:, 0:PW], ACT.Ln, bias=eps[:, 0:1], scale=1.0 / D))
        nc.scalar.activation(rb[:, piece(n)], lnb[:, :], ACT.Exp, scale=-0.5).then_inc(rb_ready, 1)


def norm_high(nc, act, hf, hh, hf_ready, hi_ready):
    for n in range(NPC):
        for k in range(KC):
            j = n * KC + k
            act.wait_ge(hf_ready, j + 1)
            nc.scalar.activation(hh[:, k, piece(n)], hf[:, j % NPC, :], ACT.Copy).then_inc(hi_ready, 1)


def norm_low(nc, dve, src, gain, rb, hf, hh, hl, rb_ready, hf_ready, hi_ready, lo_ready):
    steps = [(n, k) for n in range(NPC) for k in range(KC)]

    def low(j):
        n, k = steps[j]
        dve.wait_ge(hi_ready, j + 1)
        nc.vector.tensor_tensor(hl[:, k, piece(n)], hf[:, j % NPC, :], hh[:, k, piece(n)].bitcast(F32), ALU.subtract).then_inc(lo_ready, 1)

    for j, (n, k) in enumerate(steps):
        if k == 0:
            dve.wait_ge(rb_ready, n + 1)
        if j >= NPC:
            dve.wait_ge(lo_ready, j - NPC + 1)
        nc.vector.scalar_tensor_tensor(hf[:, j % NPC, :], src[:, k, piece(n)], gain[:, k:k + 1], rb[:, piece(n)], ALU.mult, ALU.mult)\
          .then_inc(hf_ready, 1)
        if j:
            low(j - 1)
    low(len(steps) - 1)


def project(nc, io, keep):
    with ExitStack() as ctx:
        sb, ps, sem = open_memory(nc, ctx)
        xT = sb("xT", [P, KC, TT])
        hh = sb("h_hi", [P, KC, TT], F32R)
        hl = sb("h_lo", [P, KC, TT], F32R)
        raw = sb("w_raw", [P, 3, KC, P])
        whi = [sb(f"w_hi{s}", [P, KC, P], F32R) for s in range(3)]
        wlo = [sb(f"w_lo{s}", [P, KC, P], F32R) for s in range(3)]
        ZQ, ZK, ZV, ZRQ, ZRF, ZRI, ZRG = [sb(f"z_{n}", [P, TT]) for n in ("q", "k", "v", "rq", "rf", "ri", "rg")]
        tm = sb("tm", [P, 3, NT + 1, P])
        sq = sb("sq", [P, 2, TT])
        rb = sb("rb", [P, 2, TT])
        lnb = sb("lnb", [P, PW])
        hf = rb[:, 1, :].rearrange("p (s w) -> p s w", s=NPC)
        zp = [ps(f"z_ps{n}", [P, 512]) for n in range(NPC)]
        ms = [ps(f"ms_ps{n}", [P, 512]) for n in range(NPC)]
        tr = [ps(f"tr_ps{n}", [P, 512]) for n in range(2)]

        x_in = [sem(f"x_in{s}") for s in range(3)]
        x_tr = [sem(f"x_tr{b}") for b in range(2)]
        x_ev = [sem(f"x_ev{b}") for b in range(2)]
        sq_ready = sem("sq_ready")
        ms_ready = sem("ms_ready")
        sq_used = sem("sq_used")
        rb_ready = sem("rb_ready")
        hf_ready = sem("hf_ready")
        hi_ready = sem("hi_ready")
        lo_ready = sem("lo_ready")
        raw_in = [sem(f"raw_in{s}") for s in range(3)]
        w_ready = sem("w_ready")
        z_ready = sem("z_ready")
        z_free = sem("z_free")
        qk_ms = sem("qk_ms")
        qk_rb = sem("qk_rb")
        qk_normed = sem("qk_normed")
        tr_ready = [sem(f"tr_ready{b}") for b in range(2)]
        tr_free = [sem(f"tr_free{b}") for b in range(2)]
        f_ready = sem("f_ready")
        NAMES = ("q", "k", "kt", "v", "rq", "f", "ri", "rg")
        STORES = {n: 32 if n in ("kt", "v", "ri") else 16 for n in NAMES}
        stored = {n: sem(f"stored_{n}") for n in NAMES}
        x_stored = sem("x_stored")

        w_view = io["w_in"][0].rearrange("(k p) (t h c) -> p t k h c", p=P, t=PARTS, h=H)
        W0, Z0, F0, R0, N0 = PARTS, NPC * PARTS, NPC, 1, 2 * NPC

        def split_at(h, c):
            return h * PARTS + (W0 + c)

        def summed(h, c, n):
            return h * (NPC * PARTS) + (Z0 + NPC * c + n + 1)

        def copied(h, c, n):
            return h * (NPC * PARTS) + (F0 + NPC * c + n + 1)

        def normed(h, i):
            return h * (2 * NPC) + (N0 + NPC * i + NPC)

        def token_major(h, i):
            return h * 6 + (R0 + 2 * i + 2)

        with nc.Block() as block:
            @block.sync
            def _(sp):
                for s, n in ((w_ready, W0), (z_ready, Z0), (z_free, F0), (tr_free[0], R0), (tr_free[1], R0), (qk_normed, N0), (qk_rb, N0)):
                    sp.sem_inc(s, n)
                for n in NAMES:
                    sp.sem_inc(stored[n], STORES[n])
                for t in range(NT + 1):
                    rows = P if t < NT else NS
                    if t >= 3:
                        sp.wait_ge(x_tr[1], t - 2)
                    src = io["x_prompt"][0, t * P:(t + 1) * P, :] if t < NT else io["x_sample"].rearrange("b t d -> (b t) d")
                    sp.dma_start(tm[0:rows, t % 3, 0:KC, :].rearrange("p k c -> p (k c)"), src).then_inc(x_in[t % 3], 16)
                sp.wait_ge(x_ev[0], NT + 1)
                sp.wait_ge(x_ev[1], NT + 1)
                sp.dma_start(io["x_d"], xT[:, :, :]).then_inc(x_stored, 16)
                with sp.Fori(0, H) as h:
                    def load(c):
                        sp.wait_ge(w_ready, split_at(h, c) - (W_BACK[c] - 1))
                        sp.dma_start(raw[:, W_SLOT[c], :, :], w_view[:, c, :, bass.ds(h, 1), :].rearrange("p k o c -> p k (o c)"))\
                          .then_inc(raw_in[W_SLOT[c]], 16)

                    def store(name, src, ready, value):
                        sp.wait_ge(ready, value)
                        sp.dma_start(io[name + "_d"][bass.ds(h, 1)].rearrange("o p t -> p (o t)"), src[:, :]).then_inc(stored[name], 16)

                    def store_tokens(name, prompt, sample, i):
                        sp.wait_ge(tr_free[0], token_major(h, i))
                        sp.dma_start(prompt.rearrange("(t p) h c -> h p t c", p=P)[bass.ds(h, 1)].rearrange("o p t c -> p (o t) c"),
                                     tm[:, i, 0:NT, :]).then_inc(stored[name], 16)
                        sp.dma_start(sample.rearrange("t h c -> h t c")[bass.ds(h, 1)].rearrange("o t c -> t (o c)"),
                                     tm[0:NS, i, NT, :]).then_inc(stored[name], 16)

                    load(0)
                    load(1)
                    load(2)
                    load(3)
                    store("q", ZQ, qk_normed, normed(h, 0))
                    load(4)
                    store("k", ZK, qk_normed, normed(h, 1))
                    load(5)
                    store_tokens("kt", io["k_prompt"], io["k_sample"], 0)
                    store("rq", ZRQ, z_free, copied(h, 3, NPC - 1))
                    store_tokens("v", io["v_prompt"], io["v_sample"], 1)
                    load(6)
                for n in ("q", "k", "kt", "v", "rq"):
                    sp.wait_ge(stored[n], STORES[n] * (H + 1))
                sp.wait_ge(x_stored, 16)

            @block.gpsimd
            def _(pool):
                link = keep["pool_chain"].of(pool)
                with link.loop(H, PARTS) as h:
                    for c in range(PARTS):
                        s = W_SLOT[c]
                        pool.wait_ge(raw_in[s], h * (16 * W_USES[s]) + 16 * (W_NTH[c] + 1))
                        pool.wait_ge(z_ready, h * (NPC * PARTS) + (Z0 + NPC * (c - W_BACK[c] + 1)))
                        split_weights(nc, keep["ones"][:, :], raw[:, s, :, :], whi[s][:, :, :], wlo[s][:, :, :], link).then_inc(w_ready, 1)

            @block.tensor
            def _(pe):
                for t in range(NT + 1):
                    rows = P if t < NT else NS
                    pe.wait_ge(x_in[t % 3], 16 * (t // 3 + 1))
                    for half in range(2):
                        if t:
                            pe.wait_ge(x_ev[half], t)
                        for j in range(4):
                            last = nc.tensor.transpose(tr[half][:, j * P:j * P + rows], tm[0:rows, t % 3, half * 4 + j, :], keep["ident"][0:rows, 0:rows])
                        last.then_inc(x_tr[half], 1)
                norm_sums(nc, pe, keep["ones"], sq, ms, sq_ready, sq_used, ms_ready)

                with pe.Fori(0, H) as h:
                    def main(c, n):
                        s = W_SLOT[c]
                        if n == 0:
                            pe.wait_ge(w_ready, split_at(h, c) + 1)
                        if c == 0:
                            pe.wait_ge(lo_ready, KC * (n + 1))
                        pe.wait_ge(z_free, copied(h, c, n) - NPC)
                        split_product(nc, zp[n][:, 0:PW], whi[s], wlo[s], hh[:, :, piece(n)], hl[:, :, piece(n)]).then_inc(z_ready, 1)

                    def sums(i):
                        for n in range(NPC):
                            pe.wait_ge(z_free, copied(h, i, n))
                            if i:
                                pe.wait_ge(qk_rb, h * (2 * NPC) + (N0 + n + 1))
                            nc.tensor.matmul(ms[n][:, 0:PW], keep["blk"][:, :], sq[:, i, piece(n)], start=True, stop=True).then_inc(qk_ms, 1)

                    def tokens(i, src, ready, value):
                        pe.wait_ge(ready, value)
                        for b, first, end, use in ((0, 0, 4, 2 * i), (1, 4, 8, i), (0, 8, 9, 2 * i + 1)):
                            pe.wait_ge(tr_free[b], h * (6, 3)[b] + (use + R0))
                            for t in range(first, end):
                                rows = P if t < NT else NS
                                last = nc.tensor.transpose(tr[b][0:rows, (t - first) * P:(t - first + 1) * P], src[:, t * P:t * P + rows], keep["ident"][:, :])
                            last.then_inc(tr_ready[b], 1)

                    main(0, 0), main(0, 1), main(0, 2)
                    main(1, 0), sums(0), main(1, 1), main(1, 2)
                    main(2, 0), sums(1), main(2, 1), main(2, 2)
                    main(3, 0), tokens(0, ZK, qk_normed, normed(h, 1)), main(3, 1)
                    tokens(1, ZV, z_free, copied(h, 2, NPC - 1)), main(3, 2)
                    main(4, 0), main(4, 1), main(4, 2)
                    main(5, 0), main(5, 1), main(5, 2)
                    main(6, 0), tokens(2, ZRI, z_free, copied(h, 5, NPC - 1)), main(6, 1), main(6, 2)

            @block.scalar
            def _(act):
                a = nc.scalar.activation
                link = keep["act_chain"].of(act)
                for t in range(NT + 1):
                    rows = P if t < NT else NS
                    act.wait_ge(x_tr[1], t + 1)
                    a(xT[:, 4:8, t * P:t * P + rows], tr[1][:, :].rearrange("p (k c) -> p k c", k=4)[:, :, 0:rows], ACT.Copy).then_inc(x_ev[1], 1)
                act.wait_ge(x_ev[0], NT + 1)
                act.wait_ge(x_ev[1], NT + 1)
                norm_squares(nc, act, xT, sq, sq_ready, sq_used)
                norm_inverse(nc, act, keep["eps"], ms, rb[:, 0, :], lnb, ms_ready, rb_ready, link)
                norm_high(nc, act, hf, hh, hf_ready, hi_ready)

                with link.loop(H, 2 * NPC) as h:
                    def free(name):
                        act.wait_ge(stored[name], h * STORES[name] + STORES[name])

                    def copy(c, n, dst, func=ACT.Copy):
                        act.wait_ge(z_ready, summed(h, c, n))
                        return a(dst[:, piece(n)], zp[n][:, 0:PW], func)

                    def squared(c, n, dst):
                        copy(c, n, dst)
                        a(sq[:, c, piece(n)], zp[n][:, 0:PW], ACT.Square).then_inc(z_free, 1)

                    def inverse(i):
                        for n in range(NPC):
                            act.wait_ge(qk_rb, h * (2 * NPC) + (N0 + NPC * i + n))
                            act.wait_ge(qk_ms, h * (2 * NPC) + (NPC * i + n + 1))
                            link(a(lnb[:, :], ms[n][:, 0:PW], ACT.Ln, bias=keep["eps"][:, 0:1], scale=1.0 / HD))
                            a(rb[:, i, piece(n)], lnb[:, :], ACT.Exp, scale=-0.5).then_inc(qk_rb, 1)

                    free("q")
                    for n in range(NPC):
                        squared(0, n, ZQ)
                    free("k")
                    squared(1, 0, ZK)
                    inverse(0)
                    squared(1, 1, ZK), squared(1, 2, ZK)
                    free("v")
                    copy(2, 0, ZV).then_inc(z_free, 1)
                    inverse(1)
                    copy(2, 1, ZV).then_inc(z_free, 1), copy(2, 2, ZV).then_inc(z_free, 1)
                    free("rq")
                    for n in range(NPC):
                        copy(3, n, ZRQ).then_inc(z_free, 1)
                    free("f")
                    for n in range(NPC):
                        copy(4, n, ZRF, ACT.Sigmoid).then_inc(z_free, 1)
                    free("ri")
                    for n in range(NPC):
                        copy(5, n, ZRI).then_inc(z_free, 1)
                    free("rg")
                    for n in range(NPC):
                        copy(6, n, ZRG, ACT.Silu).then_inc(z_free, 1)
                    act.wait_ge(f_ready, h + 1)
                    act.dma_start(io["f_d"][bass.ds(h, 1)].rearrange("o p t -> p (o t)"), ZRF[:, :]).then_inc(stored["f"], 16)
                    act.wait_ge(tr_free[0], token_major(h, 2))
                    act.dma_start(io["ri_d"][bass.ds(h, 1)].rearrange("o p t c -> p (o t) c")[:, 0:NT, :], tm[:, 2, 0:NT, :]).then_inc(stored["ri"], 16)
                    act.dma_start(io["ri_d"][bass.ds(h, 1)].rearrange("o p t c -> p (o t) c")[0:NS, NT, :], tm[0:NS, 2, NT, :]).then_inc(stored["ri"], 16)
                    act.wait_ge(z_free, copied(h, 6, NPC - 1))
                    act.dma_start(io["rg_d"][bass.ds(h, 1)].rearrange("o p t -> p (o t)"), ZRG[:, :]).then_inc(stored["rg"], 16)
                for n in ("f", "ri", "rg"):
                    act.wait_ge(stored[n], STORES[n] * (H + 1))

            @block.vector
            def _(dve):
                v = nc.vector
                for t in range(NT + 1):
                    rows = P if t < NT else NS
                    dve.wait_ge(x_tr[0], t + 1)
                    v.tensor_copy(xT[:, 0:4, t * P:t * P + rows], tr[0][:, :].rearrange("p (k c) -> p k c", k=4)[:, :, 0:rows]).then_inc(x_ev[0], 1)
                dve.wait_ge(x_ev[1], NT + 1)
                norm_low(nc, dve, xT, vector(keep, "norm1_g"), rb[:, 0, :], hf, hh, hl, rb_ready, hf_ready, hi_ready, lo_ready)

                with dve.Fori(0, H) as h:
                    def scale(i, z):
                        for n in range(NPC):
                            dve.wait_ge(qk_rb, h * (2 * NPC) + (N0 + NPC * i + n + 1))
                            v.scalar_tensor_tensor(z[:, piece(n)], z[:, piece(n)], vector(keep, "qk_norm_g")[:, i:i + 1], rb[:, i, piece(n)],
                                                   ALU.mult, ALU.mult).then_inc(qk_normed, 1)

                    def tokens(i, name):
                        dve.wait_ge(stored[name], h * STORES[name] + STORES[name])
                        for b, first, end, use in ((0, 0, 4, 2 * i), (1, 4, 8, i), (0, 8, 9, 2 * i + 1)):
                            dve.wait_ge(tr_ready[b], h * (6, 3)[b] + (use + 1))
                            rows = P if first < NT else NS
                            v.tensor_copy(tm[0:rows, i, first:end, :].rearrange("p t c -> p (t c)"), tr[b][0:rows, 0:(end - first) * P]).then_inc(tr_free[b], 1)

                    scale(0, ZQ)
                    scale(1, ZK)
                    tokens(0, "kt")
                    tokens(1, "v")
                    dve.wait_ge(z_free, copied(h, 4, NPC - 1))
                    v.tensor_scalar(ZRF[:, :], ZRF[:, :], keep["lb1"][:, bass.ds(h, 1)], keep["lb0"][:, bass.ds(h, 1)], ALU.mult, ALU.add).then_inc(f_ready, 1)
                    tokens(2, "ri")


G_USE = {0: 0, 1: 2, 2: 4, 3: 7, 4: 9, 5: 11, 6: 13, 7: 15}
SG_USE, KD_USE, U_USE, SU_USE, O_USE, SO_USE = 6, 17, 20, 22, 24, 26
REC_USES = 27
REC_PER = (14, 13)
REC_SLOT = [(), (0, 1, 2), (3, 4, 5, 6), (7, 8), (9, 10, 11, 12), (13, 14, 15, 16), (17, 18, 19, 20), (21, 22, 23), (24, 25, 26)]
T_GROUPS = [(i + 4) // 4 for i in range(NT)]
T_FIRST = [sum(T_GROUPS[:i]) for i in range(NT)]
T_PER = sum(T_GROUPS)


def blocks_of(x, w, n):
    return x[:, 0:n].rearrange("p (b s w) -> p b s w", s=2, w=w // 2)


def heads(nc, io, keep):
    with ExitStack() as ctx:
        sb, ps, sem = open_memory(nc, ctx)
        Q = [sb(f"q{p}", [P, T]) for p in range(2)]
        K = [sb(f"k{p}", [P, T]) for p in range(2)]
        V = [sb(f"v{p}", [P, NT, P]) for p in range(2)]
        RQ = [sb(f"rq{p}", [P, TT]) for p in range(2)]
        F = [sb(f"f{p}", [P, TT]) for p in range(2)]
        RI = [sb(f"ri{p}", [P, NT + 1, P]) for p in range(2)]
        OA = [sb(f"oa{p}", [P, T]) for p in range(2)]
        OR = [sb(f"or{p}", [P, TT]) for p in range(2)]
        gates = sb("gates", [1, 2 * LEVELS + SLEVELS])
        near = sb("near", [P, 2, 2 * P])
        E = sb("E", [P, 2, T])
        A = [sb(f"A{p}", [P, T]) for p in range(2)]
        At = [sb(f"At{p}", [P, T]) for p in range(2)]
        mx = sb("mx", [P, 2, 2])
        negm = sb("negm", [P, 2])
        farb = sb("farb", [P, 2])
        ls = sb("ls", [P, 2, 2])
        lt = sb("lt", [P, 2])
        rl = sb("rl", [P, 2])
        c1 = sb("c1", [P, 1])
        LF = sb("LF", [P, TT])
        resets = sb("resets", [P, TT])
        b = sb("b", [P, TT])
        KK = sb("KK", [P, TT])
        EB = sb("EB", [P, TT])
        KD = sb("KD", [P, TT])
        QD = sb("QD", [P, TT])
        X = [sb(f"X{p}", [P, TT]) for p in range(2)]
        KDT = sb("KDT", [P, NT + 1, P])
        KDM = sb("KDM", [NS, NB, P])
        AT = sb("AT", [P, NT, P])
        ATS = sb("ATS", [NS, NS])
        ST = sb("ST", [P, NT + 1, P])
        SIN = sb("SIN", [P, NB, P])
        SOUT = sb("SOUT", [P, NB, P])
        S = ps("S", [P, 2, T])
        trp = ps("trp", [P, 512])
        pvp = ps("pvp", [P, 512])
        rec = [ps(f"rec{p}", [P, 512]) for p in range(2)]

        loaded = [sem(f"loaded{p}") for p in range(2)]
        states_in = sem("states_in")
        s_ready = sem("s_ready")
        small = sem("small")
        mx_ready = sem("mx_ready")
        e_ready = sem("e_ready")
        a_ready = sem("a_ready")
        t_ready = sem("t_ready")
        t_free = sem("t_free")
        pv_ready = sem("pv_ready")
        pv_free = sem("pv_free")
        lf_ready = sem("lf_ready")
        kk_ready = sem("kk_ready")
        b_ready = sem("b_ready")
        d_ready = sem("d_ready")
        ex_ready = sem("ex_ready")
        x_ready = sem("x_ready")
        dk_ready = sem("dk_ready")
        ek_ready = sem("ek_ready")
        kd_ready = sem("kd_ready")
        eb_ready = sem("eb_ready")
        qd_ready = sem("qd_ready")
        kdm_ready = sem("kdm_ready")
        rec_ready = [sem(f"rec_ready{p}") for p in range(2)]
        rec_free = [sem(f"rec_free{p}") for p in range(2)]
        cleared = sem("cleared")
        oa_stored = [sem(f"oa_stored{p}") for p in range(2)]
        or_stored = [sem(f"or_stored{p}") for p in range(2)]
        st_stored = sem("st_stored")
        so_stored = sem("so_stored")
        LOADS = 7 * 16
        SMALL = sum(7 if i > 1 else 4 for i in range(NT)) + (SLEVELS - 1) + 6

        def ready(h, u):
            return h * REC_PER[u % 2] + (u // 2 + 2)

        def freed(h, u):
            return h * REC_PER[u % 2] + (u // 2 + 2)

        def each_head(eng, body):
            with eng.Fori(0, H // 2) as pair:
                for par in range(2):
                    body(pair * 2 + par, par, pair)

        with nc.Block() as block:
            @block.sync
            def _(sp):
                for s in (*rec_ready, *rec_free, t_free, pv_free, t_ready):
                    sp.sem_inc(s, 1)
                for s in (*oa_stored, *or_stored, st_stored, so_stored):
                    sp.sem_inc(s, 16)

                def load(h):
                    p = h % 2
                    for dst, src in ((Q[p][:, :], io["q_d"][h, :, 0:T]), (K[p][:, :], io["k_d"][h, :, 0:T]),
                                     (F[p][:, :], io["f_d"][h]), (RQ[p][:, :], io["rq_d"][h]),
                                     (V[p][:, :, :], io["v_prompt"].rearrange("(t p) h c -> h p t c", p=P)[h]),
                                     (RI[p][:, 0:NT, :], io["ri_d"][h, :, 0:NT, :]), (RI[p][0:NS, NT, :], io["ri_d"][h, 0:NS, NT, :])):
                        sp.dma_start(dst, src).then_inc(loaded[p], 16)

                def states(h):
                    sp.dma_start(SIN[:, :, :], io["state_hgrn"][0].rearrange("b h k v -> h k b v")[h]).then_inc(states_in, 16)

                load(0)
                states(0)
                load(1)
                for h in range(H):
                    p = h % 2
                    sp.wait_ge(rec_free[(U_USE + 1) % 2], freed(h, U_USE + 1))
                    sp.dma_start(io["hgrn_prompt"][h], ST[:, NT, :]).then_inc(st_stored, 16)
                    sp.wait_ge(rec_free[(SU_USE + 1) % 2], freed(h, SU_USE + 1))
                    sp.dma_start(io["hgrn_sample"].rearrange("b h k v -> h k b v")[h], SOUT[:, :, :]).then_inc(so_stored, 16)
                    sp.wait_ge(rec_free[0], freed(h, SO_USE))
                    if h + 1 < H:
                        states(h + 1)
                    sp.wait_ge(rec_free[1], freed(h, O_USE + 1))
                    sp.dma_start(io["o_d"][H + h], OR[p][:, :]).then_inc(or_stored[p], 16)
                    sp.wait_ge(pv_free, h * NT + NT + 1)
                    sp.dma_start(io["o_d"][h, :, 0:T], OA[p][:, :]).then_inc(oa_stored[p], 16)
                    if h + 2 < H:
                        load(h + 2)
                for p in range(2):
                    sp.wait_ge(oa_stored[p], 16 * 3)
                    sp.wait_ge(or_stored[p], 16 * 3)
                sp.wait_ge(st_stored, 16 * (H + 1))
                sp.wait_ge(so_stored, 16 * (H + 1))

            @block.gpsimd
            def _(pool):
                tt = nc.gpsimd.tensor_tensor

                def body(h, par, pair):
                    def tokens(l):
                        return TT if l < SLEVELS else T

                    def distances(l):
                        bl, xl = blocks_of(b, 2 ** l, tokens(l)), blocks_of(X[(l + 1) % 2], 2 ** l, tokens(l))
                        w = 2 ** l // 2
                        mid = bl[:, :, 0, w - 1:w].broadcast_to([P, tokens(l) // (2 * w), w])
                        last = {1: None, 2: None, 3: SG_USE, 4: SG_USE}.get(l, G_USE[l - 2] + 1 if l > 4 else None)
                        if last is not None:
                            pool.wait_ge(rec_ready[last % 2], ready(h, last))
                        elif l == 1:
                            pool.wait_ge(b_ready, h + 1)
                        tt(xl[:, :, 0, :], mid, bl[:, :, 0, :], ALU.subtract)
                        tt(xl[:, :, 1, :], bl[:, :, 1, :], mid, ALU.subtract).then_inc(d_ready, 1)

                    def weigh(l):
                        xl = blocks_of(X[(l + 1) % 2], 2 ** l, tokens(l))
                        pool.wait_ge(ex_ready, h * (LEVELS - 1) + l)
                        tt(xl[:, :, 0, :], xl[:, :, 0, :], blocks_of(KK, 2 ** l, tokens(l))[:, :, 0, :], ALU.mult)
                        tt(xl[:, :, 1, :], xl[:, :, 1, :], blocks_of(RQ[par], 2 ** l, tokens(l))[:, :, 1, :], ALU.mult).then_inc(x_ready, 1)

                    distances(1), distances(2), weigh(1), weigh(2)
                    distances(3), distances(4), weigh(3)
                    distances(5), weigh(4), weigh(5)
                    distances(6), distances(7)
                    for first, n, w in ((0, NT, P), (T, NB, TS)):
                        view = b[:, first:first + n * w].rearrange("p (n w) -> p n w", w=w)
                        last = tt(KD[:, first:first + n * w].rearrange("p (n w) -> p n w", w=w), view[:, :, w - 1:w].broadcast_to([P, n, w]), view, ALU.subtract)
                    last.then_inc(dk_ready, 1)
                    weigh(6), weigh(7)
                    pool.wait_ge(ek_ready, h + 1)
                    tt(KD[:, :], KD[:, :], KK[:, :], ALU.mult).then_inc(kd_ready, 1)
                    pool.wait_ge(eb_ready, h + 1)
                    tt(QD[:, :], RQ[par][:, :], EB[:, :], ALU.mult).then_inc(qd_ready, 1)

                each_head(pool, body)

            @block.tensor
            def _(pe):
                mm = nc.tensor.matmul

                def body(h, par, pair):
                    def scores(i):
                        if i == 0:
                            pe.wait_ge(loaded[par], pair * LOADS + LOADS)
                            if par == 0:
                                pass
                        pe.wait_ge(e_ready, h * NT + (i + 1))
                        n = (i + 1) * P
                        for m in range(2):
                            rows = slice(m * HD, (m + 1) * HD)
                            for c in range(0, n, 512):
                                w = min(512, n - c)
                                last = mm(S[:, m, c:c + w], Q[par][rows, i * P:(i + 1) * P], K[par][rows, c:c + w], start=True, stop=True)
                        last.then_inc(s_ready, 1)

                    def attend(i):
                        pe.wait_ge(a_ready, h * NT + (i + 1))
                        for g in range(T_GROUPS[i]):
                            pe.wait_ge(t_free, h * T_PER + (T_FIRST[i] + g + 1))
                            for j in range(4 * g, min(4 * g + 4, i + 1)):
                                last = nc.tensor.transpose(trp[:, (j % 4) * P:(j % 4 + 1) * P], A[i % 2][:, j * P:(j + 1) * P], keep["ident"][:, :])
                            last.then_inc(t_ready, 1)
                        pe.wait_ge(pv_free, h * NT + (i + 1))
                        for j in range(i + 1):
                            if j % 4 == 0:
                                pe.wait_ge(t_free, h * T_PER + (T_FIRST[i] + j // 4 + 2))
                            last = mm(pvp[:, 0:P], V[par][:, j, :], At[i % 2][:, j * P:(j + 1) * P], start=(j == 0), stop=(j == i))
                        last.then_inc(pv_ready, 1)

                    def tiles(u):
                        return range(4 * ((u - 1) % 2), 0)

                    def recur(u):
                        bank = rec[u % 2]
                        pe.wait_ge(rec_free[u % 2], freed(h, u) - 1)
                        for l, first in G_USE.items():
                            if u in (first, first + 1):
                                left, right = (KK, RQ[par]) if l == 0 else (X[(l + 1) % 2],) * 2
                                pe.wait_ge(*((kk_ready, h + 1) if l == 0 else (x_ready, h * (LEVELS - 1) + l)))
                                for j in range(4):
                                    t = slice((4 * (u - first) + j) * P, (4 * (u - first) + j + 1) * P)
                                    last = mm(bank[:, j * P:(j + 1) * P], left[:, t], right[:, t], start=True, stop=True)
                        if u == SG_USE:
                            for l in range(SLEVELS):
                                left, right = (KK, RQ[par]) if l == 0 else (X[(l + 1) % 2],) * 2
                                last = mm(bank[0:NS, l * NS:(l + 1) * NS], left[:, T:TT], right[:, T:TT], start=True, stop=True)
                        if KD_USE <= u < KD_USE + 3:
                            pe.wait_ge(kd_ready, h + 1)
                            for j, t in enumerate(range(4 * (u - KD_USE), min(4 * (u - KD_USE) + 4, NT + 1))):
                                rows = P if t < NT else NS
                                last = nc.tensor.transpose(bank[0:rows, j * P:(j + 1) * P], KD[:, t * P:t * P + rows], keep["ident"][:, :])
                        if U_USE <= u < U_USE + 2:
                            if u == U_USE:
                                pe.wait_ge(rec_free[1], freed(h, KD_USE + 2))
                            for j in range(4):
                                t = 4 * (u - U_USE) + j
                                last = mm(bank[:, j * P:(j + 1) * P], KDT[:, t, :], RI[par][:, t, :], start=True, stop=True)
                        if SU_USE <= u < SU_USE + 2:
                            pe.wait_ge(kdm_ready, h + 1)
                            for j in range(4):
                                last = mm(bank[:, j * P:(j + 1) * P], KDM[:, 4 * (u - SU_USE) + j, :], RI[par][0:NS, NT, :], start=True, stop=True)
                        if O_USE <= u < O_USE + 2:
                            if u == O_USE:
                                pe.wait_ge(rec_free[1], freed(h, U_USE + 1))
                            pe.wait_ge(qd_ready, h + 1)
                            for j in range(4):
                                t = 4 * (u - O_USE) + j
                                out = bank[:, j * P:(j + 1) * P]
                                mm(out, RI[par][:, t, :], AT[:, t, :], start=True, stop=False)
                                last = mm(out, ST[:, t, :], QD[:, t * P:(t + 1) * P], start=False, stop=True)
                        if u == SO_USE:
                            pe.wait_ge(states_in, 16 * h + 16)
                            mm(bank[:, 0:NS], RI[par][0:NS, NT, :], ATS[:, :], start=True, stop=False)
                            for s in range(NB):
                                last = mm(bank[:, s * TS:(s + 1) * TS], SIN[:, s, :], QD[:, T + s * TS:T + (s + 1) * TS], start=False, stop=(s == NB - 1))
                        last.then_inc(rec_ready[u % 2], 1)

                    for i in range(NT):
                        scores(i)
                        if i:
                            attend(i - 1)
                        for u in REC_SLOT[i]:
                            recur(u)
                    for u in REC_SLOT[NT]:
                        recur(u)
                    attend(NT - 1)

                each_head(pe, body)

            @block.scalar
            def _(act):
                a = nc.scalar.activation
                act.sem_inc(e_ready, 1)

                def body(h, par, pair):
                    def exponentials(i):
                        act.wait_ge(mx_ready, h * NT + (i + 1))
                        n0 = max(0, i - 1) * P
                        n1 = (i + 1) * P
                        for m in range(2):
                            if n0:
                                a(E[:, m, 0:n0], S[:, m, 0:n0], ACT.Exp, bias=farb[:, m:m + 1], accum_out=ls[:, m, 1:2])
                            last = a(E[:, m, n0:n1], near[:, m, 2 * P - (n1 - n0):2 * P], ACT.Exp, bias=negm[:, m:m + 1], accum_out=ls[:, m, 0:1])
                        last.then_inc(e_ready, 1)

                    def evacuate(i):
                        for g in range(T_GROUPS[i]):
                            act.wait_ge(t_ready, h * T_PER + (T_FIRST[i] + g + 2))
                            w = min(4, i + 1 - 4 * g) * P
                            a(At[i % 2][:, 4 * g * P:4 * g * P + w], trp[:, 0:w], ACT.Copy).then_inc(t_free, 1)
                        if i == 0:
                            act.wait_ge(oa_stored[par], pair * 16 + 16)
                        act.wait_ge(pv_ready, h * NT + (i + 1))
                        a(OA[par][:, i * P:(i + 1) * P], pvp[:, 0:P], ACT.Copy).then_inc(pv_free, 1)

                    def level(l):
                        n = TT if l < SLEVELS else T
                        act.wait_ge(d_ready, h * (LEVELS - 1) + l)
                        a(X[(l + 1) % 2][:, 0:n], X[(l + 1) % 2][:, 0:n], ACT.Exp).then_inc(ex_ready, 1)

                    def consume(u):
                        if u in range(KD_USE, KD_USE + 3):
                            act.wait_ge(rec_ready[u % 2], ready(h, u))
                            if u < KD_USE + 2:
                                t = 4 * (u - KD_USE)
                                a(KDT[:, t:t + 4, :].rearrange("p t c -> p (t c)"), rec[u % 2][:, :], ACT.Copy).then_inc(rec_free[u % 2], 1)
                            else:
                                a(KDT[0:NS, NT, :], rec[u % 2][0:NS, 0:P], ACT.Copy).then_inc(rec_free[u % 2], 1)
                        if u in range(O_USE, SO_USE + 1):
                            if u == O_USE:
                                act.wait_ge(or_stored[par], pair * 16 + 16)
                            act.wait_ge(rec_ready[u % 2], ready(h, u))
                            c, n = (u - O_USE) * 512, 512 if u < SO_USE else NS
                            a(OR[par][:, c:c + n], rec[u % 2][:, 0:n], ACT.Copy).then_inc(rec_free[u % 2], 1)

                    act.wait_ge(loaded[par], pair * LOADS + LOADS)
                    a(LF[:, :], F[par][:, :], ACT.Ln).then_inc(lf_ready, 1)
                    for i in range(NT):
                        exponentials(i)
                        if i:
                            evacuate(i - 1)
                        for u in REC_SLOT[i]:
                            consume(u)
                        if i == 0:
                            level(1), level(2)
                        if i == 1:
                            a(EB[:, :], b[:, :], ACT.Exp).then_inc(eb_ready, 1)
                        if i == 2:
                            level(3)
                        if i == 3:
                            level(4), level(5)
                        if i == 4:
                            level(6), level(7)
                            act.wait_ge(dk_ready, h + 1)
                            a(KD[:, :], KD[:, :], ACT.Exp).then_inc(ek_ready, 1)
                    for u in REC_SLOT[NT]:
                        consume(u)
                    evacuate(NT - 1)

                each_head(act, body)

            @block.vector
            def _(dve):
                v = nc.vector
                v.memset(AT[:, :, :], 0.0)
                v.memset(ATS[:, :], 0.0)
                v.memset(ST[:, 0, :], 0.0)
                v.memset(resets[:, :], 1.0).then_inc(cleared, 1)
                dve.wait_ge(cleared, 1)
                v.memset(resets[:, 0:T:P], 0.0)
                v.memset(resets[:, T:TT:TS], 0.0).then_inc(cleared, 1)
                dve.wait_ge(cleared, 2)

                def body(h, par, pair):
                    count, gated = [0], [0]

                    def link(ins):
                        ins.then_inc(small, 1)
                        count[0] += 1
                        dve.wait_ge(small, h * SMALL + count[0])

                    def gate():
                        v.memset(gates[:, gated[0]:gated[0] + 1], 0.0)
                        gated[0] += 1

                    def maxima(i):
                        n0, n1 = max(0, i - 1) * P, (i + 1) * P
                        w = n1 - n0
                        dve.wait_ge(s_ready, h * NT + (i + 1))
                        bias = keep["bias"][:, bass.ds(h, 1), 2 * P - w:2 * P].broadcast_to([P, 2, w])
                        link(v.tensor_tensor(near[:, :, 2 * P - w:2 * P], S[:, :, n0:n1], bias, ALU.add))
                        if not n0:
                            link(v.tensor_reduce(mx[:, 0, :], near[:, :, 2 * P - w:2 * P], AX.X, ALU.max))
                            v.tensor_scalar(negm[:, :], mx[:, 0, :], -1.0, None, ALU.mult).then_inc(mx_ready, 1)
                            return
                        v.tensor_reduce(mx[:, 0, :], near[:, :, 2 * P - w:2 * P], AX.X, ALU.max)
                        link(v.tensor_reduce(mx[:, 1, :], S[:, :, 0:n0], AX.X, ALU.max))
                        far = keep["far"][:, bass.ds(h, 1)]
                        link(v.scalar_tensor_tensor(mx[:, 0, :], mx[:, 1, :], far, mx[:, 0, :], ALU.add, ALU.max))
                        link(v.tensor_scalar(negm[:, :], mx[:, 0, :], -1.0, None, ALU.mult))
                        v.tensor_scalar(farb[:, :], negm[:, :], far, None, ALU.add).then_inc(mx_ready, 1)

                    def combine(i):
                        n1 = (i + 1) * P
                        dve.wait_ge(e_ready, h * NT + (i + 2))
                        l = ls[:, :, 0]
                        if i > 1:
                            link(v.tensor_tensor(lt[:, :], ls[:, :, 0], ls[:, :, 1], ALU.add))
                            l = lt[:, :]
                        link(v.reciprocal(rl[:, :], l))
                        if i >= 2:
                            dve.wait_ge(t_ready, h * T_PER + (T_FIRST[i - 1] + 1))
                        else:
                            dve.wait_ge(t_ready, h * T_PER + 1)
                        v.tensor_scalar(c1[:, :], rl[:, 1:2], keep["lam"][:, 1:2], None, ALU.mult)
                        link(v.tensor_scalar(A[i % 2][:, 0:n1], E[:, 0, 0:n1], rl[:, 0:1], None, ALU.mult))
                        v.scalar_tensor_tensor(A[i % 2][:, 0:n1], E[:, 1, 0:n1], c1[:, 0:1], A[i % 2][:, 0:n1], ALU.mult, ALU.add).then_inc(a_ready, 1)

                    def consume(u):
                        bank = rec[u % 2]
                        for l, first in G_USE.items():
                            if u in (first, first + 1):
                                dve.wait_ge(rec_ready[u % 2], ready(h, u))
                                if u == 0:
                                    dve.wait_ge(rec_ready[1], h * REC_PER[1] + 1)
                                gate()
                                t = 4 * (u - first)
                                v.copy_predicated(AT[:, t:t + 4, :], keep["lmask"][:, l:l + 1, :].broadcast_to([P, 4, P]),
                                                  bank[:, :].rearrange("p (t c) -> p t c", t=4)).then_inc(rec_free[u % 2], 1)
                        if u == SG_USE:
                            dve.wait_ge(rec_ready[u % 2], ready(h, u))
                            gate()
                            for l in range(SLEVELS):
                                last = v.copy_predicated(ATS[:, :], keep["lmask"][0:NS, l, 0:NS], bank[0:NS, l * NS:(l + 1) * NS])
                                if l < SLEVELS - 1:
                                    link(last)
                                    gate()
                            last.then_inc(rec_free[u % 2], 1)
                        if u == KD_USE + 2:
                            dve.wait_ge(rec_free[u % 2], freed(h, u))
                            v.tensor_tensor(KDM[:, :, :], KDT[0:NS, NT:NT + 1, :].broadcast_to([NS, NB, P]),
                                            keep["rowmask"][:, :].rearrange("p (b o) -> p b o", o=1).broadcast_to([NS, NB, P]), ALU.mult).then_inc(kdm_ready, 1)
                        if U_USE <= u < U_USE + 2:
                            dve.wait_ge(rec_ready[u % 2], ready(h, u))
                            if u == U_USE:
                                dve.wait_ge(eb_ready, h + 1)
                            else:
                                dve.wait_ge(rec_free[(u - 1) % 2], freed(h, u - 1))
                                dve.wait_ge(st_stored, h * 16 + 16)
                            for j in range(4):
                                t = 4 * (u - U_USE) + j
                                last = v.scalar_tensor_tensor(ST[:, t + 1, :], ST[:, t, :], EB[:, t * P + P - 1:t * P + P], bank[:, j * P:(j + 1) * P], ALU.mult, ALU.add)
                                if j < 3:
                                    link(last)
                            last.then_inc(rec_free[u % 2], 1)
                        if SU_USE <= u < SU_USE + 2:
                            dve.wait_ge(rec_ready[u % 2], ready(h, u))
                            if u == SU_USE:
                                dve.wait_ge(states_in, 16 * h + 16)
                                dve.wait_ge(so_stored, h * 16 + 16)
                            for j in range(4):
                                s = 4 * (u - SU_USE) + j
                                last = v.scalar_tensor_tensor(SOUT[:, s, :], SIN[:, s, :], EB[:, T + s * TS + TS - 1:T + s * TS + TS], bank[:, j * P:(j + 1) * P], ALU.mult, ALU.add)
                            last.then_inc(rec_free[u % 2], 1)

                    for i in range(NT):
                        maxima(i)
                        for u in REC_SLOT[i]:
                            consume(u)
                        if i == 0:
                            dve.wait_ge(loaded[par], pair * LOADS + LOADS)
                            v.tensor_scalar(KK[:, :], F[par][:, :], -1.0, 1.0, ALU.mult, ALU.add).then_inc(kk_ready, 1)
                            dve.wait_ge(lf_ready, h + 1)
                            v.tensor_tensor_scan(b[:, :], resets[:, :], LF[:, :], 0.0, ALU.mult, ALU.add).then_inc(b_ready, 1)
                        combine(i)
                    for u in REC_SLOT[NT]:
                        consume(u)
                    assert count[0] == SMALL, (count, SMALL)

                each_head(dve, body)


def samples(nc, io, keep):
    with ExitStack() as ctx:
        sb, ps, sem = open_memory(nc, ctx)
        pt = sb("pt", [1, 2 * NB], I32)
        kp = [sb(f"kp{p}", [P, 2, FW]) for p in range(2)]
        vp = [sb(f"vp{p}", [P, 2, FW]) for p in range(2)]
        KT = [sb(f"KT{p}", [P, H, PAST]) for p in range(2)]
        KN = sb("KN", [P, H, NS])
        QS = sb("QS", [P, H, NS])
        QZ = sb("QZ", [P, NB, H, 32])
        VN = sb("VN", [NS, FW])
        sc = sb("sc", [P, 2, NK])
        smx = sb("smx", [P, 2])
        snm = sb("snm", [P, 2])
        ssum = sb("ssum", [P, 2])
        srl = sb("srl", [P, 2])
        sfac = sb("sfac", [P, 3])
        PT = sb("PT", [P, 2, 2, P])
        PTN = sb("PTN", [NS, 2, P])
        OS = sb("OS", [P, H, NB, TS])
        trs = [ps(f"trs{p}", [P, 512]) for p in range(2)]
        Sg = [ps(f"Sg{g}", [P, 512]) for g in range(2)]
        ptp = ps("ptp", [P, 512])
        opv = ps("opv", [P, 512])

        table_in = sem("table_in")
        news_in = sem("news_in")
        k_in = [sem(f"k_in{p}") for p in range(2)]
        v_in = [sem(f"v_in{p}") for p in range(2)]
        tr_ready = sem("str_ready")
        tr_free = [sem(f"str_free{p}") for p in range(2)]
        qz_ready = sem("qz_ready")
        sg_ready = sem("sg_ready")
        smx_ready = sem("smx_ready")
        sx_ready = sem("sx_ready")
        p_ready = sem("p_ready")
        pt_ready = sem("pt_ready")
        pt_free = sem("pt_free")
        pv_ready = sem("spv_ready")
        os_ready = sem("os_ready")
        os_stored = sem("os_stored")

        with nc.Block() as block:
            @block.sync
            def _(sp):
                sp.dma_start(pt[:, :], io["page_table"].rearrange("(o b) n -> o (b n)", o=1)).then_inc(table_in, 16)
                sp.dma_start(QS[:, :, :], io["q_d"].rearrange("h p t -> p h t")[:, :, T:TT]).then_inc(news_in, 16)
                sp.dma_start(KN[:, :, :], io["k_d"].rearrange("h p t -> p h t")[:, :, T:TT]).then_inc(news_in, 16)
                sp.dma_start(VN[:, :], io["v_sample"].rearrange("t h c -> t (h c)")).then_inc(news_in, 16)
                sp.wait_ge(table_in, 16)
                for s in range(NB):
                    if s >= 2:
                        sp.wait_ge(tr_ready, 2 * (s - 2) + 2)
                    for g in range(2):
                        page = sp.value_load(pt[0:1, 2 * s + g:2 * s + g + 1], min_val=0, max_val=io["cache_k"].shape[1] - 1)
                        sp.dma_start(kp[s % 2][:, g, :], io["cache_k"][0].rearrange("n p h m d -> n p (h m d)")[bass.ds(page, 1)].rearrange("o p c -> p (o c)"))\
                          .then_inc(k_in[s % 2], 16)
                for s in range(NB):
                    if s >= 2:
                        sp.wait_ge(pv_ready, s - 1)
                    for g in range(2):
                        page = sp.value_load(pt[0:1, 2 * s + g:2 * s + g + 1], min_val=0, max_val=io["cache_v"].shape[1] - 1)
                        sp.dma_start(vp[s % 2][:, g, :], io["cache_v"][0].rearrange("n p h c -> n p (h c)")[bass.ds(page, 1)].rearrange("o p c -> p (o c)"))\
                          .then_inc(v_in[s % 2], 16)
                sp.wait_ge(os_ready, 1)
                sp.dma_start(io["o_d"][0:H].rearrange("h p t -> p h t")[:, :, T:TT], OS[:, :, :, :].rearrange("p h b t -> p h (b t)")).then_inc(os_stored, 16)
                sp.wait_ge(os_stored, 16)

            @block.tensor
            def _(pe):
                mm = nc.tensor.matmul
                for s in range(NB):
                    pe.wait_ge(k_in[s % 2], 32 * (s // 2 + 1))
                    for g in range(2):
                        if s:
                            pe.wait_ge(tr_free[g], s)
                        for h in range(H):
                            last = nc.tensor.transpose(trs[g][:, h * P:(h + 1) * P], kp[s % 2][:, g, h * P:(h + 1) * P], keep["ident"][:, :])
                        last.then_inc(tr_ready, 1)
                    if s == 0:
                        pe.wait_ge(qz_ready, 1)
                        pe.wait_ge(news_in, 48)
                    for g in range(2):
                        pe.wait_ge(tr_free[g], s + 1)
                    rows = slice(32 * (s % 4), 32 * (s % 4) + 32)
                    for h in range(H):
                        mm(Sg[s // 4][rows, 0:PAST], QZ[:, s, h, :], KT[s % 2][:, h, :], start=(h == 0), stop=(h == H - 1), tile_position=(0, rows.start))
                    for h in range(H):
                        last = mm(Sg[s // 4][rows, PAST:NK], QZ[:, s, h, :], KN[:, h, :], start=(h == 0), stop=(h == H - 1), tile_position=(0, rows.start))
                    last.then_inc(sg_ready, 1)
                for g in range(2):
                    pe.wait_ge(p_ready, g + 1)
                    if g:
                        pe.wait_ge(pt_free, 1)
                    nc.tensor.transpose(ptp[:, 0:P], sc[:, g, 0:P], keep["ident"][:, :])
                    nc.tensor.transpose(ptp[:, P:2 * P], sc[:, g, P:2 * P], keep["ident"][:, :])
                    nc.tensor.transpose(ptp[0:NS, 2 * P:3 * P], sc[:, g, PAST:NK], keep["ident"][:, :]).then_inc(pt_ready, 1)
                for s in range(NB):
                    g = s // 4
                    if s % 4 == 0:
                        pe.wait_ge(pt_free, g + 1)
                    pe.wait_ge(v_in[s % 2], 32 * (s // 2 + 1))
                    for h in range(H):
                        cols = slice(32 * (s % 4) + 8 * h, 32 * (s % 4) + 8 * h + 8)
                        out = opv[:, 32 * s + 8 * h:32 * s + 8 * h + 8]
                        for j in range(2):
                            mm(out, vp[s % 2][:, j, h * P:(h + 1) * P], PT[:, g, j, cols], start=(j == 0), stop=False)
                        last = mm(out, VN[:, h * P:(h + 1) * P], PTN[:, g, cols], start=False, stop=True)
                    last.then_inc(pv_ready, 1)

            @block.scalar
            def _(act):
                a = nc.scalar.activation
                for s in range(NB):
                    act.wait_ge(tr_ready, 2 * s + 2)
                    if s >= 2:
                        act.wait_ge(sg_ready, s - 1)
                    a(KT[s % 2][:, :, P:2 * P], trs[1][:, :].rearrange("p (h c) -> p h c", h=H), ACT.Copy).then_inc(tr_free[1], 1)
                for g in range(2):
                    act.wait_ge(smx_ready, g + 1)
                    a(sc[:, g, :], sc[:, g, :], ACT.Exp, bias=snm[:, g:g + 1], accum_out=ssum[:, g:g + 1]).then_inc(sx_ready, 1)

            @block.vector
            def _(dve):
                v = nc.vector
                link = keep["dve_chain"].of(dve)
                link(v.memset(QZ[:, :, :, :], 0.0))
                dve.wait_ge(news_in, 48)
                for h in range(H):
                    for m in range(2):
                        rows, col = slice(m * HD, (m + 1) * HD), 8 * h + 4 * m
                        last = v.tensor_copy(QZ[rows, :, h, col:col + TS], QS[rows, h, :].rearrange("p (b t) -> p b t", t=TS))
                last.then_inc(qz_ready, 1)

                def keys(s):
                    dve.wait_ge(tr_ready, 2 * s + 1)
                    if s >= 2:
                        dve.wait_ge(sg_ready, s - 1)
                    v.tensor_copy(KT[s % 2][:, :, 0:P], trs[0][:, :].rearrange("p (h c) -> p h c", h=H)).then_inc(tr_free[0], 1)

                link(v.tensor_scalar(sfac[:, 0:1], keep["rowsel"][:, 1:2], keep["lam"][:, 1:2], None, ALU.mult))
                link(v.tensor_tensor(sfac[:, 0:1], sfac[:, 0:1], keep["rowsel"][:, 0:1], ALU.add))
                for s in range(NB):
                    keys(s)
                for g in range(2):
                    dve.wait_ge(sg_ready, 4 * g + 4)
                    link(v.tensor_tensor(sc[:, g, :], Sg[g][:, 0:NK], keep["sbias"][:, g, :], ALU.add))
                    link(v.tensor_reduce(smx[:, g:g + 1], sc[:, g, :], AX.X, ALU.max))
                    v.tensor_scalar(snm[:, g:g + 1], smx[:, g:g + 1], -1.0, None, ALU.mult).then_inc(smx_ready, 1)
                for g in range(2):
                    dve.wait_ge(sx_ready, g + 1)
                    link(v.reciprocal(srl[:, g:g + 1], ssum[:, g:g + 1]))
                    link(v.tensor_tensor(sfac[:, 1 + g:2 + g], srl[:, g:g + 1], sfac[:, 0:1], ALU.mult))
                    v.tensor_scalar(sc[:, g, :], sc[:, g, :], sfac[:, 1 + g:2 + g], None, ALU.mult).then_inc(p_ready, 1)
                for g in range(2):
                    dve.wait_ge(pt_ready, g + 1)
                    v.tensor_copy(PT[:, g, :, :], ptp[:, 0:2 * P].rearrange("p (j c) -> p j c", j=2))
                    v.tensor_copy(PTN[:, g, :], ptp[0:NS, 2 * P:3 * P]).then_inc(pt_free, 1)
                dve.wait_ge(pv_ready, NB)
                both = opv[:, 0:32 * NB].rearrange("p (b h m t) -> p h b m t", b=NB, h=H, m=2)
                link(v.tensor_copy(OS[:, :, :, :], both[:, :, :, 0, :]))
                for h in range(H):
                    last = v.tensor_tensor(OS[:, h, :, :], OS[:, h, :, :], both[:, h, :, 1, :], ALU.add)
                last.then_inc(os_ready, 1)


def mix(nc, io, keep, acc):
    with ExitStack() as ctx:
        sb, ps, sem = open_memory(nc, ctx)
        hh = sb("m_hi", [P, 2 * H, TT], F32R)
        hl = sb("m_lo", [P, 2 * H, TT], F32R)
        O = sb("O", [P, 2 * H, TT])
        rb = sb("m_rb", [P, H, TT])
        sq = sb("m_sq", [P, 2, TT])
        rg = sb("m_rg", [P, 1, TT])
        raw = sb("m_raw", [P, KC, P])
        whi = [sb(f"m_whi{s}", [P, KC, P], F32R) for s in range(2)]
        wlo = [sb(f"m_wlo{s}", [P, KC, P], F32R) for s in range(2)]
        zp = [ps(f"m_ps{n}", [P, 512]) for n in range(NPC)]
        ms = [ps(f"m_ms{n}", [P, 512]) for n in range(NPC)]

        x_back = sem("x_back")
        o_in = [sem(f"o_in{j}") for j in range(H)]
        rg_in = sem("rg_in")
        raw_in = sem("m_raw_in")
        w_ready = sem("m_w_ready")
        sq_ready = sem("m_sq_ready")
        ms_ready = sem("m_ms_ready")
        ln_ready = sem("m_ln_ready")
        rb_ready = sem("m_rb_ready")
        on_ready = sem("on_ready")
        hi_ready = sem("m_hi_ready")
        lo_ready = sem("m_lo_ready")
        z_ready = sem("m_z_ready")
        z_free = sem("m_z_free")
        w_view = io["w_out"][0].rearrange("(k p) (d c) -> d p k c", p=P, c=P)

        with nc.Block() as block:
            @block.sync
            def _(sp):
                for s, n in ((w_ready, 2), (z_ready, 2 * NPC), (z_free, NPC)):
                    sp.sem_inc(s, n)
                for j in range(H):
                    sp.dma_start(O[:, 2 * j:2 * j + 2, :], io["o_d"][2 * j:2 * j + 2].rearrange("h p t -> p h t")).then_inc(o_in[j], 16)
                sp.dma_start(acc[:, :, :], io["x_d"]).then_inc(x_back, 16)
                with sp.Fori(0, KC) as d:
                    sp.wait_ge(w_ready, d + 2)
                    sp.dma_start(raw[:, :, :], w_view[bass.ds(d, 1)].rearrange("o p k c -> p (o k) c")).then_inc(raw_in, 16)

            @block.gpsimd
            def _(pool):
                link = keep["pool_chain"].of(pool)
                with link.loop(KC // 2, 2) as pair:
                    for s in range(2):
                        pool.wait_ge(raw_in, pair * 32 + 16 * (s + 1))
                        pool.wait_ge(z_ready, pair * (2 * NPC) + NPC * (s + 1))
                        split_weights(nc, keep["ones"][:, :], raw[:, :, :], whi[s][:, :, :], wlo[s][:, :, :], link).then_inc(w_ready, 1)

            @block.tensor
            def _(pe):
                for j in range(2 * H):
                    pe.wait_ge(sq_ready, j + 1)
                    for n in range(NPC):
                        if j:
                            pe.wait_ge(ln_ready, NPC * (j - 1) + n + 1)
                        nc.tensor.matmul(ms[n][:, 0:PW], keep["ones"][:, :], sq[:, j % 2, piece(n)], start=True, stop=True).then_inc(ms_ready, 1)
                pe.wait_ge(lo_ready, 2 * H)
                with pe.Fori(0, KC // 2) as pair:
                    for s in range(2):
                        pe.wait_ge(w_ready, pair * 2 + (s + 3))
                        for n in range(NPC):
                            pe.wait_ge(z_free, pair * (2 * NPC) + (NPC * s + n + 1))
                            split_product(nc, zp[n][:, 0:PW], whi[s], wlo[s], hh[:, :, piece(n)], hl[:, :, piece(n)]).then_inc(z_ready, 1)

            @block.scalar
            def _(act):
                a = nc.scalar.activation
                for g in range(2):
                    for i in range(H):
                        j = g * H + i
                        act.wait_ge(o_in[j // 2], 16)
                        if j >= 2:
                            act.wait_ge(ms_ready, NPC * (j - 1))
                        a(sq[:, j % 2, :], O[:, j, :], ACT.Square).then_inc(sq_ready, 1)
                        if g and i == 0:
                            act.wait_ge(on_ready, H)
                        for n in range(NPC):
                            act.wait_ge(ms_ready, NPC * j + n + 1)
                            a(rb[:, i, piece(n)], ms[n][:, 0:PW], ACT.Ln, bias=keep["eps"][:, 0:1], scale=1.0 / P).then_inc(ln_ready, 1)
                    for i in range(H):
                        act.wait_ge(ln_ready, NPC * (g * H + H))
                        a(rb[:, i, :], rb[:, i, :], ACT.Exp, scale=-0.5).then_inc(rb_ready, 1)
                    for i in range(H):
                        j = g * H + i
                        if g:
                            if i:
                                act.wait_ge(on_ready, j)
                            act.dma_start(rg[:, 0, :], io["rg_d"][i]).then_inc(rg_in, 16)
                        act.wait_ge(on_ready, j + 1)
                        a(hh[:, j, :], O[:, j, :], ACT.Copy).then_inc(hi_ready, 1)

            @block.vector
            def _(dve):
                v = nc.vector
                link = keep["dve_chain"].of(dve)
                for j in range(2 * H):
                    gain = vector(keep, "subln_g" if j < H else "hgrn_onorm_g")
                    dve.wait_ge(rb_ready, j + 1)
                    ins = v.scalar_tensor_tensor(O[:, j, :], O[:, j, :], gain, rb[:, j % H, :], ALU.mult, ALU.mult)
                    if j >= H:
                        link(ins)
                        dve.wait_ge(rg_in, 16 * (j - H + 1))
                        ins = v.tensor_tensor(O[:, j, :], O[:, j, :], rg[:, 0, :], ALU.mult)
                    ins.then_inc(on_ready, 1)
                    if j:
                        dve.wait_ge(hi_ready, j)
                        v.tensor_tensor(hl[:, j - 1, :], O[:, j - 1, :], hh[:, j - 1, :].bitcast(F32), ALU.subtract).then_inc(lo_ready, 1)
                dve.wait_ge(hi_ready, 2 * H)
                v.tensor_tensor(hl[:, 2 * H - 1, :], O[:, 2 * H - 1, :], hh[:, 2 * H - 1, :].bitcast(F32), ALU.subtract).then_inc(lo_ready, 1)
                dve.wait_ge(x_back, 16)
                with dve.Fori(0, KC) as d:
                    for n in range(NPC):
                        dve.wait_ge(z_ready, d * NPC + (2 * NPC + n + 1))
                        row = acc[:, bass.ds(d, 1), piece(n)].rearrange("p o t -> p (o t)")
                        v.tensor_tensor(row, row, zp[n][:, 0:PW], ALU.add).then_inc(z_free, 1)


G2 = 2
GROUPS = FC // G2
DN_FIRST, DN_PER = 2, 2 + KC * NPC // 2


def mlp(nc, io, keep, acc):
    with ExitStack() as ctx:
        sb, ps, sem = open_memory(nc, ctx)
        hh = sb("f_hi", [P, KC, TT], F32R)
        hl = sb("f_lo", [P, KC, TT], F32R)
        raw = sb("f_raw", [P, 3, KC, P])
        names = ("g0", "u0", "g1", "u1", "d0", "d1")
        whi = {n: sb(f"f_whi_{n}", [P, KC, P], F32R) for n in names}
        wlo = {n: sb(f"f_wlo_{n}", [P, KC, P], F32R) for n in names}
        ahi = [sb(f"f_ahi{c}", [P, TT], F32R) for c in range(G2)]
        alo = [sb(f"f_alo{c}", [P, TT], F32R) for c in range(G2)]
        cp = sb("f_cp", [P, 2, TT])
        conv, prod = cp[:, 0, :], cp[:, 1, :]
        gate = sb("f_gate", [P, TT + 2])
        gsm = sb("f_gsm", [P, NB, TS + 2])
        rb = sb("f_rb", [P, TT])
        lnb = sb("f_lnb", [P, PW])
        scr = sb("f_scr", [P, P])
        g18 = sb("f_g18", [P, 2 + 2 * NB])
        cout = sb("f_cout", [2 + 2 * NB, P])
        gp = [ps(f"f_gp{n}", [P, 512]) for n in range(NPC)]
        up = [ps(f"f_up{n}", [P, 512]) for n in range(NPC)]
        dn = [ps(f"f_dn{n}", [P, 512]) for n in range(2)]

        sq_ready, sq_used, ms_ready, rb_ready = sem("f_sq_ready"), sem("f_sq_used"), sem("f_ms_ready"), sem("f_rb_ready")
        hf_ready, hi_ready, lo_ready = sem("f_hf_ready"), sem("f_hi_ready"), sem("f_lo_ready")
        raw_in = [sem(f"f_raw_in{s}") for s in range(3)]
        w_ready = sem("f_w_ready")
        scr_clear, scr_in = sem("scr_clear"), sem("scr_in")
        g_ready, g_free = sem("g_ready"), sem("g_free")
        gs_ready = sem("gs_ready")
        u_ready, u_free = sem("u_ready"), sem("u_free")
        c_ready, s_ready = sem("c_ready"), sem("f_s_ready")
        g18_ready = sem("g18_ready")
        dn_ready = [sem(f"dn_ready{b}") for b in range(2)]
        dn_free = [sem(f"dn_free{b}") for b in range(2)]
        ah_ready, al_ready = sem("ah_ready"), sem("al_ready")
        conv_stored = sem("conv_stored")
        y_ready = [sem(f"y_ready{b}") for b in range(2)]
        y_free = [sem(f"y_free{b}") for b in range(2)]
        y_stored = [sem(f"y_stored{p}") for p in range(2)]

        g_view = io["w_gate"][0].rearrange("(k p) (c f) -> c p k f", p=P, f=P)
        u_view = io["w_up"][0].rearrange("(k p) (c f) -> c p k f", p=P, f=P)
        d_view = io["w_down"][0].rearrange("(c p) (k f) -> c p k f", p=P, f=P)
        s_view = io["state_conv"][0].rearrange("b j (c f) -> c (b j) f", f=P)
        cp_view = io["conv_prompt"].rearrange("j (c f) -> c j f", f=P)
        cs_view = io["conv_sample"].rearrange("b j (c f) -> c (b j) f", f=P)
        W0 = 6

        def part(view, i):
            return view[bass.ds(i, 1)].rearrange("o p k f -> p (o k) f")

        def rows(view, i):
            return view[bass.ds(i, 1)].rearrange("o r f -> r (o f)")

        def dn_use(g, first, k):
            return k + 1 if first else g * DN_PER + (DN_FIRST - DN_PER + k + 1)

        with nc.Block() as block:
            @block.sync
            def _(sp):
                for s, n in ((w_ready, W0), (dn_free[0], 1), (dn_free[1], 1), (g_free, NPC), (u_free, NPC), (g_ready, 2 * NPC),
                             (u_ready, 2 * NPC), (conv_stored, 32), (al_ready, 2), (c_ready, 1), (s_ready, 1), (gs_ready, 1), (g18_ready, 1)):
                    sp.sem_inc(s, n)
                sp.wait_ge(scr_clear, 1)
                with sp.Fori(0, GROUPS) as g:
                    for k, (n, view) in enumerate(zip(names, (g_view, u_view, g_view, u_view, d_view, d_view))):
                        c = g * G2 + (k // 2 if k < 4 else k - 4)
                        sp.wait_ge(w_ready, g * 6 + (k + W0 - 2))
                        sp.dma_start(raw[:, k % 3, :, :], part(view, c)).then_inc(raw_in[k % 3], 16)
                        if k in (0, 2):
                            sp.wait_ge(gs_ready, g * 2 + (k // 2 + 1))
                            sp.dma_start(scr[0:2 * NB, :], rows(s_view, c)).then_inc(scr_in, 16)

            @block.gpsimd
            def _(pool):
                link = keep["pool_chain"].of(pool)
                nc.gpsimd.memset(scr[:, :], 0.0).then_inc(scr_clear, 1)
                with link.loop(GROUPS, 6) as g:
                    for k, n in enumerate(names):
                        pool.wait_ge(raw_in[k % 3], g * 32 + 16 * (k // 3 + 1))
                        if n[0] == "g":
                            pool.wait_ge(g_ready, g * (2 * NPC) + NPC * (k // 2 + 1))
                        elif n[0] == "u":
                            pool.wait_ge(u_ready, g * (2 * NPC) + NPC * (k // 2 + 1))
                        elif n == "d0":
                            pool.wait_ge(g_ready, g * (2 * NPC) + (2 * NPC + NPC + 1))
                        split_weights(nc, keep["ones"][:, :], raw[:, k % 3, :, :], whi[n][:, :, :], wlo[n][:, :, :], link).then_inc(w_ready, 1)

            @block.tensor
            def _(pe):
                norm_sums(nc, pe, keep["ones"], cp, gp, sq_ready, sq_used, ms_ready)

                def group(g, first):
                    def branch(c, b):
                        banks, ready, free = ((gp, g_ready, g_free), (up, u_ready, u_free))[b]
                        n = names[2 * c + b]
                        pe.wait_ge(w_ready, g * 6 + (2 * c + b + 1 + W0))
                        for i in range(NPC):
                            if first and c == 0 and b == 0:
                                pe.wait_ge(lo_ready, KC * (i + 1))
                            pe.wait_ge(free, g * (2 * NPC) + (NPC * c + i + 1))
                            split_product(nc, banks[i][:, 0:PW], whi[n], wlo[n], hh[:, :, piece(i)], hl[:, :, piece(i)]).then_inc(ready, 1)

                    def old_gates(c):
                        k = 0 if c == 0 else (1 if first else 1 + KC * NPC // 2)
                        pe.wait_ge(scr_in, g * 32 + 16 * (c + 1))
                        pe.wait_ge(dn_free[0], dn_use(g, first, k))
                        nc.tensor.transpose(dn[0][:, 0:P], scr[:, :], keep["ident"][:, :]).then_inc(dn_ready[0], 1)

                    def last_gates(c):
                        k = 0 if c == 0 else (1 if first else 1 + KC * NPC // 2)
                        pe.wait_ge(g18_ready, g * 2 + (c + 2))
                        pe.wait_ge(dn_free[1], dn_use(g, first, k))
                        nc.tensor.transpose(dn[1][0:2 + 2 * NB, 0:P], g18[:, :], keep["ident"][:, :]).then_inc(dn_ready[1], 1)

                    old_gates(0)
                    branch(0, 0)
                    branch(0, 1)
                    last_gates(0)
                    if not first:
                        down(g)
                    old_gates(1)
                    branch(1, 0)
                    branch(1, 1)
                    last_gates(1)

                def down(g, extra=1):
                    pe.wait_ge(w_ready, g * 6 + W0)
                    pe.wait_ge(al_ready, g * 2 + 2)
                    for j in range(KC * NPC):
                        d, n = divmod(j, NPC)
                        b = j % 2
                        pe.wait_ge(dn_free[b], dn_use(g, False, extra + j // 2))
                        out = dn[b][:, 0:PW]
                        for c in range(G2):
                            w = f"d{c}"
                            nc.tensor.matmul(out, whi[w][:, d, :], ahi[c][:, piece(n)], start=(c == 0), stop=False)
                            nc.tensor.matmul(out, whi[w][:, d, :], alo[c][:, piece(n)], start=False, stop=False)
                            last = nc.tensor.matmul(out, wlo[w][:, d, :], ahi[c][:, piece(n)], start=False, stop=(c == G2 - 1))
                        last.then_inc(dn_ready[b], 1)

                group(0, True)
                with pe.Fori(1, GROUPS) as g:
                    group(g, False)
                down(GROUPS, extra=0)
                for b in range(2):
                    pe.wait_ge(dn_free[b], dn_use(GROUPS, False, KC * NPC // 2))
                for t in range(NT + 1):
                    w = P if t < NT else NS
                    for b in range(2):
                        if t:
                            pe.wait_ge(y_free[b], t)
                        for j in range(4):
                            last = nc.tensor.transpose(gp[b][0:w, j * P:(j + 1) * P], acc[:, 4 * b + j, t * P:t * P + w], keep["ident"][:, :])
                        last.then_inc(y_ready[b], 1)

            @block.scalar
            def _(act):
                a = nc.scalar.activation
                link = keep["act_chain"].of(act)
                norm_squares(nc, act, acc, cp, sq_ready, sq_used)
                norm_inverse(nc, act, keep["eps"], gp, rb, lnb, ms_ready, rb_ready, link)
                norm_high(nc, act, gate[:, 0:TT].rearrange("p (s w) -> p s w", s=NPC), hh, hf_ready, hi_ready)

                def group(g, first):
                    def old_gates(c):
                        k = 0 if c == 0 else (1 if first else 1 + KC * NPC // 2)
                        act.wait_ge(c_ready, g * 2 + (c + 1))
                        act.wait_ge(g18_ready, g * 2 + (c + 1))
                        act.wait_ge(dn_ready[0], dn_use(g, first, k))
                        a(gsm[:, :, 0:2], dn[0][:, 0:2 * NB].rearrange("p (b j) -> p b j", j=2), ACT.Copy).then_inc(dn_free[0], 1)

                    def gates(c):
                        for i in range(NPC):
                            act.wait_ge(g_ready, g * (2 * NPC) + (2 * NPC + NPC * c + i + 1))
                            if first and c == 0 and i == 0:
                                act.wait_ge(lo_ready, KC * NPC)
                            lo, hi = i * PW, min((i + 1) * PW, T)
                            if i == NPC - 1:
                                a(gsm[:, :, 2:2 + TS], gp[i][:, hi - lo:PW].rearrange("p (b t) -> p b t", t=TS), ACT.Copy).then_inc(gs_ready, 1)
                            a(gate[:, 2 + lo:2 + hi], gp[i][:, 0:hi - lo], ACT.Copy).then_inc(g_free, 1)

                    def last_gates(c):
                        k = 0 if c == 0 else (1 if first else 1 + KC * NPC // 2)
                        act.wait_ge(dn_ready[1], dn_use(g, first, k))
                        act.wait_ge(conv_stored, g * 64 + 32 * (c + 1))
                        a(cout[:, :], dn[1][0:2 + 2 * NB, 0:P], ACT.Copy).then_inc(dn_free[1], 1)
                        act.wait_ge(dn_free[1], dn_use(g, first, k) + 1)
                        i = g * G2 + c
                        act.dma_start(rows(cp_view, i), cout[0:2, :]).then_inc(conv_stored, 16)
                        act.dma_start(rows(cs_view, i), cout[2:2 + 2 * NB, :]).then_inc(conv_stored, 16)

                    def silu(c):
                        act.wait_ge(c_ready, g * 2 + (c + 2))
                        a(conv, conv, ACT.Silu).then_inc(s_ready, 1)

                    def high(c):
                        act.wait_ge(u_free, g * (2 * NPC) + (NPC * c + 2 * NPC))
                        if c == 0 and not first:
                            act.wait_ge(g_ready, g * (2 * NPC) + (2 * NPC + NPC + 1))
                        a(ahi[c][:, :], prod, ACT.Copy).then_inc(ah_ready, 1)

                    old_gates(0), gates(0), silu(0), last_gates(0)
                    if first:
                        high(0), old_gates(1), gates(1)
                    else:
                        old_gates(1), high(0), gates(1)
                    silu(1), last_gates(1), high(1)

                group(0, True)
                with act.Fori(1, GROUPS) as g:
                    group(g, False)
                for t in range(NT + 1):
                    w = P if t < NT else NS
                    act.wait_ge(y_ready[1], t + 1)
                    if t == 0:
                        act.wait_ge(al_ready, 2 * GROUPS + 2)
                    if t >= 2:
                        act.wait_ge(y_stored[t % 2], 16 * (t // 2))
                    a(cp[0:w, t % 2, 4 * P:8 * P], gp[1][0:w, :], ACT.Copy).then_inc(y_free[1], 1)
                    act.wait_ge(y_free[0], t + 1)
                    act.wait_ge(y_free[1], t + 1)
                    dst = io["y_prompt"][0, t * P:(t + 1) * P, :] if t < NT else io["y_sample"].rearrange("b t d -> (b t) d")
                    act.dma_start(dst, cp[0:w, t % 2, 0:D]).then_inc(y_stored[t % 2], 16)
                act.wait_ge(y_stored[0], 16 * 5)
                act.wait_ge(y_stored[1], 16 * 4)
                act.wait_ge(conv_stored, 32 * (FC + 1))

            @block.vector
            def _(dve):
                v = nc.vector
                norm_low(nc, dve, acc, vector(keep, "norm2_g"), rb, gate[:, 0:TT].rearrange("p (s w) -> p s w", s=NPC), hh, hl, rb_ready, hf_ready, hi_ready, lo_ready)
                link = keep["dve_chain"].of(dve)
                dve.wait_ge(lo_ready, KC * NPC)
                link(v.memset(gate[:, 0:2], 0.0))
                PER = 8

                def group(g, first, link):
                    def w(j, c):
                        return keep["vec"][:, bass.ds(g * G2 + (VECTORS["conv_w"][0] + j * FC + c), 1)]

                    def convolve(c):
                        bias = keep["vec"][:, bass.ds(g * G2 + (VECTORS["conv_b"][0] + c), 1)]
                        dve.wait_ge(g_free, g * (2 * NPC) + (NPC + NPC * c + NPC))
                        dve.wait_ge(dn_free[1], dn_use(g, first, 0 if c == 0 else (1 if first else 1 + KC * NPC // 2)))
                        v.tensor_copy(g18[:, 0:2], gate[:, T:T + 2])
                        v.tensor_copy(g18[:, 2:2 + 2 * NB].rearrange("p (b j) -> p b j", j=2), gsm[:, :, TS:TS + 2]).then_inc(g18_ready, 1)
                        old = conv[:, T:TT].rearrange("p (b t) -> p b t", t=TS)
                        dve.wait_ge(ah_ready, g * 2 + c) if not (first and c == 0) else None
                        v.tensor_scalar(conv[:, 0:T], gate[:, 2:T + 2], w(2, c), bias, ALU.mult, ALU.add)
                        link(v.tensor_scalar(old, gsm[:, :, 2:2 + TS], w(2, c), bias, ALU.mult, ALU.add))
                        v.scalar_tensor_tensor(conv[:, 0:T], gate[:, 1:T + 1], w(1, c), conv[:, 0:T], ALU.mult, ALU.add)
                        link(v.scalar_tensor_tensor(old, gsm[:, :, 1:1 + TS], w(1, c), old, ALU.mult, ALU.add))
                        v.scalar_tensor_tensor(conv[:, 0:T], gate[:, 0:T], w(0, c), conv[:, 0:T], ALU.mult, ALU.add)
                        v.scalar_tensor_tensor(old, gsm[:, :, 0:TS], w(0, c), old, ALU.mult, ALU.add).then_inc(c_ready, 1)

                    def multiply(c):
                        dve.wait_ge(s_ready, g * 2 + (c + 2))
                        dve.wait_ge(al_ready, g * 2 + (c + 2))
                        for i in range(NPC):
                            dve.wait_ge(u_ready, g * (2 * NPC) + (2 * NPC + NPC * c + i + 1))
                            v.tensor_tensor(prod[:, piece(i)], conv[:, piece(i)], up[i][:, 0:PW], ALU.mult).then_inc(u_free, 1)

                    def low(c):
                        dve.wait_ge(ah_ready, g * 2 + (c + 1))
                        v.tensor_tensor(alo[c][:, :], prod, ahi[c][:, :].bitcast(F32), ALU.subtract).then_inc(al_ready, 1)

                    convolve(0), multiply(0)
                    if not first:
                        down(g)
                    low(0), convolve(1), multiply(1), low(1)

                def down(g, extra=1):
                    for j in range(KC * NPC):
                        d, n = divmod(j, NPC)
                        b = j % 2
                        dve.wait_ge(dn_ready[b], dn_use(g, False, extra + j // 2))
                        v.tensor_tensor(acc[:, d, piece(n)], acc[:, d, piece(n)], dn[b][:, 0:PW], ALU.add).then_inc(dn_free[b], 1)

                group(0, True, link)
                with link.loop(GROUPS - 1, 4) as g1:
                    group(g1 + 1, False, link)
                down(GROUPS, extra=0)
                for t in range(NT + 1):
                    w = P if t < NT else NS
                    dve.wait_ge(y_ready[0], t + 1)
                    if t >= 2:
                        dve.wait_ge(y_stored[t % 2], 16 * (t // 2))
                    v.tensor_copy(cp[0:w, t % 2, 0:4 * P], gp[0][0:w, :]).then_inc(y_free[0], 1)


def rel_bucket(n):
    n = np.maximum(n, 0)
    exact = N_BUCKETS // 2
    nf = np.maximum(n, 1).astype(np.float32)
    large = exact + (np.log(nf / np.float32(exact)) / np.float32(math.log(MAX_DISTANCE / exact)) * np.float32(N_BUCKETS - exact)).astype(np.int32)
    return np.where(n < exact, n, np.minimum(large, N_BUCKETS - 1))


def one_hot(distance):
    out = np.zeros((N_BUCKETS + 1,) + distance.shape, np.float32)
    b = np.where(distance < 0, N_BUCKETS, rel_bucket(distance))
    for i in range(N_BUCKETS + 1):
        out[i] = b == i
    return out


def constants():
    c = {}
    c["c_ident"] = np.eye(P, dtype=np.float32)
    half = np.arange(P) // HD
    c["c_blk"] = (half[:, None] == half[None, :]).astype(np.float32)
    c["c_dist"] = one_hot(2 * P - 1 - np.arange(BW))
    q = np.arange(TS)[:, None]
    past = PAST + q - np.arange(PAST)[None, :]
    new = q - (np.arange(NS) % TS)[None, :]
    c["c_sdist"] = one_hot(np.concatenate([past, new], 1))
    row = np.arange(P) // 32
    m = np.zeros((P, 2, NK), np.float32)
    for g in range(2):
        other = (4 * g + row)[:, None] != (np.arange(NS) // TS)[None, :]
        m[:, g, PAST:] = np.where(other, np.float32(MASKED), 0)
    c["c_smask"] = m
    s, t = np.arange(P)[:, None], np.arange(P)[None, :]
    lm = np.zeros((P, LEVELS, P), np.int32)
    lm[:, 0] = s == t
    for l in range(1, LEVELS):
        w = 2 ** l
        lm[:, l] = (s // w == t // w) & (s % w < w // 2) & (t % w >= w // 2)
    c["c_lmask"] = lm
    c["c_rowmask"] = (np.arange(NS)[:, None] // TS == np.arange(NB)[None, :]).astype(np.float32)
    c["c_rowsel"] = (np.arange(P)[:, None] // TS % 2 == np.arange(2)[None, :]).astype(np.float32)
    return c


INPUTS = ["x_prompt", "x_sample", "cache_k", "cache_v", "page_table", "state_hgrn", "state_conv", "rel_bias",
          "norm1_g", "w_in", "qk_norm_g", "lambda_qk", "subln_g", "hgrn_lb", "hgrn_onorm_g", "w_out",
          "norm2_g", "w_gate", "w_up", "conv_w", "conv_b", "w_down"]
OUTPUTS = [("y_prompt", (1, T, D)), ("y_sample", (NB, TS, D)), ("k_prompt", (T, H, P)), ("v_prompt", (T, H, P)),
           ("hgrn_prompt", (H, P, P)), ("conv_prompt", (2, FF)), ("k_sample", (NS, H, P)), ("v_sample", (NS, H, P)),
           ("hgrn_sample", (NB, H, P, P)), ("conv_sample", (NB, 2, FF))]
SHAPES = [(1, T, D), (NB, TS, D), (1, 1, T, H, 2, HD), (1, 1, T, H, P), (1, 1, H, P, P), (1, 1, 2, FF),
          (1, NB, TS, H, 2, HD), (1, NB, TS, H, P), (1, NB, H, P, P), (1, NB, 2, FF)]
SCRATCH = [("skew", (H, P, BW)), ("x_d", (P, KC, TT)), ("q_d", (H, P, TT)), ("k_d", (H, P, TT)), ("rq_d", (H, P, TT)),
           ("f_d", (H, P, TT)), ("rg_d", (H, P, TT)), ("ri_d", (H, P, NT + 1, P)), ("o_d", (2 * H, P, TT))]


def program(nc, arrays, upto=9):
    io = {}
    for name, a in arrays.items():
        io[name] = nc.dram_tensor(name, a.shape, mybir.dt.from_np(a.dtype), kind="ExternalInput").ap()
    for name, shape in OUTPUTS:
        io[name] = nc.dram_tensor(name, shape, F32, kind="ExternalOutput").ap()
    for name, shape in SCRATCH:
        io[name] = nc.dram_tensor(name, shape, F32, kind="Internal").ap()
    with ExitStack() as ctx:
        sb, ps, sem = open_memory(nc, ctx)
        keep = {n: sb(n, shape, dt) for n, shape, dt in (
            ("ident", [P, P], F32), ("blk", [P, P], F32), ("ones", [P, P], F32), ("eps", [P, 1], F32),
            ("lmask", [P, LEVELS, P], I32), ("rowmask", [NS, NB], F32), ("rowsel", [P, 2], F32), ("bias", [P, H, 2 * P], F32), ("far", [P, H], F32),
            ("sbias", [P, 2, NK], F32), ("lam", [P, 2], F32), ("lb0", [P, H], F32), ("lb1", [P, H], F32),
            ("vec", [P, NVEC], F32))}
        for name in ("dve", "act", "pool"):
            keep[f"{name}_chain"] = Chain(sem(f"{name}_done"))
        prepare(nc, io, keep)
        if upto >= 1:
            project(nc, io, keep)
        if upto >= 2:
            heads(nc, io, keep)
        if upto >= 3:
            samples(nc, io, keep)
        if upto >= 4:
            acc = sb("residual", [P, KC, TT])
            mix(nc, io, keep, acc)
            if upto >= 5:
                mlp(nc, io, keep, acc)


def kernel(**inputs):
    import concourse.bacc as bacc
    from concourse.bass_utils import run_bass_kernel_spmd

    nc = bacc.Bacc("TRN2", target_bir_lowering=False, num_devices=1)
    arrays = {n: np.ascontiguousarray(inputs[n]) for n in INPUTS}
    arrays.update(constants())
    program(nc, arrays)
    r = run_bass_kernel_spmd(nc, [arrays], core_ids=[0])
    return tuple(np.asarray(r.results[0][n]).reshape(s) for (n, _), s in zip(OUTPUTS, SHAPES))
```

```python
import math
from contextlib import ExitStack

import numpy as np
import concourse.bass as bass
from concourse import mybir

F32 = mybir.dt.float32
F32R = mybir.dt.float32r
I32 = mybir.dt.int32
ALU = mybir.AluOpType
ACT = mybir.ActivationFunctionType
AX = mybir.AxisListType

P = 128
D = 1024
KC = D // P
T = 1024
NB = 8
TS = 4
NS = NB * TS
TT = T + NS
NT = T // P
NPC = 3
PW = TT // NPC
H = 4
HD = 64
FW = H * P
PARTS = 7
FF = 2816
FC = FF // P
PAGE = 128
PAST = 256
EPS = 1e-6
MASKED = -1.0e30
LEVELS = 8
SLEVELS = 3
LAM_INIT = 0.8 - 0.6 * math.exp(0.0)
N_BUCKETS, MAX_DISTANCE = 32, 128
BW = 3 * P
NK = PAST + NS

W_SLOT = [0, 1, 0, 1, 0, 1, 2]
W_USES = [3, 3, 1]
W_NTH = [0, 0, 1, 1, 2, 2, 0]
W_BACK = [3, 3, 2, 2, 2, 2, 7]


VECTORS = {"norm1_g": (0, KC), "norm2_g": (8, KC), "conv_w": (16, 3 * FC), "conv_b": (82, FC), "qk_norm_g": (104, 2),
           "subln_g": (106, 1), "hgrn_onorm_g": (107, 1), "hgrn_lb": (108, 2 * H)}
NVEC = 116
TABLES = 19


def vector(keep, name):
    first, rows = VECTORS[name]
    return keep["vec"][:, first:first + rows]


def piece(n):
    return slice(n * PW, (n + 1) * PW)


class Chain:

    def __init__(self, sem):
        self.sem, self.n = sem, 0

    def of(self, eng):
        self.eng = eng
        return self

    def __call__(self, ins):
        ins.then_inc(self.sem, 1)
        self.n = self.n + 1
        self.eng.wait_ge(self.sem, self.n)

    def loop(self, count, per):
        return _ChainLoop(self, count, per)


class _ChainLoop:
    def __init__(self, chain, count, per):
        self.chain, self.count, self.per = chain, count, per

    def __enter__(self):
        self.start = self.chain.n
        self.fori = self.chain.eng.Fori(0, self.count)
        i = self.fori.__enter__()
        self.chain.n = 0
        self.base = i * self.per + self.start
        self.chain.n = self.base
        self.i = i
        return i

    def __exit__(self, *a):
        self.chain.n = self.start + self.count * self.per
        return self.fori.__exit__(*a)


def open_memory(nc, ctx):
    def sb(name, shape, dt=F32):
        return ctx.enter_context(nc.sbuf_tensor(name, shape, dt))

    def ps(name, shape):
        return ctx.enter_context(nc.psum_tensor(name, shape, F32))

    def sem(name):
        return ctx.enter_context(nc.semaphore(name))

    return sb, ps, sem


def prepare(nc, io, keep):
    with ExitStack() as ctx:
        sb, ps, sem = open_memory(nc, ctx)
        rel = sb("rel", [33, H])
        dist = sb("dist", [33, BW])
        sdist = sb("sdist", [33, TS, NK])
        relrow = sb("relrow", [33, H, P])
        selrow = sb("selrow", [33, TS, P])
        smask = sb("smask", [P, 2, NK])
        skew = sb("skew_rows", [P, H, BW])
        lq = sb("lq", [P, 4, HD])
        lprod = sb("lprod", [P, 2, HD])
        lsum = sb("lsum", [P, 2])
        lexp = sb("lexp", [P, 2])
        vrows = sb("vrows", [NVEC, P])
        lbm = sb("lbm", [P, H])
        lbe = sb("lbe", [P, 2, H])
        lbs = sb("lbs", [P, H])
        pb = ps("pb", [P, H, 512])
        psb = ps("psb", [P, 512])
        pvec = ps("pvec", [P, 512])
        lbr = keep["vec"][:, VECTORS["hgrn_lb"][0]:NVEC].rearrange("p (a h) -> p a h", a=2)
        gqk = vector(keep, "qk_norm_g")
        gsub = vector(keep, "subln_g")
        tables_in = sem("tables_in")
        rel_ready = sem("rel_ready")
        bias_ready = sem("bias_ready")
        skew_ready = sem("skew_ready")
        skewed = sem("skewed")
        exp_ready = sem("exp_ready")
        exp_wanted = sem("exp_wanted")

        with nc.Block() as block:
            @block.sync
            def _(sp):
                sp.dma_start(rel[0:32, :], io["rel_bias"]).then_inc(tables_in, 16)
                sp.dma_start(dist[:, :], io["c_dist"]).then_inc(tables_in, 16)
                sp.dma_start(sdist[:, :, :], io["c_sdist"]).then_inc(tables_in, 16)
                sp.dma_start(smask[:, :, :], io["c_smask"]).then_inc(tables_in, 16)
                sp.dma_start(lq[:, :, :], io["lambda_qk"].broadcast_to([P, 4, HD])).then_inc(tables_in, 16)
                sp.dma_start(keep["ident"][:, :], io["c_ident"]).then_inc(tables_in, 16)
                sp.dma_start(keep["blk"][:, :], io["c_blk"]).then_inc(tables_in, 16)
                sp.dma_start(keep["lmask"][:, :], io["c_lmask"]).then_inc(tables_in, 16)
                sp.dma_start(keep["slmask"][:, :, :], io["c_slmask"]).then_inc(tables_in, 16)
                sp.dma_start(keep["rowmask"][:, :], io["c_rowmask"]).then_inc(tables_in, 16)
                sp.dma_start(keep["rowsel"][:, :], io["c_rowsel"]).then_inc(tables_in, 16)
                for name, view in (("norm1_g", "o (k p) -> (o k) p"), ("norm2_g", "o (k p) -> (o k) p"), ("conv_w", "o j (c p) -> (o j c) p"),
                                   ("conv_b", "o (c p) -> (o c) p"), ("qk_norm_g", "o a m d -> (o a) (m d)"), ("subln_g", "o p -> o p"),
                                   ("hgrn_onorm_g", "o p -> o p"), ("hgrn_lb", "a (h p) -> (a h) p")):
                    first, rows = VECTORS[name]
                    src = io[name] if view == "o p -> o p" else io[name].rearrange(view, **({"p": P} if "(k p)" in view or "(c p)" in view or "(h p)" in view else {}))
                    sp.dma_start(vrows[first:first + rows, :], src).then_inc(tables_in, 16)
                sp.wait_ge(skew_ready, H)
                sp.dma_start(io["skew"].rearrange("h p w -> p h w"), skew[:, :, :]).then_inc(skewed, 16)
                sp.wait_ge(skewed, 16)
                for h in range(H):
                    flat = io["skew"][h].rearrange("p w -> (p w)")
                    shifted = flat[P - 1:P - 1 + P * (BW - 1)].rearrange("(p w) -> p w", w=BW - 1)
                    sp.dma_start(keep["bias"][:, h, :], shifted[:, 0:2 * P]).then_inc(skewed, 16)
                sp.wait_ge(skewed, 16 * (H + 1))

            @block.vector
            def _(dve):
                link = keep["dve_chain"].of(dve)
                v = nc.vector
                v.memset(keep["ones"][:, :], 1.0)
                v.memset(keep["eps"][:, :], EPS)
                v.memset(selrow[:, :, :], 0.0)
                link(v.memset(rel[32:33, :], MASKED))
                dve.wait_ge(tables_in, 16 * TABLES)
                v.tensor_copy(relrow[:, :, :], rel[:, :].rearrange("p (h o) -> p h o", o=1).broadcast_to([33, H, P])).then_inc(rel_ready, 1)
                for t in range(TS):
                    for b in range(4):
                        out = selrow[:, t, 32 * b:32 * b + 32].rearrange("p (h m t) -> p h m t", h=H, m=2)[:, :, :, t]
                        src = rel[:, :].rearrange("p (h o) -> p h o", o=1).broadcast_to([33, H, 2])
                        v.tensor_copy(out, src).then_inc(rel_ready, 1)
                dve.wait_ge(bias_ready, 1)
                link(v.tensor_copy(keep["vec"][:, :], pvec[:, 0:NVEC]))
                link(v.tensor_tensor(lprod[:, :, :], lq[:, 0:4:2, :], lq[:, 1:4:2, :], ALU.mult))
                v.tensor_reduce(lsum[:, :], lprod[:, :, :], AX.X, ALU.add).then_inc(exp_wanted, 1)
                link(v.tensor_tensor(lbm[:, :], lbr[:, 0, :], lbr[:, 1, :], ALU.max))
                for a in range(2):
                    last = v.tensor_tensor(lbr[:, a, :], lbr[:, a, :], lbm[:, :], ALU.subtract)
                last.then_inc(exp_wanted, 1)
                dve.wait_ge(exp_ready, 1)
                link(v.tensor_tensor(lsum[:, 0:1], lexp[:, 0:1], lexp[:, 1:2], ALU.subtract))
                link(v.tensor_scalar(keep["lam"][:, 0:1], lsum[:, 0:1], LAM_INIT, None, ALU.add))
                link(v.tensor_scalar(keep["lam"][:, 1:2], keep["lam"][:, 0:1], -1.0, None, ALU.mult))
                dve.wait_ge(exp_ready, 2)
                link(v.tensor_tensor(lbs[:, :], lbe[:, 0, :], lbe[:, 1, :], ALU.add))
                link(v.reciprocal(lbm[:, :], lbs[:, :]))
                link(v.tensor_tensor(keep["lb0"][:, :], lbe[:, 0, :], lbm[:, :], ALU.mult))
                link(v.tensor_scalar(keep["lb1"][:, :], keep["lb0"][:, :], -1.0, 1.0, ALU.mult, ALU.add))
                link(v.tensor_scalar(gqk[:, 0:1], gqk[:, 0:1], HD ** -0.5, None, ALU.mult))
                link(v.tensor_scalar(gsub, gsub, 1.0 - LAM_INIT, None, ALU.mult))
                for h in range(H):
                    dve.wait_ge(bias_ready, h + 2)
                    v.tensor_copy(skew[:, h, :], pb[:, h, 0:BW]).then_inc(skew_ready, 1)
                    link(v.tensor_copy(keep["far"][:, h:h + 1], pb[:, h, 0:1]))
                dve.wait_ge(bias_ready, H + 2)
                for g in range(2):
                    link(v.tensor_tensor(keep["sbias"][:, g, :], psb[:, 0:NK], smask[:, g, :], ALU.add))

            @block.scalar
            def _(act):
                act.wait_ge(exp_wanted, 1)
                nc.scalar.activation(lexp[:, :], lsum[:, :], ACT.Exp).then_inc(exp_ready, 1)
                act.wait_ge(exp_wanted, 2)
                nc.scalar.activation(lbe[:, :, :], lbr[:, :, :], ACT.Exp).then_inc(exp_ready, 1)

            @block.tensor
            def _(pe):
                pe.wait_ge(tables_in, 16 * TABLES)
                nc.tensor.transpose(pvec[:, 0:NVEC], vrows[:, :], keep["ident"][0:NVEC, 0:NVEC]).then_inc(bias_ready, 1)
                pe.wait_ge(rel_ready, 1)
                for h in range(H):
                    nc.tensor.matmul(pb[:, h, 0:BW], relrow[:, h, :], dist[:, :], start=True, stop=True).then_inc(bias_ready, 1)
                pe.wait_ge(rel_ready, 1 + 4 * TS)
                for t in range(TS):
                    last = nc.tensor.matmul(psb[:, 0:NK], selrow[:, t, :], sdist[:, t, :], start=(t == 0), stop=(t == TS - 1))
                last.then_inc(bias_ready, 1)


def split_weights(nc, ones, raw, hi, lo, link):
    link(nc.gpsimd.tensor_tensor(hi, raw, ones.rearrange("p (o c) -> p o c", o=1).broadcast_to(list(raw.shape)), ALU.mult))
    return nc.gpsimd.tensor_tensor(lo, raw, hi.bitcast(F32), ALU.subtract)


def split_product(nc, out, whi, wlo, hi, lo):
    chunks = hi.shape[1]
    for k in range(chunks):
        nc.tensor.matmul(out, whi[:, k, :], hi[:, k, :], start=(k == 0), stop=False)
        nc.tensor.matmul(out, whi[:, k, :], lo[:, k, :], start=False, stop=False)
        last = nc.tensor.matmul(out, wlo[:, k, :], hi[:, k, :], start=False, stop=(k == chunks - 1))
    return last



def norm_squares(nc, act, src, sq, sq_ready, sq_used):
    for k in range(KC):
        if k >= 2:
            act.wait_ge(sq_used, k - 1)
        nc.scalar.activation(sq[:, k % 2, :], src[:, k, :], ACT.Square).then_inc(sq_ready, 1)


def norm_sums(nc, pe, ones, sq, ms, sq_ready, sq_used, ms_ready):
    for k in range(KC):
        pe.wait_ge(sq_ready, k + 1)
        for n in range(NPC):
            last = nc.tensor.matmul(ms[n][:, 0:PW], ones[:, :], sq[:, k % 2, piece(n)], start=(k == 0), stop=(k == KC - 1))
            if k == KC - 1:
                last.then_inc(ms_ready, 1)
        if k < KC - 1:
            last.then_inc(sq_used, 1)


def norm_inverse(nc, act, eps, ms, rb, lnb, ms_ready, rb_ready, link):
    for n in range(NPC):
        if n:
            act.wait_ge(rb_ready, n)
        act.wait_ge(ms_ready, n + 1)
        link(nc.scalar.activation(lnb[:, :], ms[n][:, 0:PW], ACT.Ln, bias=eps[:, 0:1], scale=1.0 / D))
        nc.scalar.activation(rb[:, piece(n)], lnb[:, :], ACT.Exp, scale=-0.5).then_inc(rb_ready, 1)


def norm_high(nc, act, hf, hh, hf_ready, hi_ready):
    for n in range(NPC):
        for k in range(KC):
            j = n * KC + k
            act.wait_ge(hf_ready, j + 1)
            nc.scalar.activation(hh[:, k, piece(n)], hf[:, j % NPC, :], ACT.Copy).then_inc(hi_ready, 1)


def norm_low(nc, dve, src, gain, rb, hf, hh, hl, rb_ready, hf_ready, hi_ready, lo_ready):
    steps = [(n, k) for n in range(NPC) for k in range(KC)]

    def low(j):
        n, k = steps[j]
        dve.wait_ge(hi_ready, j + 1)
        nc.vector.tensor_tensor(hl[:, k, piece(n)], hf[:, j % NPC, :], hh[:, k, piece(n)].bitcast(F32), ALU.subtract).then_inc(lo_ready, 1)

    for j, (n, k) in enumerate(steps):
        if k == 0:
            dve.wait_ge(rb_ready, n + 1)
        if j >= NPC:
            dve.wait_ge(lo_ready, j - NPC + 1)
        nc.vector.scalar_tensor_tensor(hf[:, j % NPC, :], src[:, k, piece(n)], gain[:, k:k + 1], rb[:, piece(n)], ALU.mult, ALU.mult)\
          .then_inc(hf_ready, 1)
        if j:
            low(j - 1)
    low(len(steps) - 1)


def project(nc, io, keep):
    with ExitStack() as ctx:
        sb, ps, sem = open_memory(nc, ctx)
        xT = sb("xT", [P, KC, TT])
        hh = sb("h_hi", [P, KC, TT], F32R)
        hl = sb("h_lo", [P, KC, TT], F32R)
        raw = sb("w_raw", [P, 3, KC, P])
        whi = [sb(f"w_hi{s}", [P, KC, P], F32R) for s in range(3)]
        wlo = [sb(f"w_lo{s}", [P, KC, P], F32R) for s in range(3)]
        ZQ, ZK, ZV, ZRQ, ZRF, ZRI, ZRG = [sb(f"z_{n}", [P, TT]) for n in ("q", "k", "v", "rq", "rf", "ri", "rg")]
        tm = sb("tm", [P, 3, NT + 1, P])
        sq = sb("sq", [P, 2, TT])
        rb = sb("rb", [P, 2, TT])
        lnb = sb("lnb", [P, PW])
        hf = rb[:, 1, :].rearrange("p (s w) -> p s w", s=NPC)
        KK, LF, B, EB, KD, QD = [xT[:, k, :] for k in range(6)]
        rest = xT[:, 6:8, :].rearrange("p k t -> p (k t)")
        KDT = rest[:, 0:(NT + 1) * P].rearrange("p (t c) -> p t c", c=P)
        ends = rest[:, (NT + 1) * P:(NT + 1) * P + NT + NB]
        zp = [ps(f"z_ps{n}", [P, 512]) for n in range(NPC)]
        ms = [ps(f"ms_ps{n}", [P, 512]) for n in range(NPC)]
        tr = [ps(f"tr_ps{n}", [P, 512]) for n in range(2)]

        x_in = [sem(f"x_in{s}") for s in range(3)]
        x_tr = [sem(f"x_tr{b}") for b in range(2)]
        x_ev = [sem(f"x_ev{b}") for b in range(2)]
        sq_ready = sem("sq_ready")
        ms_ready = sem("ms_ready")
        sq_used = sem("sq_used")
        rb_ready = sem("rb_ready")
        hf_ready = sem("hf_ready")
        hi_ready = sem("hi_ready")
        lo_ready = sem("lo_ready")
        raw_in = [sem(f"raw_in{s}") for s in range(3)]
        w_ready = sem("w_ready")
        z_ready = sem("z_ready")
        z_free = sem("z_free")
        qk_ms = sem("qk_ms")
        qk_rb = sem("qk_rb")
        qk_normed = sem("qk_normed")
        tr_ready = [sem(f"tr_ready{b}") for b in range(2)]
        tr_free = [sem(f"tr_free{b}") for b in range(2)]
        f_ready = sem("f_ready")
        lf_ready = sem("lf_ready")
        b_ready = sem("b_ready")
        eb_ready = sem("eb_ready")
        dk_ready = sem("dk_ready")
        ek_ready = sem("ek_ready")
        kd_ready = sem("kd_ready")
        qd_ready = sem("qd_ready")
        NAMES = ("q", "k", "kt", "v", "rq", "kk", "b", "qd", "kd", "ri", "rg")
        STORES = {n: {"kt": 32, "v": 32, "ri": 32, "kd": 48}.get(n, 16) for n in NAMES}
        stored = {n: sem(f"stored_{n}") for n in NAMES}
        x_stored = sem("x_stored")

        w_view = io["w_in"][0].rearrange("(k p) (t h c) -> p t k h c", p=P, t=PARTS, h=H)
        W0, Z0, F0, R0, N0 = PARTS, NPC * PARTS, NPC, 1, 2 * NPC
        TR_PER = (8, 4)

        def split_at(h, c):
            return h * PARTS + (W0 + c)

        def summed(h, c, n):
            return h * (NPC * PARTS) + (Z0 + NPC * c + n + 1)

        def copied(h, c, n):
            return h * (NPC * PARTS) + (F0 + NPC * c + n + 1)

        def normed(h, i):
            return h * (2 * NPC) + (N0 + NPC * i + NPC)

        def token_major(h, i):
            return h * TR_PER[0] + (R0 + 2 * i + 2)

        with nc.Block() as block:
            @block.sync
            def _(sp):
                for s, n in ((w_ready, W0), (z_ready, Z0), (z_free, F0), (tr_free[0], R0), (tr_free[1], R0), (qk_normed, N0), (qk_rb, N0)):
                    sp.sem_inc(s, n)
                for n in NAMES:
                    sp.sem_inc(stored[n], STORES[n])
                sp.sem_inc(qd_ready, 1)
                for t in range(NT + 1):
                    rows = P if t < NT else NS
                    if t >= 3:
                        sp.wait_ge(x_tr[1], t - 2)
                    src = io["x_prompt"][0, t * P:(t + 1) * P, :] if t < NT else io["x_sample"].rearrange("b t d -> (b t) d")
                    sp.dma_start(tm[0:rows, t % 3, 0:KC, :].rearrange("p k c -> p (k c)"), src).then_inc(x_in[t % 3], 16)
                sp.wait_ge(x_ev[0], NT + 1)
                sp.wait_ge(x_ev[1], NT + 1)
                sp.dma_start(io["x_d"], xT[:, :, :]).then_inc(x_stored, 16)
                with sp.Fori(0, H) as h:
                    def load(c):
                        sp.wait_ge(w_ready, split_at(h, c) - (W_BACK[c] - 1))
                        sp.dma_start(raw[:, W_SLOT[c], :, :], w_view[:, c, :, bass.ds(h, 1), :].rearrange("p k o c -> p k (o c)"))\
                          .then_inc(raw_in[W_SLOT[c]], 16)

                    def store(name, src, ready, value):
                        sp.wait_ge(ready, value)
                        sp.dma_start(io[name + "_d"][bass.ds(h, 1)].rearrange("o p t -> p (o t)"), src[:, :]).then_inc(stored[name], 16)

                    def store_tokens(name, prompt, sample, i):
                        sp.wait_ge(tr_free[0], token_major(h, i))
                        sp.dma_start(prompt.rearrange("(t p) h c -> h p t c", p=P)[bass.ds(h, 1)].rearrange("o p t c -> p (o t) c"),
                                     tm[:, i, 0:NT, :]).then_inc(stored[name], 16)
                        sp.dma_start(sample.rearrange("t h c -> h t c")[bass.ds(h, 1)].rearrange("o t c -> t (o c)"),
                                     tm[0:NS, i, NT, :]).then_inc(stored[name], 16)

                    load(0)
                    load(1)
                    load(2)
                    load(3)
                    store("q", ZQ, qk_normed, normed(h, 0))
                    load(4)
                    store("k", ZK, qk_normed, normed(h, 1))
                    load(5)
                    store_tokens("kt", io["k_prompt"], io["k_sample"], 0)
                    store("rq", ZRQ, z_free, copied(h, 3, NPC - 1))
                    store_tokens("v", io["v_prompt"], io["v_sample"], 1)
                    load(6)
                for n in ("q", "k", "kt", "v", "rq"):
                    sp.wait_ge(stored[n], STORES[n] * (H + 1))
                sp.wait_ge(x_stored, 16)

            @block.gpsimd
            def _(pool):
                link = keep["pool_chain"].of(pool)
                with link.loop(H, PARTS) as h:
                    for c in range(PARTS):
                        s = W_SLOT[c]
                        pool.wait_ge(raw_in[s], h * (16 * W_USES[s]) + 16 * (W_NTH[c] + 1))
                        pool.wait_ge(z_ready, h * (NPC * PARTS) + (Z0 + NPC * (c - W_BACK[c] + 1)))
                        split_weights(nc, keep["ones"][:, :], raw[:, s, :, :], whi[s][:, :, :], wlo[s][:, :, :], link).then_inc(w_ready, 1)

            @block.tensor
            def _(pe):
                for t in range(NT + 1):
                    rows = P if t < NT else NS
                    pe.wait_ge(x_in[t % 3], 16 * (t // 3 + 1))
                    for half in range(2):
                        if t:
                            pe.wait_ge(x_ev[half], t)
                        for j in range(4):
                            last = nc.tensor.transpose(tr[half][:, j * P:j * P + rows], tm[0:rows, t % 3, half * 4 + j, :], keep["ident"][0:rows, 0:rows])
                        last.then_inc(x_tr[half], 1)
                norm_sums(nc, pe, keep["ones"], sq, ms, sq_ready, sq_used, ms_ready)

                with pe.Fori(0, H) as h:
                    def main(c, n):
                        s = W_SLOT[c]
                        if n == 0:
                            pe.wait_ge(w_ready, split_at(h, c) + 1)
                        if c == 0:
                            pe.wait_ge(lo_ready, KC * (n + 1))
                        pe.wait_ge(z_free, copied(h, c, n) - NPC)
                        split_product(nc, zp[n][:, 0:PW], whi[s], wlo[s], hh[:, :, piece(n)], hl[:, :, piece(n)]).then_inc(z_ready, 1)

                    def sums(i):
                        for n in range(NPC):
                            pe.wait_ge(z_free, copied(h, i, n))
                            if i:
                                pe.wait_ge(qk_rb, h * (2 * NPC) + (N0 + n + 1))
                            nc.tensor.matmul(ms[n][:, 0:PW], keep["blk"][:, :], sq[:, i, piece(n)], start=True, stop=True).then_inc(qk_ms, 1)

                    def tokens(i, src, ready, value):
                        pe.wait_ge(ready, value)
                        for b, first, end, use in ((0, 0, 4, 2 * i), (1, 4, 8, i), (0, 8, 9, 2 * i + 1)):
                            pe.wait_ge(tr_free[b], h * TR_PER[b] + (use + R0))
                            for t in range(first, end):
                                rows = P if t < NT else NS
                                last = nc.tensor.transpose(tr[b][0:rows, (t - first) * P:(t - first + 1) * P], src[:, t * P:t * P + rows], keep["ident"][:, :])
                            last.then_inc(tr_ready[b], 1)

                    main(0, 0), main(0, 1), main(0, 2)
                    main(1, 0), sums(0), main(1, 1), main(1, 2)
                    main(2, 0), sums(1), main(2, 1), main(2, 2)
                    main(3, 0), tokens(0, ZK, qk_normed, normed(h, 1)), main(3, 1)
                    tokens(1, ZV, z_free, copied(h, 2, NPC - 1)), main(3, 2)
                    main(4, 0), main(4, 1), main(4, 2)
                    main(5, 0), main(5, 1), main(5, 2)
                    main(6, 0), tokens(2, ZRI, z_free, copied(h, 5, NPC - 1)), main(6, 1), tokens(3, KD, kd_ready, h + 1), main(6, 2)

            @block.scalar
            def _(act):
                a = nc.scalar.activation
                link = keep["act_chain"].of(act)
                for t in range(NT + 1):
                    rows = P if t < NT else NS
                    act.wait_ge(x_tr[1], t + 1)
                    a(xT[:, 4:8, t * P:t * P + rows], tr[1][:, :].rearrange("p (k c) -> p k c", k=4)[:, :, 0:rows], ACT.Copy).then_inc(x_ev[1], 1)
                act.wait_ge(x_ev[0], NT + 1)
                act.wait_ge(x_ev[1], NT + 1)
                norm_squares(nc, act, xT, sq, sq_ready, sq_used)
                norm_inverse(nc, act, keep["eps"], ms, rb[:, 0, :], lnb, ms_ready, rb_ready, link)
                norm_high(nc, act, hf, hh, hf_ready, hi_ready)

                with link.loop(H, 2 * NPC) as h:
                    def free(name):
                        act.wait_ge(stored[name], h * STORES[name] + STORES[name])

                    def copy(c, n, dst, func=ACT.Copy):
                        act.wait_ge(z_ready, summed(h, c, n))
                        return a(dst[:, piece(n)], zp[n][:, 0:PW], func)

                    def squared(c, n, dst):
                        copy(c, n, dst)
                        a(sq[:, c, piece(n)], zp[n][:, 0:PW], ACT.Square).then_inc(z_free, 1)

                    def inverse(i):
                        for n in range(NPC):
                            act.wait_ge(qk_rb, h * (2 * NPC) + (N0 + NPC * i + n))
                            act.wait_ge(qk_ms, h * (2 * NPC) + (NPC * i + n + 1))
                            link(a(lnb[:, :], ms[n][:, 0:PW], ACT.Ln, bias=keep["eps"][:, 0:1], scale=1.0 / HD))
                            a(rb[:, i, piece(n)], lnb[:, :], ACT.Exp, scale=-0.5).then_inc(qk_rb, 1)

                    free("q")
                    for n in range(NPC):
                        squared(0, n, ZQ)
                    free("k")
                    squared(1, 0, ZK)
                    inverse(0)
                    squared(1, 1, ZK), squared(1, 2, ZK)
                    free("v")
                    copy(2, 0, ZV).then_inc(z_free, 1)
                    inverse(1)
                    copy(2, 1, ZV).then_inc(z_free, 1), copy(2, 2, ZV).then_inc(z_free, 1)
                    free("rq")
                    act.wait_ge(qd_ready, h + 1)
                    for n in range(NPC):
                        copy(3, n, ZRQ).then_inc(z_free, 1)
                    for n in range(NPC):
                        copy(4, n, ZRF, ACT.Sigmoid).then_inc(z_free, 1)
                    free("ri")
                    copy(5, 0, ZRI).then_inc(z_free, 1)
                    act.wait_ge(f_ready, h * 2 + 1)
                    a(LF, ZRF[:, :], ACT.Ln).then_inc(lf_ready, 1)
                    copy(5, 1, ZRI).then_inc(z_free, 1)
                    act.wait_ge(b_ready, h + 1)
                    a(EB, B, ACT.Exp).then_inc(eb_ready, 1)
                    act.wait_ge(dk_ready, h + 1)
                    a(KD, KD, ACT.Exp).then_inc(ek_ready, 1)
                    copy(5, 2, ZRI).then_inc(z_free, 1)
                    free("rg")
                    for n in range(NPC):
                        copy(6, n, ZRG, ACT.Silu).then_inc(z_free, 1)
                    for name, src, ready in (("kk", KK, f_ready), ("b", B, b_ready), ("qd", QD, qd_ready)):
                        act.wait_ge(ready, {"kk": h * 2 + 2, "b": h + 1, "qd": h + 2}[name])
                        act.dma_start(io[name + "_d"][bass.ds(h, 1)].rearrange("o p t -> p (o t)"), src).then_inc(stored[name], 16)
                    act.wait_ge(tr_free[0], token_major(h, 2))
                    for name, src in (("ri", tm[:, 2]), ("kd", KDT)):
                        if name == "kd":
                            act.wait_ge(tr_free[0], token_major(h, 3))
                        act.dma_start(io[name + "_d"][bass.ds(h, 1)].rearrange("o p t c -> p (o t) c")[:, 0:NT, :], src[:, 0:NT, :]).then_inc(stored[name], 16)
                        act.dma_start(io[name + "_d"][bass.ds(h, 1)].rearrange("o p t c -> p (o t) c")[0:NS, NT, :], src[0:NS, NT, :]).then_inc(stored[name], 16)
                    act.dma_start(io["ends_d"][bass.ds(h, 1)].rearrange("o p t -> p (o t)"), ends).then_inc(stored["kd"], 16)
                    act.wait_ge(z_free, copied(h, 6, NPC - 1))
                    act.dma_start(io["rg_d"][bass.ds(h, 1)].rearrange("o p t -> p (o t)"), ZRG[:, :]).then_inc(stored["rg"], 16)
                for n in ("kk", "b", "qd", "kd", "ri", "rg"):
                    act.wait_ge(stored[n], STORES[n] * (H + 1))

            @block.vector
            def _(dve):
                v = nc.vector
                for t in range(NT + 1):
                    rows = P if t < NT else NS
                    dve.wait_ge(x_tr[0], t + 1)
                    v.tensor_copy(xT[:, 0:4, t * P:t * P + rows], tr[0][:, :].rearrange("p (k c) -> p k c", k=4)[:, :, 0:rows]).then_inc(x_ev[0], 1)
                dve.wait_ge(x_ev[1], NT + 1)
                norm_low(nc, dve, xT, vector(keep, "norm1_g"), rb[:, 0, :], hf, hh, hl, rb_ready, hf_ready, hi_ready, lo_ready)
                dve.wait_ge(x_stored, 16)
                dve.wait_ge(lo_ready, KC * NPC)

                with dve.Fori(0, H) as h:
                    def scale(i, z):
                        for n in range(NPC):
                            dve.wait_ge(qk_rb, h * (2 * NPC) + (N0 + NPC * i + n + 1))
                            v.scalar_tensor_tensor(z[:, piece(n)], z[:, piece(n)], vector(keep, "qk_norm_g")[:, i:i + 1], rb[:, i, piece(n)],
                                                   ALU.mult, ALU.mult).then_inc(qk_normed, 1)

                    def tokens(i, name, dst):
                        dve.wait_ge(stored[name], h * STORES[name] + STORES[name])
                        for b, first, end, use in ((0, 0, 4, 2 * i), (1, 4, 8, i), (0, 8, 9, 2 * i + 1)):
                            dve.wait_ge(tr_ready[b], h * TR_PER[b] + (use + 1))
                            rows = P if first < NT else NS
                            v.tensor_copy(dst[0:rows, first:end, :].rearrange("p t c -> p (t c)"), tr[b][0:rows, 0:(end - first) * P]).then_inc(tr_free[b], 1)

                    scale(0, ZQ)
                    scale(1, ZK)
                    tokens(0, "kt", tm[:, 0])
                    tokens(1, "v", tm[:, 1])
                    dve.wait_ge(z_free, copied(h, 4, NPC - 1))
                    v.tensor_scalar(ZRF[:, :], ZRF[:, :], keep["lb1"][:, bass.ds(h, 1)], keep["lb0"][:, bass.ds(h, 1)], ALU.mult, ALU.add).then_inc(f_ready, 1)
                    dve.wait_ge(f_ready, h * 2 + 1)
                    dve.wait_ge(stored["kk"], h * 16 + 16)
                    v.tensor_scalar(KK, ZRF[:, :], -1.0, 1.0, ALU.mult, ALU.add).then_inc(f_ready, 1)
                    dve.wait_ge(stored["b"], h * 16 + 16)
                    dve.wait_ge(lf_ready, h + 1)
                    for first, n, w in ((0, NT, P), (T, NB, TS)):
                        for t in range(first, first + n * w, w):
                            last = v.tensor_tensor_scan(B[:, t:t + w], keep["ones"][:, 0:w], LF[:, t:t + w], 0.0, ALU.mult, ALU.add)
                    last.then_inc(b_ready, 1)
                    dve.wait_ge(b_ready, h + 1)
                    for first, n, w in ((0, NT, P), (T, NB, TS)):
                        view = B[:, first:first + n * w].rearrange("p (n w) -> p n w", w=w)
                        last = v.tensor_tensor(KD[:, first:first + n * w].rearrange("p (n w) -> p n w", w=w), view[:, :, w - 1:w].broadcast_to([P, n, w]), view, ALU.subtract)
                    last.then_inc(dk_ready, 1)
                    tokens(2, "ri", tm[:, 2])
                    dve.wait_ge(eb_ready, h + 1)
                    dve.wait_ge(stored["qd"], h * 16 + 16)
                    v.tensor_tensor(QD, ZRQ[:, :], EB, ALU.mult).then_inc(qd_ready, 1)
                    dve.wait_ge(stored["kd"], h * 48 + 48)
                    v.tensor_copy(ends[:, 0:NT], EB[:, P - 1:T:P])
                    v.tensor_copy(ends[:, NT:NT + NB], EB[:, T + TS - 1:TT:TS])
                    dve.wait_ge(ek_ready, h + 1)
                    v.tensor_tensor(KD, KD, KK, ALU.mult).then_inc(kd_ready, 1)
                    tokens(3, "kd", KDT)


L_USE = {0: 0, 1: 4, 2: 5, 3: 7, 4: 8, 5: 11, 6: 12, 7: 13}
SG_USE, U_USE, SU_USE, O_USE, SO_USE = 6, 2, 9, 14, 16
REC_USES = 17
REC_PER = (9, 8)
REC_SLOT = [(0, 1), (2, 3), (4, 5, 6), (7, 8), (9, 10), (11,12), (13,), (14,), (15, 16)]
LEVEL_SLOT = [(2, 3), (4,), (5,), (6,), (7,), (), (), ()]
AHEAD = (1,)
HP = P // 2
KDM_SLOT = 3
T_GROUPS = [(i + 4) // 4 for i in range(NT)]
T_FIRST = [sum(T_GROUPS[:i]) for i in range(NT)]
T_PER = sum(T_GROUPS)


def blocks_of(x, w, n):
    return x[:, 0:n].rearrange("p (b s w) -> p b s w", s=2, w=w // 2)


def heads(nc, io, keep):
    with ExitStack() as ctx:
        sb, ps, sem = open_memory(nc, ctx)
        Q = [sb(f"q{p}", [P, 2, T]) for p in range(2)]
        K = [sb(f"k{p}", [P, T]) for p in range(2)]
        V = [sb(f"v{p}", [P, NT, P]) for p in range(2)]
        RQ = [sb(f"rq{p}", [P, TT]) for p in range(2)]
        KK = [sb(f"kk{p}", [P, TT]) for p in range(2)]
        B = [sb(f"b{p}", [P, TT]) for p in range(2)]
        QD = [sb(f"qd{p}", [P, TT]) for p in range(2)]
        KDT = [sb(f"kdt{p}", [P, NT + 1, P]) for p in range(2)]
        ends = [sb(f"ends{p}", [P, NT + NB]) for p in range(2)]
        RI = [sb(f"ri{p}", [P, NT + 1, P]) for p in range(2)]
        OA = [sb(f"oa{p}", [P, T]) for p in range(2)]
        OR = [sb(f"or{p}", [P, TT]) for p in range(2)]
        gates = sb("gates", [1, LEVELS + 1 + SLEVELS])
        near = sb("near", [P, 2, 2 * P])
        E = sb("E", [P, 2, T])
        A = [sb(f"A{p}", [P, T]) for p in range(2)]
        At = [sb(f"At{p}", [P, T]) for p in range(2)]
        mx = sb("mx", [P, 2, 2])
        negm = sb("negm", [P, 2])
        farb = sb("farb", [P, 2])
        ls = sb("ls", [P, 2, 2])
        lt = sb("lt", [P, 2])
        rl = sb("rl", [P, 2])
        c1 = sb("c1", [P, 1])
        X = [sb(f"X{p}", [P, TT]) for p in range(1, LEVELS)]
        KDM = sb("KDM", [NS, NB, P])
        AT = sb("AT", [P, NT, P])
        ATS = sb("ATS", [NS, NS])
        ST = sb("ST", [P, NT + 1, P])
        SIN = sb("SIN", [P, NB, P])
        SOUT = sb("SOUT", [P, NB, P])
        S = ps("S", [P, 2, T])
        trp = ps("trp", [P, 512])
        pvp = ps("pvp", [P, 512])
        rec = [ps(f"rec{p}", [P, 512]) for p in range(2)]

        early_in = [sem(f"early_in{p}") for p in range(2)]
        loaded = [sem(f"loaded{p}") for p in range(2)]
        states_in = sem("states_in")
        s_ready = sem("s_ready")
        small = sem("small")
        mx_ready = sem("mx_ready")
        e_ready = sem("e_ready")
        a_ready = sem("a_ready")
        t_ready = sem("t_ready")
        t_free = sem("t_free")
        pv_ready = sem("pv_ready")
        pv_free = sem("pv_free")
        d_ready = sem("d_ready")
        ex_ready = sem("ex_ready")
        x_ready = sem("x_ready")
        kdm_ready = sem("kdm_ready")
        zeroed = sem("zeroed")
        rec_ready = [sem(f"rec_ready{p}") for p in range(2)]
        rec_free = [sem(f"rec_free{p}") for p in range(2)]
        oa_stored = [sem(f"oa_stored{p}") for p in range(2)]
        or_stored = [sem(f"or_stored{p}") for p in range(2)]
        st_stored = sem("st_stored")
        so_stored = sem("so_stored")
        LOADS = 7 * 16
        SMALL = sum(11 if i > 1 else 6 for i in range(NT)) + (SLEVELS - 1) + 6

        def ready(h, u):
            return h * REC_PER[u % 2] + (REC_PER[u % 2] + u // 2 + 1)

        def ready_before(h, u):
            return h * REC_PER[u % 2] + (u // 2 + 1)

        freed = ready

        def each_head(eng, body):
            with eng.Fori(0, H // 2) as pair:
                for par in range(2):
                    body(pair * 2 + par, par, pair)

        with nc.Block() as block:
            @block.sync
            def _(sp):
                for s in (t_free, pv_free, t_ready):
                    sp.sem_inc(s, 1)
                for b in range(2):
                    sp.sem_inc(rec_ready[b], REC_PER[b])
                    sp.sem_inc(rec_free[b], REC_PER[b])
                for s in (*oa_stored, *or_stored, st_stored, so_stored):
                    sp.sem_inc(s, 16)

                def load(h):
                    p = h % 2
                    for ready, copies in ((early_in, ((Q[p][0:HD, 0, :], io["q_d"][h, 0:HD, 0:T]), (Q[p][HD:P, 1, :], io["q_d"][h, HD:P, 0:T]), (K[p][:, :], io["k_d"][h, :, 0:T]),
                                                      (B[p][:, :], io["b_d"][h]), (KK[p][:, :], io["kk_d"][h]), (RQ[p][:, :], io["rq_d"][h]))),
                                          (loaded, ((V[p][:, :, :], io["v_prompt"].rearrange("(t p) h c -> h p t c", p=P)[h]),
                                                    (KDT[p][:, 0:NT, :], io["kd_d"][h, :, 0:NT, :]), (KDT[p][0:NS, NT, :], io["kd_d"][h, 0:NS, NT, :]),
                                                    (RI[p][:, 0:NT, :], io["ri_d"][h, :, 0:NT, :]), (RI[p][0:NS, NT, :], io["ri_d"][h, 0:NS, NT, :]),
                                                    (QD[p][:, :], io["qd_d"][h]), (ends[p][:, :], io["ends_d"][h])))):
                        for dst, src in copies:
                            sp.dma_start(dst, src).then_inc(ready[p], 16)

                def states(h):
                    sp.dma_start(SIN[:, :, :], io["state_hgrn"][0].rearrange("b h k v -> h k b v")[h]).then_inc(states_in, 16)

                load(0)
                states(0)
                load(1)
                for h in range(H):
                    p = h % 2
                    sp.wait_ge(rec_free[(U_USE + 1) % 2], freed(h, U_USE + 1))
                    sp.dma_start(io["hgrn_prompt"][h], ST[:, NT, :]).then_inc(st_stored, 16)
                    sp.wait_ge(rec_free[(SU_USE + 1) % 2], freed(h, SU_USE + 1))
                    sp.dma_start(io["hgrn_sample"].rearrange("b h k v -> h k b v")[h], SOUT[:, :, :]).then_inc(so_stored, 16)
                    sp.wait_ge(rec_free[SO_USE % 2], freed(h, SO_USE))
                    if h + 1 < H:
                        states(h + 1)
                    sp.wait_ge(rec_free[(O_USE + 1) % 2], freed(h, O_USE + 1))
                    sp.dma_start(io["o_d"][H + h], OR[p][:, :]).then_inc(or_stored[p], 16)
                    sp.wait_ge(pv_free, h * NT + NT + 1)
                    sp.dma_start(io["o_d"][h, :, 0:T], OA[p][:, :]).then_inc(oa_stored[p], 16)
                    if h + 2 < H:
                        load(h + 2)
                for p in range(2):
                    sp.wait_ge(oa_stored[p], 16 * 3)
                    sp.wait_ge(or_stored[p], 16 * 3)
                sp.wait_ge(st_stored, 16 * (H + 1))
                sp.wait_ge(so_stored, 16 * (H + 1))

            @block.gpsimd
            def _(pool):
                tt = nc.gpsimd.tensor_tensor

                def body(h, par, pair):
                    def tokens(l):
                        return TT if l < SLEVELS else T

                    def distances(l):
                        bl, xl = blocks_of(B[par], 2 ** l, tokens(l)), blocks_of(X[l - 1], 2 ** l, tokens(l))
                        w = 2 ** l // 2
                        mid = bl[:, :, 0, w - 1:w].broadcast_to([P, tokens(l) // (2 * w), w])
                        u = SG_USE if l < SLEVELS else L_USE[l]
                        pool.wait_ge(rec_ready[u % 2], ready_before(h, u))
                        tt(xl[:, :, 0, :], mid, bl[:, :, 0, :], ALU.subtract)
                        tt(xl[:, :, 1, :], bl[:, :, 1, :], mid, ALU.subtract).then_inc(d_ready, 1)

                    def weigh(l):
                        xl = blocks_of(X[l - 1], 2 ** l, tokens(l))
                        pool.wait_ge(ex_ready, h * (LEVELS - 1) + l)
                        tt(xl[:, :, 0, :], xl[:, :, 0, :], blocks_of(KK[par], 2 ** l, tokens(l))[:, :, 0, :], ALU.mult)
                        tt(xl[:, :, 1, :], xl[:, :, 1, :], blocks_of(RQ[par], 2 ** l, tokens(l))[:, :, 1, :], ALU.mult).then_inc(x_ready, 1)

                    pool.wait_ge(early_in[par], pair * 96 + 96)
                    distances(1), distances(2)
                    for l in range(1, LEVELS - 2):
                        weigh(l), distances(l + 2)
                    weigh(LEVELS - 2), weigh(LEVELS - 1)

                each_head(pool, body)

            @block.tensor
            def _(pe):
                mm = nc.tensor.matmul

                def body(h, par, pair):
                    def scores(i):
                        if i == 0:
                            pe.wait_ge(early_in[par], pair * 96 + 96)
                        n = (i + 1) * P
                        for m in range(2):
                            pe.wait_ge(e_ready, h * (2 * NT) + (2 * i + m + 1))
                            for c in range(0, n, 512):
                                w = min(512, n - c)
                                last = mm(S[:, m, c:c + w], Q[par][:, m, i * P:(i + 1) * P], K[par][:, c:c + w], start=True, stop=True)
                            last.then_inc(s_ready, 1)

                    def attend(i, uses):
                        uses = list(uses)

                        def between():
                            if uses:
                                recur(uses.pop(0))

                        def values(first, end):
                            pe.wait_ge(t_free, h * T_PER + (T_FIRST[i] + first // 4 + 2))
                            for j in range(first, end):
                                last = mm(pvp[:, 0:P], V[par][:, j, :], At[i % 2][:, j * P:(j + 1) * P], start=(j == 0), stop=(j == i))
                            return last

                        if i == 0:
                            pe.wait_ge(loaded[par], pair * LOADS + LOADS)
                        pe.wait_ge(a_ready, h * NT + (i + 1))
                        for g in range(T_GROUPS[i]):
                            pe.wait_ge(t_free, h * T_PER + (T_FIRST[i] + g + 1))
                            for j in range(4 * g, min(4 * g + 4, i + 1)):
                                last = nc.tensor.transpose(trp[:, (j % 4) * P:(j % 4 + 1) * P], A[i % 2][:, j * P:(j + 1) * P], keep["ident"][:, :])
                            last.then_inc(t_ready, 1)
                            between()
                        pe.wait_ge(pv_free, h * NT + (i + 1))
                        for j in range(0, i + 1, 4):
                            last = values(j, min(j + 4, i + 1))
                        last.then_inc(pv_ready, 1)
                        for u in uses:
                            recur(u)

                    def recur(u):
                        bank = rec[u % 2]
                        pe.wait_ge(rec_free[u % 2], freed(h, u) - 1)
                        if u in (L_USE[0], L_USE[0] + 1):
                            pe.wait_ge(early_in[par], pair * 96 + 96)
                            for j in range(4):
                                t = slice((4 * (u - L_USE[0]) + j) * P, (4 * (u - L_USE[0]) + j + 1) * P)
                                last = mm(bank[:, j * P:(j + 1) * P], KK[par][:, t], RQ[par][:, t], start=True, stop=True)
                        for l in range(1, LEVELS):
                            if u == L_USE[l]:
                                pe.wait_ge(x_ready, h * (LEVELS - 1) + l)
                                for t in range(NT):
                                    tile = X[l - 1][:, t * P:(t + 1) * P]
                                    last = mm(bank[:, t * HP:(t + 1) * HP], tile, blocks_of(tile, 2 ** l, P)[:, :, 1, :], start=True, stop=True)
                        if u == SG_USE:
                            for l in range(SLEVELS):
                                left, right = (KK[par], RQ[par]) if l == 0 else (X[l - 1],) * 2
                                last = mm(bank[0:NS, l * NS:(l + 1) * NS], left[:, T:TT], right[:, T:TT], start=True, stop=True)
                        if U_USE <= u < U_USE + 2:
                            for j in range(4):
                                t = 4 * (u - U_USE) + j
                                last = mm(bank[:, j * P:(j + 1) * P], KDT[par][:, t, :], RI[par][:, t, :], start=True, stop=True)
                        if SU_USE <= u < SU_USE + 2:
                            pe.wait_ge(kdm_ready, h + 1)
                            for j in range(4):
                                last = mm(bank[:, j * P:(j + 1) * P], KDM[:, 4 * (u - SU_USE) + j, :], RI[par][0:NS, NT, :], start=True, stop=True)
                        if O_USE <= u < O_USE + 2:
                            if u == O_USE:
                                pe.wait_ge(rec_free[(U_USE + 1) % 2], freed(h, U_USE + 1))
                            for j in range(4):
                                t = 4 * (u - O_USE) + j
                                out = bank[:, j * P:(j + 1) * P]
                                mm(out, RI[par][:, t, :], AT[:, t, :], start=True, stop=False)
                                last = mm(out, ST[:, t, :], QD[par][:, t * P:(t + 1) * P], start=False, stop=True)
                        if u == SO_USE:
                            pe.wait_ge(states_in, 16 * h + 16)
                            mm(bank[:, 0:NS], RI[par][0:NS, NT, :], ATS[:, :], start=True, stop=False)
                            for s in range(NB):
                                last = mm(bank[:, s * TS:(s + 1) * TS], SIN[:, s, :], QD[par][:, T + s * TS:T + (s + 1) * TS], start=False, stop=(s == NB - 1))
                        last.then_inc(rec_ready[u % 2], 1)

                    for i in range(NT):
                        scores(i)
                        if i:
                            attend(i - 1, REC_SLOT[i])
                        else:
                            for u in REC_SLOT[i]:
                                recur(u)
                    for u in REC_SLOT[NT]:
                        recur(u)
                    attend(NT - 1, ())

                pe.wait_ge(zeroed, 2)
                each_head(pe, body)

            @block.scalar
            def _(act):
                a = nc.scalar.activation
                act.sem_inc(e_ready, 2)

                def level(l, ahead=0, h=0):
                    n = TT if l < SLEVELS else T
                    act.wait_ge(d_ready, h * (LEVELS - 1) + (ahead * (LEVELS - 1) + l))
                    a(X[l - 1][:, 0:n], X[l - 1][:, 0:n], ACT.Exp).then_inc(ex_ready, 1)

                def body(h, par, pair, last=False):
                    def exponentials(i):
                        n0 = max(0, i - 1) * P
                        n1 = (i + 1) * P
                        for m in range(2):
                            act.wait_ge(mx_ready, h * (2 * NT) + (2 * i + m + 1))
                            if n0:
                                a(E[:, m, 0:n0], S[:, m, 0:n0], ACT.Exp, bias=farb[:, m:m + 1], accum_out=ls[:, m, 1:2])
                            a(E[:, m, n0:n1], near[:, m, 2 * P - (n1 - n0):2 * P], ACT.Exp, bias=negm[:, m:m + 1], accum_out=ls[:, m, 0:1]).then_inc(e_ready, 1)

                    def transposed(i):
                        for g in range(T_GROUPS[i]):
                            act.wait_ge(t_ready, h * T_PER + (T_FIRST[i] + g + 2))
                            w = min(4, i + 1 - 4 * g) * P
                            a(At[i % 2][:, 4 * g * P:4 * g * P + w], trp[:, 0:w], ACT.Copy).then_inc(t_free, 1)

                    def attended(i):
                        if i == 0:
                            act.wait_ge(oa_stored[par], pair * 16 + 16)
                        act.wait_ge(pv_ready, h * NT + (i + 1))
                        a(OA[par][:, i * P:(i + 1) * P], pvp[:, 0:P], ACT.Copy).then_inc(pv_free, 1)

                    def consume(u):
                        if u in range(O_USE, SO_USE + 1):
                            if u == O_USE:
                                act.wait_ge(or_stored[par], pair * 16 + 16)
                            act.wait_ge(rec_ready[u % 2], ready(h, u))
                            c, n = (u - O_USE) * 512, 512 if u < SO_USE else NS
                            a(OR[par][:, c:c + n], rec[u % 2][:, 0:n], ACT.Copy).then_inc(rec_free[u % 2], 1)

                    for i in range(NT):
                        if i:
                            transposed(i - 1)
                        exponentials(i)
                        if i:
                            attended(i - 1)
                        for u in REC_SLOT[i]:
                            consume(u)
                        for l in LEVEL_SLOT[i]:
                            level(l, 0, h)
                        if i == NT - 2 and not last:
                            for l in AHEAD:
                                level(l, 1, h)
                    for u in REC_SLOT[NT]:
                        consume(u)
                    transposed(NT - 1)
                    attended(NT - 1)

                for l in AHEAD:
                    level(l)
                with act.Fori(0, H // 2 - 1) as pair:
                    for par in range(2):
                        body(pair * 2 + par, par, pair)
                for par in range(2):
                    body(H - 2 + par, par, H // 2 - 1, last=(par == 1))

            @block.vector
            def _(dve):
                v = nc.vector
                for p in range(2):
                    v.memset(Q[p][HD:P, 0, :], 0.0)
                    v.memset(Q[p][0:HD, 1, :], 0.0).then_inc(zeroed, 1)
                v.memset(AT[:, :, :], 0.0)
                v.memset(ATS[:, :], 0.0)
                keep["dve_chain"].of(dve)(v.memset(ST[:, 0, :], 0.0))

                def body(h, par, pair):
                    count, gated = [0], [0]

                    def link(ins):
                        ins.then_inc(small, 1)
                        count[0] += 1
                        dve.wait_ge(small, h * SMALL + count[0])

                    def gate():
                        v.memset(gates[:, gated[0]:gated[0] + 1], 0.0)
                        gated[0] += 1

                    def maxima(i):
                        n0, n1 = max(0, i - 1) * P, (i + 1) * P
                        w = n1 - n0
                        bias = keep["bias"][:, bass.ds(h, 1), 2 * P - w:2 * P].rearrange("p o c -> p (o c)")
                        far = keep["far"][:, bass.ds(h, 1)]
                        for m in range(2):
                            neg, scores = negm[:, m:m + 1], near[:, m, 2 * P - w:2 * P]
                            dve.wait_ge(s_ready, h * (2 * NT) + (2 * i + m + 1))
                            link(v.tensor_tensor(scores, S[:, m, n0:n1], bias, ALU.add))
                            if not n0:
                                link(v.tensor_reduce(mx[:, 0, m:m + 1], scores, AX.X, ALU.max))
                                v.tensor_scalar(neg, mx[:, 0, m:m + 1], -1.0, None, ALU.mult).then_inc(mx_ready, 1)
                            else:
                                v.tensor_reduce(mx[:, 0, m:m + 1], scores, AX.X, ALU.max)
                                link(v.tensor_reduce(mx[:, 1, m:m + 1], S[:, m, 0:n0], AX.X, ALU.max))
                                link(v.scalar_tensor_tensor(mx[:, 0, m:m + 1], mx[:, 1, m:m + 1], far, mx[:, 0, m:m + 1], ALU.add, ALU.max))
                                link(v.tensor_scalar(neg, mx[:, 0, m:m + 1], -1.0, None, ALU.mult))
                                v.tensor_scalar(farb[:, m:m + 1], neg, far, None, ALU.add).then_inc(mx_ready, 1)

                    def combine(i):
                        n1 = (i + 1) * P
                        dve.wait_ge(e_ready, h * (2 * NT) + (2 * i + 4))
                        l = ls[:, :, 0]
                        if i > 1:
                            link(v.tensor_tensor(lt[:, :], ls[:, :, 0], ls[:, :, 1], ALU.add))
                            l = lt[:, :]
                        link(v.reciprocal(rl[:, :], l))
                        if i >= 2:
                            dve.wait_ge(t_ready, h * T_PER + (T_FIRST[i - 1] + 1))
                        else:
                            dve.wait_ge(t_ready, h * T_PER + 1)
                        v.tensor_scalar(c1[:, :], rl[:, 1:2], keep["lam"][:, 1:2], None, ALU.mult)
                        link(v.tensor_scalar(A[i % 2][:, 0:n1], E[:, 0, 0:n1], rl[:, 0:1], None, ALU.mult))
                        v.scalar_tensor_tensor(A[i % 2][:, 0:n1], E[:, 1, 0:n1], c1[:, 0:1], A[i % 2][:, 0:n1], ALU.mult, ALU.add).then_inc(a_ready, 1)

                    def consume(u):
                        bank = rec[u % 2]
                        if u in (L_USE[0], L_USE[0] + 1):
                            dve.wait_ge(rec_ready[u % 2], ready(h, u))
                            if u == L_USE[0]:
                                dve.wait_ge(rec_ready[(O_USE + 1) % 2], ready_before(h, O_USE + 1))
                            gate()
                            t = 4 * (u - L_USE[0])
                            v.copy_predicated(AT[:, t:t + 4, :], keep["lmask"][:, 0:P].rearrange("p (o c) -> p o c", o=1).broadcast_to([P, 4, P]),
                                              bank[:, :].rearrange("p (t c) -> p t c", t=4)).then_inc(rec_free[u % 2], 1)
                        for l in range(1, LEVELS):
                            if u == L_USE[l]:
                                dve.wait_ge(rec_ready[u % 2], ready(h, u))
                                dve.wait_ge(rec_free[(u - 1) % 2], freed(h, u - 1))
                                gate()
                                n, w = P // 2 ** l, 2 ** l // 2
                                mask = keep["lmask"][:, P + (l - 1) * HP:P + l * HP].rearrange("p (o n w) -> p o n w", o=1, w=w).broadcast_to([P, NT, n, w])
                                v.copy_predicated(AT[:, :, :].rearrange("p t (n s w) -> p t n s w", s=2, w=w)[:, :, :, 1, :], mask,
                                                  bank[:, :].rearrange("p (t n w) -> p t n w", t=NT, w=w)).then_inc(rec_free[u % 2], 1)
                        if u == SG_USE:
                            dve.wait_ge(rec_ready[u % 2], ready(h, u))
                            gate()
                            for l in range(SLEVELS):
                                last = v.copy_predicated(ATS[:, :], keep["slmask"][:, l, :], bank[0:NS, l * NS:(l + 1) * NS])
                                if l < SLEVELS - 1:
                                    link(last)
                                    gate()
                            last.then_inc(rec_free[u % 2], 1)
                        if U_USE <= u < U_USE + 2:
                            dve.wait_ge(rec_ready[u % 2], ready(h, u))
                            if u > U_USE:
                                dve.wait_ge(rec_free[(u - 1) % 2], freed(h, u - 1))
                                dve.wait_ge(st_stored, h * 16 + 16)
                            for j in range(4):
                                t = 4 * (u - U_USE) + j
                                last = v.scalar_tensor_tensor(ST[:, t + 1, :], ST[:, t, :], ends[par][:, t:t + 1], bank[:, j * P:(j + 1) * P], ALU.mult, ALU.add)
                                if j < 3:
                                    link(last)
                            last.then_inc(rec_free[u % 2], 1)
                        if SU_USE <= u < SU_USE + 2:
                            dve.wait_ge(rec_ready[u % 2], ready(h, u))
                            if u == SU_USE:
                                dve.wait_ge(states_in, 16 * h + 16)
                                dve.wait_ge(so_stored, h * 16 + 16)
                            for j in range(4):
                                s = 4 * (u - SU_USE) + j
                                last = v.scalar_tensor_tensor(SOUT[:, s, :], SIN[:, s, :], ends[par][:, NT + s:NT + s + 1], bank[:, j * P:(j + 1) * P], ALU.mult, ALU.add)
                            last.then_inc(rec_free[u % 2], 1)

                    for i in range(NT):
                        if i:
                            combine(i - 1)
                        maxima(i)
                        if i == KDM_SLOT:
                            dve.wait_ge(loaded[par], pair * LOADS + LOADS)
                            dve.wait_ge(rec_ready[(SU_USE + 1) % 2], ready_before(h, SU_USE + 1))
                            v.tensor_tensor(KDM[:, :, :], KDT[par][0:NS, NT:NT + 1, :].broadcast_to([NS, NB, P]),
                                            keep["rowmask"][:, :].rearrange("p (b o) -> p b o", o=1).broadcast_to([NS, NB, P]), ALU.mult).then_inc(kdm_ready, 1)
                        for u in REC_SLOT[i]:
                            consume(u)
                    combine(NT - 1)
                    for u in REC_SLOT[NT]:
                        consume(u)
                    assert count[0] == SMALL, (count, SMALL)

                each_head(dve, body)


def samples(nc, io, keep):
    with ExitStack() as ctx:
        sb, ps, sem = open_memory(nc, ctx)
        pt = sb("pt", [1, 2 * NB], I32)
        kp = [sb(f"kp{p}", [P, 2, FW]) for p in range(2)]
        vp = [sb(f"vp{p}", [P, 2, FW]) for p in range(2)]
        KT = [sb(f"KT{p}", [P, H, PAST]) for p in range(2)]
        KN = sb("KN", [P, H, NS])
        QS = sb("QS", [P, H, NS])
        QZ = sb("QZ", [P, NB, H, 32])
        VN = sb("VN", [NS, FW])
        sc = sb("sc", [P, 2, NK])
        smx = sb("smx", [P, 2])
        snm = sb("snm", [P, 2])
        ssum = sb("ssum", [P, 2])
        srl = sb("srl", [P, 2])
        sfac = sb("sfac", [P, 3])
        PT = sb("PT", [P, 2, 2, P])
        PTN = sb("PTN", [NS, 2, P])
        OS = sb("OS", [P, H, NB, TS])
        trs = [ps(f"trs{p}", [P, 512]) for p in range(2)]
        Sg = [ps(f"Sg{g}", [P, 512]) for g in range(2)]
        ptp = ps("ptp", [P, 512])
        opv = ps("opv", [P, 512])

        table_in = sem("table_in")
        news_in = sem("news_in")
        k_in = [sem(f"k_in{p}") for p in range(2)]
        v_in = [sem(f"v_in{p}") for p in range(2)]
        tr_ready = sem("str_ready")
        tr_free = [sem(f"str_free{p}") for p in range(2)]
        qz_ready = sem("qz_ready")
        sg_ready = sem("sg_ready")
        smx_ready = sem("smx_ready")
        sx_ready = sem("sx_ready")
        p_ready = sem("p_ready")
        pt_ready = sem("pt_ready")
        pt_free = sem("pt_free")
        pv_ready = sem("spv_ready")
        os_ready = sem("os_ready")
        os_stored = sem("os_stored")

        with nc.Block() as block:
            @block.sync
            def _(sp):
                sp.dma_start(pt[:, :], io["page_table"].rearrange("(o b) n -> o (b n)", o=1)).then_inc(table_in, 16)
                sp.dma_start(QS[:, :, :], io["q_d"].rearrange("h p t -> p h t")[:, :, T:TT]).then_inc(news_in, 16)
                sp.dma_start(KN[:, :, :], io["k_d"].rearrange("h p t -> p h t")[:, :, T:TT]).then_inc(news_in, 16)
                sp.dma_start(VN[:, :], io["v_sample"].rearrange("t h c -> t (h c)")).then_inc(news_in, 16)
                sp.wait_ge(table_in, 16)
                for s in range(NB):
                    if s >= 2:
                        sp.wait_ge(tr_ready, 2 * (s - 2) + 2)
                    for g in range(2):
                        page = sp.value_load(pt[0:1, 2 * s + g:2 * s + g + 1], min_val=0, max_val=io["cache_k"].shape[1] - 1)
                        sp.dma_start(kp[s % 2][:, g, :], io["cache_k"][0].rearrange("n p h m d -> n p (h m d)")[bass.ds(page, 1)].rearrange("o p c -> p (o c)"))\
                          .then_inc(k_in[s % 2], 16)
                for s in range(NB):
                    if s >= 2:
                        sp.wait_ge(pv_ready, s - 1)
                    for g in range(2):
                        page = sp.value_load(pt[0:1, 2 * s + g:2 * s + g + 1], min_val=0, max_val=io["cache_v"].shape[1] - 1)
                        sp.dma_start(vp[s % 2][:, g, :], io["cache_v"][0].rearrange("n p h c -> n p (h c)")[bass.ds(page, 1)].rearrange("o p c -> p (o c)"))\
                          .then_inc(v_in[s % 2], 16)
                sp.wait_ge(os_ready, 1)
                sp.dma_start(io["o_d"][0:H].rearrange("h p t -> p h t")[:, :, T:TT], OS[:, :, :, :].rearrange("p h b t -> p h (b t)")).then_inc(os_stored, 16)
                sp.wait_ge(os_stored, 16)

            @block.tensor
            def _(pe):
                mm = nc.tensor.matmul
                for s in range(NB):
                    pe.wait_ge(k_in[s % 2], 32 * (s // 2 + 1))
                    for g in range(2):
                        if s:
                            pe.wait_ge(tr_free[g], s)
                        for h in range(H):
                            last = nc.tensor.transpose(trs[g][:, h * P:(h + 1) * P], kp[s % 2][:, g, h * P:(h + 1) * P], keep["ident"][:, :])
                        last.then_inc(tr_ready, 1)
                    if s == 0:
                        pe.wait_ge(qz_ready, 1)
                        pe.wait_ge(news_in, 48)
                    for g in range(2):
                        pe.wait_ge(tr_free[g], s + 1)
                    rows = slice(32 * (s % 4), 32 * (s % 4) + 32)
                    for h in range(H):
                        mm(Sg[s // 4][rows, 0:PAST], QZ[:, s, h, :], KT[s % 2][:, h, :], start=(h == 0), stop=(h == H - 1), tile_position=(0, rows.start))
                    for h in range(H):
                        last = mm(Sg[s // 4][rows, PAST:NK], QZ[:, s, h, :], KN[:, h, :], start=(h == 0), stop=(h == H - 1), tile_position=(0, rows.start))
                    last.then_inc(sg_ready, 1)
                for g in range(2):
                    pe.wait_ge(p_ready, g + 1)
                    if g:
                        pe.wait_ge(pt_free, 1)
                    nc.tensor.transpose(ptp[:, 0:P], sc[:, g, 0:P], keep["ident"][:, :])
                    nc.tensor.transpose(ptp[:, P:2 * P], sc[:, g, P:2 * P], keep["ident"][:, :])
                    nc.tensor.transpose(ptp[0:NS, 2 * P:3 * P], sc[:, g, PAST:NK], keep["ident"][:, :]).then_inc(pt_ready, 1)
                for s in range(NB):
                    g = s // 4
                    if s % 4 == 0:
                        pe.wait_ge(pt_free, g + 1)
                    pe.wait_ge(v_in[s % 2], 32 * (s // 2 + 1))
                    for h in range(H):
                        cols = slice(32 * (s % 4) + 8 * h, 32 * (s % 4) + 8 * h + 8)
                        out = opv[:, 32 * s + 8 * h:32 * s + 8 * h + 8]
                        for j in range(2):
                            mm(out, vp[s % 2][:, j, h * P:(h + 1) * P], PT[:, g, j, cols], start=(j == 0), stop=False)
                        last = mm(out, VN[:, h * P:(h + 1) * P], PTN[:, g, cols], start=False, stop=True)
                    last.then_inc(pv_ready, 1)

            @block.scalar
            def _(act):
                a = nc.scalar.activation
                for s in range(NB):
                    act.wait_ge(tr_ready, 2 * s + 2)
                    if s >= 2:
                        act.wait_ge(sg_ready, s - 1)
                    a(KT[s % 2][:, :, P:2 * P], trs[1][:, :].rearrange("p (h c) -> p h c", h=H), ACT.Copy).then_inc(tr_free[1], 1)
                for g in range(2):
                    act.wait_ge(smx_ready, g + 1)
                    a(sc[:, g, :], sc[:, g, :], ACT.Exp, bias=snm[:, g:g + 1], accum_out=ssum[:, g:g + 1]).then_inc(sx_ready, 1)

            @block.vector
            def _(dve):
                v = nc.vector
                link = keep["dve_chain"].of(dve)
                link(v.memset(QZ[:, :, :, :], 0.0))
                dve.wait_ge(news_in, 48)
                for h in range(H):
                    for m in range(2):
                        rows, col = slice(m * HD, (m + 1) * HD), 8 * h + 4 * m
                        last = v.tensor_copy(QZ[rows, :, h, col:col + TS], QS[rows, h, :].rearrange("p (b t) -> p b t", t=TS))
                last.then_inc(qz_ready, 1)

                def keys(s):
                    dve.wait_ge(tr_ready, 2 * s + 1)
                    if s >= 2:
                        dve.wait_ge(sg_ready, s - 1)
                    v.tensor_copy(KT[s % 2][:, :, 0:P], trs[0][:, :].rearrange("p (h c) -> p h c", h=H)).then_inc(tr_free[0], 1)

                link(v.tensor_scalar(sfac[:, 0:1], keep["rowsel"][:, 1:2], keep["lam"][:, 1:2], None, ALU.mult))
                link(v.tensor_tensor(sfac[:, 0:1], sfac[:, 0:1], keep["rowsel"][:, 0:1], ALU.add))
                for s in range(NB):
                    keys(s)
                for g in range(2):
                    dve.wait_ge(sg_ready, 4 * g + 4)
                    link(v.tensor_tensor(sc[:, g, :], Sg[g][:, 0:NK], keep["sbias"][:, g, :], ALU.add))
                    link(v.tensor_reduce(smx[:, g:g + 1], sc[:, g, :], AX.X, ALU.max))
                    v.tensor_scalar(snm[:, g:g + 1], smx[:, g:g + 1], -1.0, None, ALU.mult).then_inc(smx_ready, 1)
                for g in range(2):
                    dve.wait_ge(sx_ready, g + 1)
                    link(v.reciprocal(srl[:, g:g + 1], ssum[:, g:g + 1]))
                    link(v.tensor_tensor(sfac[:, 1 + g:2 + g], srl[:, g:g + 1], sfac[:, 0:1], ALU.mult))
                    v.tensor_scalar(sc[:, g, :], sc[:, g, :], sfac[:, 1 + g:2 + g], None, ALU.mult).then_inc(p_ready, 1)
                for g in range(2):
                    dve.wait_ge(pt_ready, g + 1)
                    v.tensor_copy(PT[:, g, :, :], ptp[:, 0:2 * P].rearrange("p (j c) -> p j c", j=2))
                    v.tensor_copy(PTN[:, g, :], ptp[0:NS, 2 * P:3 * P]).then_inc(pt_free, 1)
                dve.wait_ge(pv_ready, NB)
                both = opv[:, 0:32 * NB].rearrange("p (b h m t) -> p h b m t", b=NB, h=H, m=2)
                link(v.tensor_copy(OS[:, :, :, :], both[:, :, :, 0, :]))
                for h in range(H):
                    last = v.tensor_tensor(OS[:, h, :, :], OS[:, h, :, :], both[:, h, :, 1, :], ALU.add)
                last.then_inc(os_ready, 1)


def mix(nc, io, keep, acc):
    with ExitStack() as ctx:
        sb, ps, sem = open_memory(nc, ctx)
        hh = sb("m_hi", [P, 2 * H, TT], F32R)
        hl = sb("m_lo", [P, 2 * H, TT], F32R)
        O = sb("O", [P, 2 * H, TT])
        rb = sb("m_rb", [P, H, TT])
        sq = sb("m_sq", [P, 2, TT])
        rg = sb("m_rg", [P, 1, TT])
        raw = sb("m_raw", [P, KC, P])
        whi = [sb(f"m_whi{s}", [P, KC, P], F32R) for s in range(2)]
        wlo = [sb(f"m_wlo{s}", [P, KC, P], F32R) for s in range(2)]
        zp = [ps(f"m_ps{n}", [P, 512]) for n in range(NPC)]
        ms = [ps(f"m_ms{n}", [P, 512]) for n in range(NPC)]

        x_back = sem("x_back")
        o_in = [sem(f"o_in{j}") for j in range(H)]
        rg_in = sem("rg_in")
        raw_in = sem("m_raw_in")
        w_ready = sem("m_w_ready")
        sq_ready = sem("m_sq_ready")
        ms_ready = sem("m_ms_ready")
        ln_ready = sem("m_ln_ready")
        rb_ready = sem("m_rb_ready")
        on_ready = sem("on_ready")
        hi_ready = sem("m_hi_ready")
        lo_ready = sem("m_lo_ready")
        z_ready = sem("m_z_ready")
        z_free = sem("m_z_free")
        w_view = io["w_out"][0].rearrange("(k p) (d c) -> d p k c", p=P, c=P)

        with nc.Block() as block:
            @block.sync
            def _(sp):
                for s, n in ((w_ready, 2), (z_ready, 2 * NPC), (z_free, NPC)):
                    sp.sem_inc(s, n)
                for j in range(H):
                    sp.dma_start(O[:, 2 * j:2 * j + 2, :], io["o_d"][2 * j:2 * j + 2].rearrange("h p t -> p h t")).then_inc(o_in[j], 16)
                sp.dma_start(acc[:, :, :], io["x_d"]).then_inc(x_back, 16)
                with sp.Fori(0, KC) as d:
                    sp.wait_ge(w_ready, d + 2)
                    sp.dma_start(raw[:, :, :], w_view[bass.ds(d, 1)].rearrange("o p k c -> p (o k) c")).then_inc(raw_in, 16)

            @block.gpsimd
            def _(pool):
                link = keep["pool_chain"].of(pool)
                with link.loop(KC // 2, 2) as pair:
                    for s in range(2):
                        pool.wait_ge(raw_in, pair * 32 + 16 * (s + 1))
                        pool.wait_ge(z_ready, pair * (2 * NPC) + NPC * (s + 1))
                        split_weights(nc, keep["ones"][:, :], raw[:, :, :], whi[s][:, :, :], wlo[s][:, :, :], link).then_inc(w_ready, 1)

            @block.tensor
            def _(pe):
                for j in range(2 * H):
                    pe.wait_ge(sq_ready, j + 1)
                    for n in range(NPC):
                        if j:
                            pe.wait_ge(ln_ready, NPC * (j - 1) + n + 1)
                        nc.tensor.matmul(ms[n][:, 0:PW], keep["ones"][:, :], sq[:, j % 2, piece(n)], start=True, stop=True).then_inc(ms_ready, 1)
                pe.wait_ge(lo_ready, 2 * H)
                with pe.Fori(0, KC // 2) as pair:
                    for s in range(2):
                        pe.wait_ge(w_ready, pair * 2 + (s + 3))
                        for n in range(NPC):
                            pe.wait_ge(z_free, pair * (2 * NPC) + (NPC * s + n + 1))
                            split_product(nc, zp[n][:, 0:PW], whi[s], wlo[s], hh[:, :, piece(n)], hl[:, :, piece(n)]).then_inc(z_ready, 1)

            @block.scalar
            def _(act):
                a = nc.scalar.activation
                for g in range(2):
                    for i in range(H):
                        j = g * H + i
                        act.wait_ge(o_in[j // 2], 16)
                        if j >= 2:
                            act.wait_ge(ms_ready, NPC * (j - 1))
                        a(sq[:, j % 2, :], O[:, j, :], ACT.Square).then_inc(sq_ready, 1)
                        if g and i == 0:
                            act.wait_ge(on_ready, H)
                        for n in range(NPC):
                            act.wait_ge(ms_ready, NPC * j + n + 1)
                            a(rb[:, i, piece(n)], ms[n][:, 0:PW], ACT.Ln, bias=keep["eps"][:, 0:1], scale=1.0 / P).then_inc(ln_ready, 1)
                    for i in range(H):
                        act.wait_ge(ln_ready, NPC * (g * H + H))
                        a(rb[:, i, :], rb[:, i, :], ACT.Exp, scale=-0.5).then_inc(rb_ready, 1)
                    for i in range(H):
                        j = g * H + i
                        if g:
                            if i:
                                act.wait_ge(on_ready, j)
                            act.dma_start(rg[:, 0, :], io["rg_d"][i]).then_inc(rg_in, 16)
                        act.wait_ge(on_ready, j + 1)
                        a(hh[:, j, :], O[:, j, :], ACT.Copy).then_inc(hi_ready, 1)

            @block.vector
            def _(dve):
                v = nc.vector
                link = keep["dve_chain"].of(dve)
                for j in range(2 * H):
                    gain = vector(keep, "subln_g" if j < H else "hgrn_onorm_g")
                    dve.wait_ge(rb_ready, j + 1)
                    ins = v.scalar_tensor_tensor(O[:, j, :], O[:, j, :], gain, rb[:, j % H, :], ALU.mult, ALU.mult)
                    if j >= H:
                        link(ins)
                        dve.wait_ge(rg_in, 16 * (j - H + 1))
                        ins = v.tensor_tensor(O[:, j, :], O[:, j, :], rg[:, 0, :], ALU.mult)
                    ins.then_inc(on_ready, 1)
                    if j:
                        dve.wait_ge(hi_ready, j)
                        v.tensor_tensor(hl[:, j - 1, :], O[:, j - 1, :], hh[:, j - 1, :].bitcast(F32), ALU.subtract).then_inc(lo_ready, 1)
                dve.wait_ge(hi_ready, 2 * H)
                v.tensor_tensor(hl[:, 2 * H - 1, :], O[:, 2 * H - 1, :], hh[:, 2 * H - 1, :].bitcast(F32), ALU.subtract).then_inc(lo_ready, 1)
                dve.wait_ge(x_back, 16)
                with dve.Fori(0, KC) as d:
                    for n in range(NPC):
                        dve.wait_ge(z_ready, d * NPC + (2 * NPC + n + 1))
                        row = acc[:, bass.ds(d, 1), piece(n)].rearrange("p o t -> p (o t)")
                        v.tensor_tensor(row, row, zp[n][:, 0:PW], ALU.add).then_inc(z_free, 1)


G2 = 2
GROUPS = FC // G2
DN_FIRST, DN_PER = 2, 2 + KC * NPC // 2


def mlp(nc, io, keep, acc):
    with ExitStack() as ctx:
        sb, ps, sem = open_memory(nc, ctx)
        hh = sb("f_hi", [P, KC, TT], F32R)
        hl = sb("f_lo", [P, KC, TT], F32R)
        raw = sb("f_raw", [P, 3, KC, P])
        names = ("g0", "u0", "g1", "u1", "d0", "d1")
        whi = {n: sb(f"f_whi_{n}", [P, KC, P], F32R) for n in names}
        wlo = {n: sb(f"f_wlo_{n}", [P, KC, P], F32R) for n in names}
        ahi = [sb(f"f_ahi{c}", [P, TT], F32R) for c in range(G2)]
        alo = [sb(f"f_alo{c}", [P, TT], F32R) for c in range(G2)]
        cp = sb("f_cp", [P, 2, TT])
        conv, prod = cp[:, 0, :], cp[:, 1, :]
        gate = sb("f_gate", [P, TT + 2])
        gsm = sb("f_gsm", [P, NB, TS + 2])
        rb = sb("f_rb", [P, TT])
        lnb = sb("f_lnb", [P, PW])
        scr = sb("f_scr", [P, P])
        g18 = sb("f_g18", [P, 2 + 2 * NB])
        cout = sb("f_cout", [2 + 2 * NB, P])
        gp = [ps(f"f_gp{n}", [P, 512]) for n in range(NPC)]
        up = [ps(f"f_up{n}", [P, 512]) for n in range(NPC)]
        dn = [ps(f"f_dn{n}", [P, 512]) for n in range(2)]

        sq_ready, sq_used, ms_ready, rb_ready = sem("f_sq_ready"), sem("f_sq_used"), sem("f_ms_ready"), sem("f_rb_ready")
        hf_ready, hi_ready, lo_ready = sem("f_hf_ready"), sem("f_hi_ready"), sem("f_lo_ready")
        raw_in = [sem(f"f_raw_in{s}") for s in range(3)]
        w_ready = sem("f_w_ready")
        scr_clear, scr_in = sem("scr_clear"), sem("scr_in")
        g_ready, g_free = sem("g_ready"), sem("g_free")
        gs_ready = sem("gs_ready")
        u_ready, u_free = sem("u_ready"), sem("u_free")
        c_ready, s_ready = sem("c_ready"), sem("f_s_ready")
        g18_ready = sem("g18_ready")
        dn_ready = [sem(f"dn_ready{b}") for b in range(2)]
        dn_free = [sem(f"dn_free{b}") for b in range(2)]
        ah_ready, al_ready = sem("ah_ready"), sem("al_ready")
        conv_stored = sem("conv_stored")
        y_ready = [sem(f"y_ready{b}") for b in range(2)]
        y_free = [sem(f"y_free{b}") for b in range(2)]
        y_stored = [sem(f"y_stored{p}") for p in range(2)]

        g_view = io["w_gate"][0].rearrange("(k p) (c f) -> c p k f", p=P, f=P)
        u_view = io["w_up"][0].rearrange("(k p) (c f) -> c p k f", p=P, f=P)
        d_view = io["w_down"][0].rearrange("(c p) (k f) -> c p k f", p=P, f=P)
        s_view = io["state_conv"][0].rearrange("b j (c f) -> c (b j) f", f=P)
        cp_view = io["conv_prompt"].rearrange("j (c f) -> c j f", f=P)
        cs_view = io["conv_sample"].rearrange("b j (c f) -> c (b j) f", f=P)
        W0 = 6

        def part(view, i):
            return view[bass.ds(i, 1)].rearrange("o p k f -> p (o k) f")

        def rows(view, i):
            return view[bass.ds(i, 1)].rearrange("o r f -> r (o f)")

        def dn_use(g, first, k):
            return k + 1 if first else g * DN_PER + (DN_FIRST - DN_PER + k + 1)

        with nc.Block() as block:
            @block.sync
            def _(sp):
                for s, n in ((w_ready, W0), (dn_free[0], 1), (dn_free[1], 1), (g_free, NPC), (u_free, NPC), (g_ready, 2 * NPC),
                             (u_ready, 2 * NPC), (conv_stored, 32), (al_ready, 2), (c_ready, 1), (s_ready, 1), (gs_ready, 1), (g18_ready, 1)):
                    sp.sem_inc(s, n)
                sp.wait_ge(scr_clear, 1)
                with sp.Fori(0, GROUPS) as g:
                    for k, (n, view) in enumerate(zip(names, (g_view, u_view, g_view, u_view, d_view, d_view))):
                        c = g * G2 + (k // 2 if k < 4 else k - 4)
                        sp.wait_ge(w_ready, g * 6 + (k + W0 - 2))
                        sp.dma_start(raw[:, k % 3, :, :], part(view, c)).then_inc(raw_in[k % 3], 16)
                        if k in (0, 2):
                            sp.wait_ge(gs_ready, g * 2 + (k // 2 + 1))
                            sp.dma_start(scr[0:2 * NB, :], rows(s_view, c)).then_inc(scr_in, 16)

            @block.gpsimd
            def _(pool):
                link = keep["pool_chain"].of(pool)
                nc.gpsimd.memset(scr[:, :], 0.0).then_inc(scr_clear, 1)
                with link.loop(GROUPS, 6) as g:
                    for k, n in enumerate(names):
                        pool.wait_ge(raw_in[k % 3], g * 32 + 16 * (k // 3 + 1))
                        if n[0] == "g":
                            pool.wait_ge(g_ready, g * (2 * NPC) + NPC * (k // 2 + 1))
                        elif n[0] == "u":
                            pool.wait_ge(u_ready, g * (2 * NPC) + NPC * (k // 2 + 1))
                        elif n == "d0":
                            pool.wait_ge(g_ready, g * (2 * NPC) + (2 * NPC + NPC + 1))
                        split_weights(nc, keep["ones"][:, :], raw[:, k % 3, :, :], whi[n][:, :, :], wlo[n][:, :, :], link).then_inc(w_ready, 1)

            @block.tensor
            def _(pe):
                norm_sums(nc, pe, keep["ones"], cp, gp, sq_ready, sq_used, ms_ready)

                def group(g, first):
                    def branch(c, b):
                        banks, ready, free = ((gp, g_ready, g_free), (up, u_ready, u_free))[b]
                        n = names[2 * c + b]
                        pe.wait_ge(w_ready, g * 6 + (2 * c + b + 1 + W0))
                        for i in range(NPC):
                            if first and c == 0 and b == 0:
                                pe.wait_ge(lo_ready, KC * (i + 1))
                            pe.wait_ge(free, g * (2 * NPC) + (NPC * c + i + 1))
                            split_product(nc, banks[i][:, 0:PW], whi[n], wlo[n], hh[:, :, piece(i)], hl[:, :, piece(i)]).then_inc(ready, 1)

                    def old_gates(c):
                        k = 0 if c == 0 else (1 if first else 1 + KC * NPC // 2)
                        pe.wait_ge(scr_in, g * 32 + 16 * (c + 1))
                        pe.wait_ge(dn_free[0], dn_use(g, first, k))
                        nc.tensor.transpose(dn[0][:, 0:P], scr[:, :], keep["ident"][:, :]).then_inc(dn_ready[0], 1)

                    def last_gates(c):
                        k = 0 if c == 0 else (1 if first else 1 + KC * NPC // 2)
                        pe.wait_ge(g18_ready, g * 2 + (c + 2))
                        pe.wait_ge(dn_free[1], dn_use(g, first, k))
                        nc.tensor.transpose(dn[1][0:2 + 2 * NB, 0:P], g18[:, :], keep["ident"][:, :]).then_inc(dn_ready[1], 1)

                    old_gates(0)
                    branch(0, 0)
                    branch(0, 1)
                    last_gates(0)
                    if not first:
                        down(g)
                    old_gates(1)
                    branch(1, 0)
                    branch(1, 1)
                    last_gates(1)

                def down(g, extra=1):
                    pe.wait_ge(w_ready, g * 6 + W0)
                    pe.wait_ge(al_ready, g * 2 + 2)
                    for j in range(KC * NPC):
                        d, n = divmod(j, NPC)
                        b = j % 2
                        pe.wait_ge(dn_free[b], dn_use(g, False, extra + j // 2))
                        out = dn[b][:, 0:PW]
                        for c in range(G2):
                            w = f"d{c}"
                            nc.tensor.matmul(out, whi[w][:, d, :], ahi[c][:, piece(n)], start=(c == 0), stop=False)
                            nc.tensor.matmul(out, whi[w][:, d, :], alo[c][:, piece(n)], start=False, stop=False)
                            last = nc.tensor.matmul(out, wlo[w][:, d, :], ahi[c][:, piece(n)], start=False, stop=(c == G2 - 1))
                        last.then_inc(dn_ready[b], 1)

                group(0, True)
                with pe.Fori(1, GROUPS) as g:
                    group(g, False)
                down(GROUPS, extra=0)
                for b in range(2):
                    pe.wait_ge(dn_free[b], dn_use(GROUPS, False, KC * NPC // 2))
                for t in range(NT + 1):
                    w = P if t < NT else NS
                    for b in range(2):
                        if t:
                            pe.wait_ge(y_free[b], t)
                        for j in range(4):
                            last = nc.tensor.transpose(gp[b][0:w, j * P:(j + 1) * P], acc[:, 4 * b + j, t * P:t * P + w], keep["ident"][:, :])
                        last.then_inc(y_ready[b], 1)

            @block.scalar
            def _(act):
                a = nc.scalar.activation
                link = keep["act_chain"].of(act)
                norm_squares(nc, act, acc, cp, sq_ready, sq_used)
                norm_inverse(nc, act, keep["eps"], gp, rb, lnb, ms_ready, rb_ready, link)
                norm_high(nc, act, gate[:, 0:TT].rearrange("p (s w) -> p s w", s=NPC), hh, hf_ready, hi_ready)

                def group(g, first):
                    def old_gates(c):
                        k = 0 if c == 0 else (1 if first else 1 + KC * NPC // 2)
                        act.wait_ge(c_ready, g * 2 + (c + 1))
                        act.wait_ge(g18_ready, g * 2 + (c + 1))
                        act.wait_ge(dn_ready[0], dn_use(g, first, k))
                        a(gsm[:, :, 0:2], dn[0][:, 0:2 * NB].rearrange("p (b j) -> p b j", j=2), ACT.Copy).then_inc(dn_free[0], 1)

                    def gates(c):
                        for i in range(NPC):
                            act.wait_ge(g_ready, g * (2 * NPC) + (2 * NPC + NPC * c + i + 1))
                            if first and c == 0 and i == 0:
                                act.wait_ge(lo_ready, KC * NPC)
                            lo, hi = i * PW, min((i + 1) * PW, T)
                            if i == NPC - 1:
                                a(gsm[:, :, 2:2 + TS], gp[i][:, hi - lo:PW].rearrange("p (b t) -> p b t", t=TS), ACT.Copy).then_inc(gs_ready, 1)
                            a(gate[:, 2 + lo:2 + hi], gp[i][:, 0:hi - lo], ACT.Copy).then_inc(g_free, 1)

                    def last_gates(c):
                        k = 0 if c == 0 else (1 if first else 1 + KC * NPC // 2)
                        act.wait_ge(dn_ready[1], dn_use(g, first, k))
                        act.wait_ge(conv_stored, g * 64 + 32 * (c + 1))
                        a(cout[:, :], dn[1][0:2 + 2 * NB, 0:P], ACT.Copy).then_inc(dn_free[1], 1)
                        act.wait_ge(dn_free[1], dn_use(g, first, k) + 1)
                        i = g * G2 + c
                        act.dma_start(rows(cp_view, i), cout[0:2, :]).then_inc(conv_stored, 16)
                        act.dma_start(rows(cs_view, i), cout[2:2 + 2 * NB, :]).then_inc(conv_stored, 16)

                    def silu(c):
                        act.wait_ge(c_ready, g * 2 + (c + 2))
                        a(conv, conv, ACT.Silu).then_inc(s_ready, 1)

                    def high(c):
                        act.wait_ge(u_free, g * (2 * NPC) + (NPC * c + 2 * NPC))
                        if c == 0 and not first:
                            act.wait_ge(g_ready, g * (2 * NPC) + (2 * NPC + NPC + 1))
                        a(ahi[c][:, :], prod, ACT.Copy).then_inc(ah_ready, 1)

                    old_gates(0), gates(0), silu(0), last_gates(0)
                    if first:
                        high(0), old_gates(1), gates(1)
                    else:
                        old_gates(1), high(0), gates(1)
                    silu(1), last_gates(1), high(1)

                group(0, True)
                with act.Fori(1, GROUPS) as g:
                    group(g, False)
                for t in range(NT + 1):
                    w = P if t < NT else NS
                    act.wait_ge(y_ready[1], t + 1)
                    if t == 0:
                        act.wait_ge(al_ready, 2 * GROUPS + 2)
                    if t >= 2:
                        act.wait_ge(y_stored[t % 2], 16 * (t // 2))
                    a(cp[0:w, t % 2, 4 * P:8 * P], gp[1][0:w, :], ACT.Copy).then_inc(y_free[1], 1)
                    act.wait_ge(y_free[0], t + 1)
                    act.wait_ge(y_free[1], t + 1)
                    dst = io["y_prompt"][0, t * P:(t + 1) * P, :] if t < NT else io["y_sample"].rearrange("b t d -> (b t) d")
                    act.dma_start(dst, cp[0:w, t % 2, 0:D]).then_inc(y_stored[t % 2], 16)
                act.wait_ge(y_stored[0], 16 * 5)
                act.wait_ge(y_stored[1], 16 * 4)
                act.wait_ge(conv_stored, 32 * (FC + 1))

            @block.vector
            def _(dve):
                v = nc.vector
                norm_low(nc, dve, acc, vector(keep, "norm2_g"), rb, gate[:, 0:TT].rearrange("p (s w) -> p s w", s=NPC), hh, hl, rb_ready, hf_ready, hi_ready, lo_ready)
                link = keep["dve_chain"].of(dve)
                dve.wait_ge(lo_ready, KC * NPC)
                link(v.memset(gate[:, 0:2], 0.0))
                PER = 8

                def group(g, first, link):
                    def w(j, c):
                        return keep["vec"][:, bass.ds(g * G2 + (VECTORS["conv_w"][0] + j * FC + c), 1)]

                    def convolve(c):
                        bias = keep["vec"][:, bass.ds(g * G2 + (VECTORS["conv_b"][0] + c), 1)]
                        dve.wait_ge(g_free, g * (2 * NPC) + (NPC + NPC * c + NPC))
                        dve.wait_ge(dn_free[1], dn_use(g, first, 0 if c == 0 else (1 if first else 1 + KC * NPC // 2)))
                        v.tensor_copy(g18[:, 0:2], gate[:, T:T + 2])
                        v.tensor_copy(g18[:, 2:2 + 2 * NB].rearrange("p (b j) -> p b j", j=2), gsm[:, :, TS:TS + 2]).then_inc(g18_ready, 1)
                        old = conv[:, T:TT].rearrange("p (b t) -> p b t", t=TS)
                        dve.wait_ge(ah_ready, g * 2 + c) if not (first and c == 0) else None
                        v.tensor_scalar(conv[:, 0:T], gate[:, 2:T + 2], w(2, c), bias, ALU.mult, ALU.add)
                        link(v.tensor_scalar(old, gsm[:, :, 2:2 + TS], w(2, c), bias, ALU.mult, ALU.add))
                        v.scalar_tensor_tensor(conv[:, 0:T], gate[:, 1:T + 1], w(1, c), conv[:, 0:T], ALU.mult, ALU.add)
                        link(v.scalar_tensor_tensor(old, gsm[:, :, 1:1 + TS], w(1, c), old, ALU.mult, ALU.add))
                        v.scalar_tensor_tensor(conv[:, 0:T], gate[:, 0:T], w(0, c), conv[:, 0:T], ALU.mult, ALU.add)
                        v.scalar_tensor_tensor(old, gsm[:, :, 0:TS], w(0, c), old, ALU.mult, ALU.add).then_inc(c_ready, 1)

                    def multiply(c):
                        dve.wait_ge(s_ready, g * 2 + (c + 2))
                        dve.wait_ge(al_ready, g * 2 + (c + 2))
                        for i in range(NPC):
                            dve.wait_ge(u_ready, g * (2 * NPC) + (2 * NPC + NPC * c + i + 1))
                            v.tensor_tensor(prod[:, piece(i)], conv[:, piece(i)], up[i][:, 0:PW], ALU.mult).then_inc(u_free, 1)

                    def low(c):
                        dve.wait_ge(ah_ready, g * 2 + (c + 1))
                        v.tensor_tensor(alo[c][:, :], prod, ahi[c][:, :].bitcast(F32), ALU.subtract).then_inc(al_ready, 1)

                    convolve(0), multiply(0)
                    if not first:
                        down(g)
                    low(0), convolve(1), multiply(1), low(1)

                def down(g, extra=1):
                    for j in range(KC * NPC):
                        d, n = divmod(j, NPC)
                        b = j % 2
                        dve.wait_ge(dn_ready[b], dn_use(g, False, extra + j // 2))
                        v.tensor_tensor(acc[:, d, piece(n)], acc[:, d, piece(n)], dn[b][:, 0:PW], ALU.add).then_inc(dn_free[b], 1)

                group(0, True, link)
                with link.loop(GROUPS - 1, 4) as g1:
                    group(g1 + 1, False, link)
                down(GROUPS, extra=0)
                for t in range(NT + 1):
                    w = P if t < NT else NS
                    dve.wait_ge(y_ready[0], t + 1)
                    if t >= 2:
                        dve.wait_ge(y_stored[t % 2], 16 * (t // 2))
                    v.tensor_copy(cp[0:w, t % 2, 0:4 * P], gp[0][0:w, :]).then_inc(y_free[0], 1)


def rel_bucket(n):
    n = np.maximum(n, 0)
    exact = N_BUCKETS // 2
    nf = np.maximum(n, 1).astype(np.float32)
    large = exact + (np.log(nf / np.float32(exact)) / np.float32(math.log(MAX_DISTANCE / exact)) * np.float32(N_BUCKETS - exact)).astype(np.int32)
    return np.where(n < exact, n, np.minimum(large, N_BUCKETS - 1))


def one_hot(distance):
    out = np.zeros((N_BUCKETS + 1,) + distance.shape, np.float32)
    b = np.where(distance < 0, N_BUCKETS, rel_bucket(distance))
    for i in range(N_BUCKETS + 1):
        out[i] = b == i
    return out


def constants():
    c = {}
    c["c_ident"] = np.eye(P, dtype=np.float32)
    half = np.arange(P) // HD
    c["c_blk"] = (half[:, None] == half[None, :]).astype(np.float32)
    c["c_dist"] = one_hot(2 * P - 1 - np.arange(BW))
    q = np.arange(TS)[:, None]
    past = PAST + q - np.arange(PAST)[None, :]
    new = q - (np.arange(NS) % TS)[None, :]
    c["c_sdist"] = one_hot(np.concatenate([past, new], 1))
    row = np.arange(P) // 32
    m = np.zeros((P, 2, NK), np.float32)
    for g in range(2):
        other = (4 * g + row)[:, None] != (np.arange(NS) // TS)[None, :]
        m[:, g, PAST:] = np.where(other, np.float32(MASKED), 0)
    c["c_smask"] = m
    s, t = np.arange(P)[:, None], np.arange(P)[None, :]
    lm = np.zeros((P, LEVELS, P), np.int32)
    lm[:, 0] = s == t
    for l in range(1, LEVELS):
        w = 2 ** l
        lm[:, l] = (s // w == t // w) & (s % w < w // 2) & (t % w >= w // 2)
    c["c_slmask"] = np.ascontiguousarray(lm[0:NS, 0:SLEVELS, 0:NS])
    halves = [lm[:, l].reshape(P, P // 2 ** l, 2, 2 ** l // 2)[:, :, 1].reshape(P, P // 2) for l in range(1, LEVELS)]
    c["c_lmask"] = np.concatenate([lm[:, 0]] + halves, 1)
    c["c_rowmask"] = (np.arange(NS)[:, None] // TS == np.arange(NB)[None, :]).astype(np.float32)
    c["c_rowsel"] = (np.arange(P)[:, None] // TS % 2 == np.arange(2)[None, :]).astype(np.float32)
    return c


INPUTS = ["x_prompt", "x_sample", "cache_k", "cache_v", "page_table", "state_hgrn", "state_conv", "rel_bias",
          "norm1_g", "w_in", "qk_norm_g", "lambda_qk", "subln_g", "hgrn_lb", "hgrn_onorm_g", "w_out",
          "norm2_g", "w_gate", "w_up", "conv_w", "conv_b", "w_down"]
OUTPUTS = [("y_prompt", (1, T, D)), ("y_sample", (NB, TS, D)), ("k_prompt", (T, H, P)), ("v_prompt", (T, H, P)),
           ("hgrn_prompt", (H, P, P)), ("conv_prompt", (2, FF)), ("k_sample", (NS, H, P)), ("v_sample", (NS, H, P)),
           ("hgrn_sample", (NB, H, P, P)), ("conv_sample", (NB, 2, FF))]
SHAPES = [(1, T, D), (NB, TS, D), (1, 1, T, H, 2, HD), (1, 1, T, H, P), (1, 1, H, P, P), (1, 1, 2, FF),
          (1, NB, TS, H, 2, HD), (1, NB, TS, H, P), (1, NB, H, P, P), (1, NB, 2, FF)]
SCRATCH = [("skew", (H, P, BW)), ("x_d", (P, KC, TT)), ("q_d", (H, P, TT)), ("k_d", (H, P, TT)), ("rq_d", (H, P, TT)),
           ("kk_d", (H, P, TT)), ("b_d", (H, P, TT)), ("qd_d", (H, P, TT)), ("kd_d", (H, P, NT + 1, P)), ("ends_d", (H, P, NT + NB)),
           ("rg_d", (H, P, TT)), ("ri_d", (H, P, NT + 1, P)), ("o_d", (2 * H, P, TT))]


def program(nc, arrays, upto=9):
    io = {}
    for name, a in arrays.items():
        io[name] = nc.dram_tensor(name, a.shape, mybir.dt.from_np(a.dtype), kind="ExternalInput").ap()
    for name, shape in OUTPUTS:
        io[name] = nc.dram_tensor(name, shape, F32, kind="ExternalOutput").ap()
    for name, shape in SCRATCH:
        io[name] = nc.dram_tensor(name, shape, F32, kind="Internal").ap()
    with ExitStack() as ctx:
        sb, ps, sem = open_memory(nc, ctx)
        keep = {n: sb(n, shape, dt) for n, shape, dt in (
            ("ident", [P, P], F32), ("blk", [P, P], F32), ("ones", [P, P], F32), ("eps", [P, 1], F32),
            ("lmask", [P, P + (LEVELS - 1) * P // 2], I32), ("slmask", [NS, SLEVELS, NS], I32), ("rowmask", [NS, NB], F32), ("rowsel", [P, 2], F32), ("bias", [P, H, 2 * P], F32), ("far", [P, H], F32),
            ("sbias", [P, 2, NK], F32), ("lam", [P, 2], F32), ("lb0", [P, H], F32), ("lb1", [P, H], F32),
            ("vec", [P, NVEC], F32))}
        for name in ("dve", "act", "pool"):
            keep[f"{name}_chain"] = Chain(sem(f"{name}_done"))
        prepare(nc, io, keep)
        if upto >= 1:
            project(nc, io, keep)
        if upto >= 2:
            heads(nc, io, keep)
        if upto >= 3:
            samples(nc, io, keep)
        if upto >= 4:
            acc = sb("residual", [P, KC, TT])
            mix(nc, io, keep, acc)
            if upto >= 5:
                mlp(nc, io, keep, acc)


def kernel(**inputs):
    import concourse.bacc as bacc
    from concourse.bass_utils import run_bass_kernel_spmd

    nc = bacc.Bacc("TRN2", target_bir_lowering=False, num_devices=1)
    arrays = {n: np.ascontiguousarray(inputs[n]) for n in INPUTS}
    arrays.update(constants())
    program(nc, arrays)
    r = run_bass_kernel_spmd(nc, [arrays], core_ids=[0])
    return tuple(np.asarray(r.results[0][n]).reshape(s) for (n, _), s in zip(OUTPUTS, SHAPES))
```

```python
import math
from contextlib import ExitStack

import numpy as np
import concourse.bass as bass
from concourse import mybir

F32 = mybir.dt.float32
F32R = mybir.dt.float32r
I32 = mybir.dt.int32
ALU = mybir.AluOpType
ACT = mybir.ActivationFunctionType
AX = mybir.AxisListType

P = 128
D = 1024
KC = D // P
T = 1024
NB = 8
TS = 4
NS = NB * TS
TT = T + NS
NT = T // P
NPC = 3
PW = TT // NPC
H = 4
HD = 64
FW = H * P
PARTS = 7
FF = 2816
FC = FF // P
PAST = 256
EPS = 1e-6
MASKED = -1.0e30
LEVELS = 8
SLEVELS = 3
LAM_INIT = 0.8 - 0.6 * math.exp(0.0)
N_BUCKETS, MAX_DISTANCE = 32, 128
BW = 3 * P
NK = PAST + NS

W_SLOT = [0, 1, 0, 1, 0, 1, 2]
W_USES = [3, 3, 1]
W_NTH = [0, 0, 1, 1, 2, 2, 0]
W_BACK = [3, 3, 2, 2, 2, 2, 7]


VECTORS = {"norm1_g": (0, KC), "norm2_g": (8, KC), "conv_w": (16, 3 * FC), "conv_b": (82, FC), "qk_norm_g": (104, 2),
           "subln_g": (106, 1), "hgrn_onorm_g": (107, 1), "hgrn_lb": (108, 2 * H)}
NVEC = 116
TABLES = 14


def vector(keep, name):
    first, rows = VECTORS[name]
    return keep["vec"][:, first:first + rows]


def piece(n):
    return slice(n * PW, (n + 1) * PW)


class Chain:

    def __init__(self, sem):
        self.sem, self.n = sem, 0

    def of(self, eng):
        self.eng = eng
        return self

    def __call__(self, ins):
        ins.then_inc(self.sem, 1)
        self.n = self.n + 1
        self.eng.wait_ge(self.sem, self.n)

    def loop(self, count, per):
        return _ChainLoop(self, count, per)


class _ChainLoop:
    def __init__(self, chain, count, per):
        self.chain, self.count, self.per = chain, count, per

    def __enter__(self):
        self.start = self.chain.n
        self.fori = self.chain.eng.Fori(0, self.count)
        i = self.fori.__enter__()
        self.chain.n = 0
        self.base = i * self.per + self.start
        self.chain.n = self.base
        self.i = i
        return i

    def __exit__(self, *a):
        self.chain.n = self.start + self.count * self.per
        return self.fori.__exit__(*a)


def open_memory(nc, ctx, sems):
    def sb(name, shape, dt=F32):
        return ctx.enter_context(nc.sbuf_tensor(name, shape, dt))

    def ps(name, shape):
        return ctx.enter_context(nc.psum_tensor(name, shape, F32))

    def sem(name):
        sems.append(nc.alloc_semaphore(name))
        return sems[-1]

    return sb, ps, sem


def clear_last(nc, keep):
    if keep["last"]:
        nc.clear_and_free_semaphores(keep["last"])
    keep["last"], keep["sems"] = keep["sems"], []


def x_tile(io, t):
    return (io["x_prompt"][0, t * P:(t + 1) * P, :], P) if t < NT else (io["x_sample"].rearrange("b t d -> (b t) d"), NS)


def prepare(nc, io, keep, x):
    with ExitStack() as ctx:
        sb, ps, sem = open_memory(nc, ctx, keep["sems"])
        rel = sb("rel", [33, H])
        dist = sb("dist", [33, BW])
        sdist = sb("sdist", [33, TS, NK])
        relrow = sb("relrow", [33, H, P])
        selrow = sb("selrow", [33, TS, P])
        smask = sb("smask", [P, 2, NK])
        skew = sb("skew_rows", [P, H, BW])
        lq = sb("lq", [P, 4, HD])
        lprod = sb("lprod", [P, 2, HD])
        lsum = sb("lsum", [P, 2])
        lexp = sb("lexp", [P, 2])
        vrows = sb("vrows", [NVEC, P])
        lbm = sb("lbm", [P, H])
        lbe = sb("lbe", [P, 2, H])
        lbs = sb("lbs", [P, H])
        pb = ps("pb", [P, H, 512])
        psb = ps("psb", [P, 512])
        pvec = ps("pvec", [P, 512])
        lbr = keep["vec"][:, VECTORS["hgrn_lb"][0]:NVEC].rearrange("p (a h) -> p a h", a=2)
        gqk = vector(keep, "qk_norm_g")
        gsub = vector(keep, "subln_g")
        tables_in = sem("tables_in")
        rel_ready = sem("rel_ready")
        bias_ready = sem("bias_ready")
        skew_ready = sem("skew_ready")
        exp_ready = sem("exp_ready")
        exp_wanted = sem("exp_wanted")

        clear_last(nc, keep)
        with nc.Block() as block:
            @block.sync
            def _(sp):
                sp.dma_start(rel[0:32, :], io["rel_bias"]).then_inc(tables_in, 16)
                sp.dma_start(dist[:, :], io["c_dist"]).then_inc(tables_in, 16)
                sp.dma_start(sdist[:, :, :], io["c_sdist"]).then_inc(tables_in, 16)
                sp.dma_start(smask[:, :, :], io["c_smask"]).then_inc(tables_in, 16)
                sp.dma_start(lq[:, :, :], io["lambda_qk"].broadcast_to([P, 4, HD])).then_inc(tables_in, 16)
                sp.dma_start(keep["ident"][:, :], io["c_ident"]).then_inc(tables_in, 16)
                for name, view in (("norm1_g", "o (k p) -> (o k) p"), ("norm2_g", "o (k p) -> (o k) p"), ("conv_w", "o j (c p) -> (o j c) p"),
                                   ("conv_b", "o (c p) -> (o c) p"), ("qk_norm_g", "o a m d -> (o a) (m d)"), ("subln_g", "o p -> o p"),
                                   ("hgrn_onorm_g", "o p -> o p"), ("hgrn_lb", "a (h p) -> (a h) p")):
                    first, rows = VECTORS[name]
                    src = io[name] if view == "o p -> o p" else io[name].rearrange(view, **({"p": P} if "(k p)" in view or "(c p)" in view or "(h p)" in view else {}))
                    sp.dma_start(vrows[first:first + rows, :], src).then_inc(tables_in, 16)
                for t in range(NT + 1):
                    src, rows = x_tile(io, t)
                    sp.dma_start(x[t][0:rows, :], src).then_inc(keep["x_in"][t // 3], 16)
                sp.dma_start(keep["blk"][:, :], io["c_blk"]).then_inc(keep["late_in"], 16)
                sp.dma_start(keep["lmask"][:, :], io["c_lmask"]).then_inc(keep["late_in"], 16)
                sp.dma_start(keep["slmask"][:, :, :], io["c_slmask"]).then_inc(keep["late_in"], 16)
                sp.dma_start(keep["rowmask"][:, :], io["c_rowmask"]).then_inc(keep["late_in"], 16)
                sp.dma_start(keep["rowsel"][:, :], io["c_rowsel"]).then_inc(keep["late_in"], 16)
                sp.wait_ge(skew_ready, H)
                sp.dma_start(io["skew"].rearrange("h p w -> p h w"), skew[:, :, :]).then_inc(keep["skewed"], 16)
                sp.wait_ge(keep["skewed"], 16)

            @block.vector
            def _(dve):
                link = keep["dve_chain"].of(dve)
                v = nc.vector
                v.memset(keep["ones"][:, :], 1.0)
                v.memset(keep["eps"][:, :], EPS)
                v.memset(selrow[:, :, :], 0.0)
                link(v.memset(rel[32:33, :], MASKED))
                dve.wait_ge(tables_in, 16 * TABLES)
                v.tensor_copy(relrow[:, :, :], rel[:, :].rearrange("p (h o) -> p h o", o=1).broadcast_to([33, H, P])).then_inc(rel_ready, 1)
                for t in range(TS):
                    for b in range(4):
                        out = selrow[:, t, 32 * b:32 * b + 32].rearrange("p (h m t) -> p h m t", h=H, m=2)[:, :, :, t]
                        src = rel[:, :].rearrange("p (h o) -> p h o", o=1).broadcast_to([33, H, 2])
                        v.tensor_copy(out, src).then_inc(rel_ready, 1)
                dve.wait_ge(bias_ready, 1)
                link(v.tensor_copy(keep["vec"][:, :], pvec[:, 0:NVEC]))
                link(v.tensor_tensor(lprod[:, :, :], lq[:, 0:4:2, :], lq[:, 1:4:2, :], ALU.mult))
                v.tensor_reduce(lsum[:, :], lprod[:, :, :], AX.X, ALU.add).then_inc(exp_wanted, 1)
                link(v.tensor_tensor(lbm[:, :], lbr[:, 0, :], lbr[:, 1, :], ALU.max))
                for a in range(2):
                    last = v.tensor_tensor(lbr[:, a, :], lbr[:, a, :], lbm[:, :], ALU.subtract)
                last.then_inc(exp_wanted, 1)
                dve.wait_ge(exp_ready, 1)
                link(v.tensor_tensor(lsum[:, 0:1], lexp[:, 0:1], lexp[:, 1:2], ALU.subtract))
                link(v.tensor_scalar(keep["lam"][:, 0:1], lsum[:, 0:1], LAM_INIT, None, ALU.add))
                link(v.tensor_scalar(keep["lam"][:, 1:2], keep["lam"][:, 0:1], -1.0, None, ALU.mult))
                dve.wait_ge(exp_ready, 2)
                link(v.tensor_tensor(lbs[:, :], lbe[:, 0, :], lbe[:, 1, :], ALU.add))
                link(v.reciprocal(lbm[:, :], lbs[:, :]))
                link(v.tensor_tensor(keep["lb0"][:, :], lbe[:, 0, :], lbm[:, :], ALU.mult))
                link(v.tensor_scalar(keep["lb1"][:, :], keep["lb0"][:, :], -1.0, 1.0, ALU.mult, ALU.add))
                link(v.tensor_scalar(gqk[:, 0:1], gqk[:, 0:1], HD ** -0.5, None, ALU.mult))
                link(v.tensor_scalar(gsub, gsub, 1.0 - LAM_INIT, None, ALU.mult))
                for h in range(H):
                    dve.wait_ge(bias_ready, h + 2)
                    v.tensor_copy(skew[:, h, :], pb[:, h, 0:BW]).then_inc(skew_ready, 1)
                    link(v.tensor_copy(keep["far"][:, h:h + 1], pb[:, h, 0:1]))
                dve.wait_ge(bias_ready, H + 2)
                for g in range(2):
                    link(v.tensor_tensor(keep["sbias"][:, g, :], psb[:, 0:NK], smask[:, g, :], ALU.add))

            @block.scalar
            def _(act):
                act.wait_ge(exp_wanted, 1)
                nc.scalar.activation(lexp[:, :], lsum[:, :], ACT.Exp).then_inc(exp_ready, 1)
                act.wait_ge(exp_wanted, 2)
                nc.scalar.activation(lbe[:, :, :], lbr[:, :, :], ACT.Exp).then_inc(exp_ready, 1)

            @block.tensor
            def _(pe):
                pe.wait_ge(tables_in, 16 * TABLES)
                nc.tensor.transpose(pvec[:, 0:NVEC], vrows[:, :], keep["ident"][0:NVEC, 0:NVEC]).then_inc(bias_ready, 1)
                pe.wait_ge(rel_ready, 1)
                for h in range(H):
                    nc.tensor.matmul(pb[:, h, 0:BW], relrow[:, h, :], dist[:, :], start=True, stop=True).then_inc(bias_ready, 1)
                pe.wait_ge(rel_ready, 1 + 4 * TS)
                for t in range(TS):
                    last = nc.tensor.matmul(psb[:, 0:NK], selrow[:, t, :], sdist[:, t, :], start=(t == 0), stop=(t == TS - 1))
                last.then_inc(bias_ready, 1)


def split_weights(nc, ones, raw, hi, lo, link):
    link(nc.gpsimd.tensor_tensor(hi, raw, ones.rearrange("p (o c) -> p o c", o=1).broadcast_to(list(raw.shape)), ALU.mult))
    return nc.gpsimd.tensor_tensor(lo, raw, hi.bitcast(F32), ALU.subtract)


def split_product(nc, out, whi, wlo, hi, lo):
    chunks = hi.shape[1]
    for k in range(chunks):
        nc.tensor.matmul(out, whi[:, k, :], hi[:, k, :], start=(k == 0), stop=False)
        nc.tensor.matmul(out, whi[:, k, :], lo[:, k, :], start=False, stop=False)
        last = nc.tensor.matmul(out, wlo[:, k, :], hi[:, k, :], start=False, stop=(k == chunks - 1))
    return last



def norm_inverse(nc, act, eps, ms, rb, ms_ready, rb_ready, link):
    for n in range(NPC):
        act.wait_ge(ms_ready, n + 1)
        last = nc.scalar.activation(rb[:, piece(n)], ms[n][:, 0:PW], ACT.Ln, bias=eps[:, 0:1], scale=1.0 / D)
    link(last)
    for n in range(NPC):
        nc.scalar.activation(rb[:, piece(n)], rb[:, piece(n)], ACT.Exp, scale=-0.5).then_inc(rb_ready, 1)


def norm_high(nc, act, hf, hh, hf_ready, hi_ready):
    for n in range(NPC):
        for k in range(KC):
            j = n * KC + k
            act.wait_ge(hf_ready, j + 1)
            nc.scalar.activation(hh[:, k, piece(n)], hf[:, j % NPC, :], ACT.Copy).then_inc(hi_ready, 1)


def norm_low(nc, dve, src, gain, rb, hf, hh, hl, rb_ready, hf_ready, hi_ready, lo_ready):
    steps = [(n, k) for n in range(NPC) for k in range(KC)]

    def low(j):
        n, k = steps[j]
        dve.wait_ge(hi_ready, j + 1)
        nc.vector.tensor_tensor(hl[:, k, piece(n)], hf[:, j % NPC, :], hh[:, k, piece(n)].bitcast(F32), ALU.subtract).then_inc(lo_ready, 1)

    for j, (n, k) in enumerate(steps):
        if k == 0:
            dve.wait_ge(rb_ready, n + 1)
        if j >= NPC:
            dve.wait_ge(lo_ready, j - NPC + 1)
        nc.vector.scalar_tensor_tensor(hf[:, j % NPC, :], src[:, k, piece(n)], gain[:, k:k + 1], rb[:, piece(n)], ALU.mult, ALU.mult)\
          .then_inc(hf_ready, 1)
        if j:
            low(j - 1)
    low(len(steps) - 1)


def project(nc, io, keep, x, z_room, tm):
    with ExitStack() as ctx:
        sb, ps, sem = open_memory(nc, ctx, keep["sems"])
        xT = sb("xT", [P, KC, TT])
        hh = sb("h_hi", [P, KC, TT], F32R)
        hl = sb("h_lo", [P, KC, TT], F32R)
        raw = sb("w_raw", [P, 3, KC, P])
        whi = [sb(f"w_hi{s}", [P, KC, P], F32R) for s in range(3)]
        wlo = [sb(f"w_lo{s}", [P, KC, P], F32R) for s in range(3)]
        ZQ, ZK, ZV, ZRQ, ZRF, ZRI, ZRG = [z_room[:, c, :] for c in range(PARTS)]
        sq = sb("sq", [P, 2, TT])
        rb = sb("rb", [P, 2, TT])
        rx = sb("rx", [P, NT + 1])
        hf = rb[:, 1, :].rearrange("p (s w) -> p s w", s=NPC)
        KK, LF, B, EB, KD, QD = [xT[:, k, :] for k in range(6)]
        rest = xT[:, 6:8, :].rearrange("p k t -> p (k t)")
        KDT = rest[:, 0:(NT + 1) * P].rearrange("p (t c) -> p t c", c=P)
        ends = rest[:, (NT + 1) * P:(NT + 1) * P + NT + NB]
        zp = [ps(f"z_ps{n}", [P, 512]) for n in range(NPC)]
        ms = [ps(f"ms_ps{n}", [P, 512]) for n in range(NPC)]
        tr = [ps(f"tr_ps{n}", [P, 512]) for n in range(2)]

        x_in = keep["x_in"]
        x_tr = [sem(f"x_tr{b}") for b in range(2)]
        x_ev = [sem(f"x_ev{b}") for b in range(2)]
        ms_ready = sem("ms_ready")
        rx_ready = sem("rx_ready")
        rx_clear = sem("rx_clear")
        rb_ready = sem("rb_ready")
        hf_ready = sem("hf_ready")
        hi_ready = sem("hi_ready")
        lo_ready = sem("lo_ready")
        raw_in = [sem(f"raw_in{s}") for s in range(3)]
        w_ready = sem("w_ready")
        z_ready = sem("z_ready")
        z_free = sem("z_free")
        qk_ms = sem("qk_ms")
        qk_rb = sem("qk_rb")
        qk_normed = sem("qk_normed")
        tr_ready = [sem(f"tr_ready{b}") for b in range(2)]
        tr_free = [sem(f"tr_free{b}") for b in range(2)]
        f_ready = sem("f_ready")
        lf_ready = sem("lf_ready")
        b_ready = sem("b_ready")
        eb_ready = sem("eb_ready")
        dk_ready = sem("dk_ready")
        ek_ready = sem("ek_ready")
        kd_ready = sem("kd_ready")
        qd_ready = sem("qd_ready")
        NAMES = ("q", "k", "kt", "v", "rq", "kk", "b", "qd", "kd", "ri", "rg")
        STORES = {n: {"kt": 32, "v": 32, "ri": 32, "kd": 48}.get(n, 16) for n in NAMES}
        stored = {n: sem(f"stored_{n}") for n in NAMES}
        x_stored = sem("x_stored")

        w_view = io["w_in"][0].rearrange("(k p) (t h c) -> p t k h c", p=P, t=PARTS, h=H)
        W0, Z0, F0, R0, N0 = PARTS, NPC * PARTS, NPC, 1, 2 * NPC
        TR_PER = (8, 4)

        def split_at(h, c):
            return h * PARTS + (W0 + c)

        def summed(h, c, n):
            return h * (NPC * PARTS) + (Z0 + NPC * c + n + 1)

        def copied(h, c, n):
            return h * (NPC * PARTS) + (F0 + NPC * c + n + 1)

        def normed(h, i):
            return h * (2 * NPC) + (N0 + NPC * i + NPC)

        def token_major(h, i):
            return h * TR_PER[0] + (R0 + 2 * i + 2)

        clear_last(nc, keep)
        with nc.Block() as block:
            @block.sync
            def _(sp):
                for s, n in ((w_ready, W0), (z_ready, Z0), (z_free, F0), (tr_free[0], R0), (tr_free[1], R0), (qk_normed, N0), (qk_rb, N0)):
                    sp.sem_inc(s, n)
                for n in NAMES:
                    sp.sem_inc(stored[n], STORES[n])
                sp.sem_inc(qd_ready, 1)
                for h in range(H):
                    flat = io["skew"][h].rearrange("p w -> (p w)")
                    shifted = flat[P - 1:P - 1 + P * (BW - 1)].rearrange("(p w) -> p w", w=BW - 1)
                    sp.dma_start(keep["bias"][:, h, :], shifted[:, 0:2 * P]).then_inc(keep["skewed"], 16)
                with sp.Fori(0, H) as h:
                    def load(c):
                        sp.wait_ge(w_ready, split_at(h, c) - (W_BACK[c] - 1))
                        sp.dma_start(raw[:, W_SLOT[c], :, :], w_view[:, c, :, bass.ds(h, 1), :].rearrange("p k o c -> p k (o c)"))\
                          .then_inc(raw_in[W_SLOT[c]], 16)

                    def store(name, src, ready, value):
                        sp.wait_ge(ready, value)
                        sp.dma_start(io[name + "_d"][bass.ds(h, 1)].rearrange("o p t -> p (o t)"), src[:, :]).then_inc(stored[name], 16)

                    def store_tokens(name, prompt, sample, i):
                        sp.wait_ge(tr_free[0], token_major(h, i))
                        sp.dma_start(prompt.rearrange("(t p) h c -> h p t c", p=P)[bass.ds(h, 1)].rearrange("o p t c -> p (o t) c"),
                                     tm[:, i, 0:NT, :]).then_inc(stored[name], 16)
                        sp.dma_start(sample.rearrange("t h c -> h t c")[bass.ds(h, 1)].rearrange("o t c -> t (o c)"),
                                     tm[0:NS, i, NT, :]).then_inc(stored[name], 16)

                    load(0)
                    load(1)
                    load(2)
                    load(3)
                    store("q", ZQ, qk_normed, normed(h, 0))
                    load(4)
                    store("k", ZK, qk_normed, normed(h, 1))
                    load(5)
                    store_tokens("kt", io["k_prompt"], io["k_sample"], 0)
                    store("rq", ZRQ, z_free, copied(h, 3, NPC - 1))
                    store_tokens("v", io["v_prompt"], io["v_sample"], 1)
                    load(6)
                for n in ("q", "k", "kt", "v", "rq"):
                    sp.wait_ge(stored[n], STORES[n] * (H + 1))
                sp.wait_ge(x_stored, 16)
                sp.wait_ge(keep["skewed"], 16 * (H + 1))

            @block.gpsimd
            def _(pool):
                link = keep["pool_chain"].of(pool)
                with link.loop(H, PARTS) as h:
                    for c in range(PARTS):
                        s = W_SLOT[c]
                        pool.wait_ge(raw_in[s], h * (16 * W_USES[s]) + 16 * (W_NTH[c] + 1))
                        pool.wait_ge(z_ready, h * (NPC * PARTS) + (Z0 + NPC * (c - W_BACK[c] + 1)))
                        split_weights(nc, keep["ones"][:, :], raw[:, s, :, :], whi[s][:, :, :], wlo[s][:, :, :], link).then_inc(w_ready, 1)

            @block.tensor
            def _(pe):
                for t in range(NT + 1):
                    rows = P if t < NT else NS
                    pe.wait_ge(x_in[t // 3], 48)
                    for half in range(2):
                        if t:
                            pe.wait_ge(x_ev[half], t)
                        for j in range(4):
                            last = nc.tensor.transpose(tr[half][:, j * P:j * P + rows], x[t][0:rows, (half * 4 + j) * P:(half * 4 + j + 1) * P], keep["ident"][0:rows, 0:rows])
                        last.then_inc(x_tr[half], 1)
                pe.wait_ge(rx_ready, 1)
                for t in range(NT + 1):
                    rows = P if t < NT else NS
                    last = nc.tensor.matmul(ms[t // 4][:, (t % 4) * P:(t % 4) * P + rows], rx[0:rows, t:t + 1].broadcast_to([rows, P]), keep["ident"][0:rows, 0:rows],
                                            start=True, stop=True)
                    if t in (3, 7, 8):
                        last.then_inc(ms_ready, 1)
                pe.wait_ge(keep["late_in"], 5 * 16)

                with pe.Fori(0, H) as h:
                    def main(c, n):
                        s = W_SLOT[c]
                        if n == 0:
                            pe.wait_ge(w_ready, split_at(h, c) + 1)
                        if c == 0:
                            pe.wait_ge(lo_ready, KC * (n + 1))
                        pe.wait_ge(z_free, copied(h, c, n) - NPC)
                        split_product(nc, zp[n][:, 0:PW], whi[s], wlo[s], hh[:, :, piece(n)], hl[:, :, piece(n)]).then_inc(z_ready, 1)

                    def sums(i):
                        for n in range(NPC):
                            pe.wait_ge(z_free, copied(h, i, n))
                            if i:
                                pe.wait_ge(qk_rb, h * (2 * NPC) + (N0 + n + 1))
                            nc.tensor.matmul(ms[n][:, 0:PW], keep["blk"][:, :], sq[:, i, piece(n)], start=True, stop=True).then_inc(qk_ms, 1)

                    def tokens(i, src, ready, value):
                        pe.wait_ge(ready, value)
                        for b, first, end, use in ((0, 0, 4, 2 * i), (1, 4, 8, i), (0, 8, 9, 2 * i + 1)):
                            pe.wait_ge(tr_free[b], h * TR_PER[b] + (use + R0))
                            for t in range(first, end):
                                rows = P if t < NT else NS
                                last = nc.tensor.transpose(tr[b][0:rows, (t - first) * P:(t - first + 1) * P], src[:, t * P:t * P + rows], keep["ident"][:, :])
                            last.then_inc(tr_ready[b], 1)

                    main(0, 0), main(0, 1), main(0, 2)
                    main(1, 0), sums(0), main(1, 1), main(1, 2)
                    main(2, 0), sums(1), main(2, 1), main(2, 2)
                    main(3, 0), tokens(0, ZK, qk_normed, normed(h, 1)), main(3, 1)
                    tokens(1, ZV, z_free, copied(h, 2, NPC - 1)), main(3, 2)
                    main(4, 0), main(4, 1), main(4, 2)
                    main(5, 0), main(5, 1), main(5, 2)
                    main(6, 0), tokens(2, ZRI, z_free, copied(h, 5, NPC - 1)), main(6, 1), tokens(3, KD, kd_ready, h + 1), main(6, 2)

            @block.scalar
            def _(act):
                a = nc.scalar.activation
                link = keep["act_chain"].of(act)
                act.wait_ge(rx_clear, 1)
                for t in range(NT + 1):
                    rows = P if t < NT else NS
                    act.wait_ge(x_in[t // 3], 48)
                    link(a(sq[0:rows, 0, 0:D], x[t][0:rows, :], ACT.Square, accum_out=rx[0:rows, t:t + 1]))
                link(a(rx[:, :], rx[:, :], ACT.Ln, bias=keep["eps"][:, 0:1], scale=1.0 / D))
                a(rx[:, :], rx[:, :], ACT.Exp, scale=-0.5).then_inc(rx_ready, 1)
                for n, w in enumerate((512, 512, NS)):
                    act.wait_ge(ms_ready, n + 1)
                    a(rb[:, 0, 512 * n:512 * n + w], ms[n][:, 0:w], ACT.Copy).then_inc(rb_ready, 1)
                norm_high(nc, act, hf, hh, hf_ready, hi_ready)
                act.wait_ge(x_ev[0], NT + 1)
                act.wait_ge(x_ev[1], NT + 1)
                act.dma_start(io["x_d"], xT[:, :, :]).then_inc(x_stored, 16)

                with link.loop(H, 2) as h:
                    def free(name):
                        act.wait_ge(stored[name], h * STORES[name] + STORES[name])

                    def copy(c, n, dst, func=ACT.Copy):
                        act.wait_ge(z_ready, summed(h, c, n))
                        return a(dst[:, piece(n)], zp[n][:, 0:PW], func)

                    def squared(c, n, dst):
                        copy(c, n, dst)
                        a(sq[:, c, piece(n)], zp[n][:, 0:PW], ACT.Square).then_inc(z_free, 1)

                    def inverse(i):
                        for n in range(NPC):
                            act.wait_ge(qk_ms, h * (2 * NPC) + (NPC * i + n + 1))
                            last = a(rb[:, i, piece(n)], ms[n][:, 0:PW], ACT.Ln, bias=keep["eps"][:, 0:1], scale=1.0 / HD)
                        link(last)
                        for n in range(NPC):
                            a(rb[:, i, piece(n)], rb[:, i, piece(n)], ACT.Exp, scale=-0.5).then_inc(qk_rb, 1)

                    free("q")
                    for n in range(NPC):
                        squared(0, n, ZQ)
                    free("k")
                    squared(1, 0, ZK)
                    inverse(0)
                    squared(1, 1, ZK), squared(1, 2, ZK)
                    free("v")
                    copy(2, 0, ZV).then_inc(z_free, 1)
                    inverse(1)
                    copy(2, 1, ZV).then_inc(z_free, 1), copy(2, 2, ZV).then_inc(z_free, 1)
                    free("rq")
                    act.wait_ge(qd_ready, h + 1)
                    for n in range(NPC):
                        copy(3, n, ZRQ).then_inc(z_free, 1)
                    for n in range(NPC):
                        copy(4, n, ZRF, ACT.Sigmoid).then_inc(z_free, 1)
                    free("ri")
                    copy(5, 0, ZRI).then_inc(z_free, 1)
                    act.wait_ge(f_ready, h * 2 + 1)
                    a(LF, ZRF[:, :], ACT.Ln).then_inc(lf_ready, 1)
                    copy(5, 1, ZRI).then_inc(z_free, 1)
                    act.wait_ge(b_ready, h + 1)
                    a(EB, B, ACT.Exp).then_inc(eb_ready, 1)
                    act.wait_ge(dk_ready, h + 1)
                    a(KD, KD, ACT.Exp).then_inc(ek_ready, 1)
                    copy(5, 2, ZRI).then_inc(z_free, 1)
                    free("rg")
                    for n in range(NPC):
                        copy(6, n, ZRG, ACT.Silu).then_inc(z_free, 1)
                    for name, src, ready in (("kk", KK, f_ready), ("b", B, b_ready), ("qd", QD, qd_ready)):
                        act.wait_ge(ready, {"kk": h * 2 + 2, "b": h + 1, "qd": h + 2}[name])
                        act.dma_start(io[name + "_d"][bass.ds(h, 1)].rearrange("o p t -> p (o t)"), src).then_inc(stored[name], 16)
                    act.wait_ge(tr_free[0], token_major(h, 2))
                    for name, src in (("ri", tm[:, 2]), ("kd", KDT)):
                        if name == "kd":
                            act.wait_ge(tr_free[0], token_major(h, 3))
                        act.dma_start(io[name + "_d"][bass.ds(h, 1)].rearrange("o p t c -> p (o t) c")[:, 0:NT, :], src[:, 0:NT, :]).then_inc(stored[name], 16)
                        act.dma_start(io[name + "_d"][bass.ds(h, 1)].rearrange("o p t c -> p (o t) c")[0:NS, NT, :], src[0:NS, NT, :]).then_inc(stored[name], 16)
                    act.dma_start(io["ends_d"][bass.ds(h, 1)].rearrange("o p t -> p (o t)"), ends).then_inc(stored["kd"], 16)
                    act.wait_ge(z_free, copied(h, 6, NPC - 1))
                    act.dma_start(io["rg_d"][bass.ds(h, 1)].rearrange("o p t -> p (o t)"), ZRG[:, :]).then_inc(stored["rg"], 16)
                for n in ("kk", "b", "qd", "kd", "ri", "rg"):
                    act.wait_ge(stored[n], STORES[n] * (H + 1))

            @block.vector
            def _(dve):
                v = nc.vector
                v.memset(rx[:, :], 1.0).then_inc(rx_clear, 1)
                for t in range(NT + 1):
                    rows = P if t < NT else NS
                    for b in range(2):
                        dve.wait_ge(x_tr[b], t + 1)
                        v.tensor_copy(xT[:, 4 * b:4 * b + 4, t * P:t * P + rows], tr[b][:, :].rearrange("p (k c) -> p k c", k=4)[:, :, 0:rows]).then_inc(x_ev[b], 1)
                dve.wait_ge(x_ev[1], NT + 1)
                norm_low(nc, dve, xT, vector(keep, "norm1_g"), rb[:, 0, :], hf, hh, hl, rb_ready, hf_ready, hi_ready, lo_ready)
                dve.wait_ge(lo_ready, KC * NPC)

                with dve.Fori(0, H) as h:
                    def scale(i, z):
                        for n in range(NPC):
                            dve.wait_ge(qk_rb, h * (2 * NPC) + (N0 + NPC * i + n + 1))
                            v.scalar_tensor_tensor(z[:, piece(n)], z[:, piece(n)], vector(keep, "qk_norm_g")[:, i:i + 1], rb[:, i, piece(n)],
                                                   ALU.mult, ALU.mult).then_inc(qk_normed, 1)

                    def tokens(i, name, dst):
                        dve.wait_ge(stored[name], h * STORES[name] + STORES[name])
                        for b, first, end, use in ((0, 0, 4, 2 * i), (1, 4, 8, i), (0, 8, 9, 2 * i + 1)):
                            dve.wait_ge(tr_ready[b], h * TR_PER[b] + (use + 1))
                            rows = P if first < NT else NS
                            v.tensor_copy(dst[0:rows, first:end, :].rearrange("p t c -> p (t c)"), tr[b][0:rows, 0:(end - first) * P]).then_inc(tr_free[b], 1)

                    scale(0, ZQ)
                    scale(1, ZK)
                    tokens(0, "kt", tm[:, 0])
                    tokens(1, "v", tm[:, 1])
                    dve.wait_ge(x_stored, 16)
                    dve.wait_ge(z_free, copied(h, 4, NPC - 1))
                    v.tensor_scalar(ZRF[:, :], ZRF[:, :], keep["lb1"][:, bass.ds(h, 1)], keep["lb0"][:, bass.ds(h, 1)], ALU.mult, ALU.add).then_inc(f_ready, 1)
                    dve.wait_ge(f_ready, h * 2 + 1)
                    dve.wait_ge(stored["kk"], h * 16 + 16)
                    v.tensor_scalar(KK, ZRF[:, :], -1.0, 1.0, ALU.mult, ALU.add).then_inc(f_ready, 1)
                    dve.wait_ge(stored["b"], h * 16 + 16)
                    dve.wait_ge(lf_ready, h + 1)
                    for first, n, w in ((0, NT, P), (T, NB, TS)):
                        for t in range(first, first + n * w, w):
                            last = v.tensor_tensor_scan(B[:, t:t + w], keep["ones"][:, 0:w], LF[:, t:t + w], 0.0, ALU.mult, ALU.add)
                    last.then_inc(b_ready, 1)
                    dve.wait_ge(b_ready, h + 1)
                    for first, n, w in ((0, NT, P), (T, NB, TS)):
                        view = B[:, first:first + n * w].rearrange("p (n w) -> p n w", w=w)
                        last = v.tensor_tensor(KD[:, first:first + n * w].rearrange("p (n w) -> p n w", w=w), view[:, :, w - 1:w].broadcast_to([P, n, w]), view, ALU.subtract)
                    last.then_inc(dk_ready, 1)
                    tokens(2, "ri", tm[:, 2])
                    dve.wait_ge(eb_ready, h + 1)
                    dve.wait_ge(stored["qd"], h * 16 + 16)
                    v.tensor_tensor(QD, ZRQ[:, :], EB, ALU.mult).then_inc(qd_ready, 1)
                    dve.wait_ge(stored["kd"], h * 48 + 48)
                    v.tensor_copy(ends[:, 0:NT], EB[:, P - 1:T:P])
                    v.tensor_copy(ends[:, NT:NT + NB], EB[:, T + TS - 1:TT:TS])
                    dve.wait_ge(ek_ready, h + 1)
                    v.tensor_tensor(KD, KD, KK, ALU.mult).then_inc(kd_ready, 1)
                    tokens(3, "kd", KDT)


L_USE = {0: 0, 1: 4, 2: 5, 3: 7, 4: 8, 5: 11, 6: 12, 7: 13}
SG_USE, U_USE, SU_USE, O_USE, SO_USE = 6, 2, 9, 14, 16
REC_PER = (9, 8)
REC_SLOT = [(0, 1), (2, 3), (4, 5, 6), (7, 8), (9, 10), (11, 12), (13,), (), (14, 15, 16)]
LEVEL_SLOT = [(2, 3), (4,), (5,), (6,), (7,), (), (), ()]
AHEAD = (1,)
HP = P // 2
KDM_SLOT = 3
T_GROUPS = [(i + 4) // 4 for i in range(NT)]
T_FIRST = [sum(T_GROUPS[:i]) for i in range(NT)]
T_PER = sum(T_GROUPS)


def blocks_of(x, w, n):
    return x[:, 0:n].rearrange("p (b s w) -> p b s w", s=2, w=w // 2)


def heads(nc, io, keep):
    with ExitStack() as ctx:
        sb, ps, sem = open_memory(nc, ctx, keep["sems"])
        Q = [sb(f"q{p}", [P, 2, T]) for p in range(2)]
        K = [sb(f"k{p}", [P, T]) for p in range(2)]
        V = [sb(f"v{p}", [P, NT, P]) for p in range(2)]
        RQ = [sb(f"rq{p}", [P, TT]) for p in range(2)]
        KK = [sb(f"kk{p}", [P, TT]) for p in range(2)]
        B = [sb(f"b{p}", [P, TT]) for p in range(2)]
        QD = [sb(f"qd{p}", [P, TT]) for p in range(2)]
        KDT = [sb(f"kdt{p}", [P, NT + 1, P]) for p in range(2)]
        ends = [sb(f"ends{p}", [P, NT + NB]) for p in range(2)]
        RI = [sb(f"ri{p}", [P, NT + 1, P]) for p in range(2)]
        OA = [sb(f"oa{p}", [P, T]) for p in range(2)]
        OR = [sb(f"or{p}", [P, TT]) for p in range(2)]
        gates = sb("gates", [1, LEVELS + 1 + SLEVELS])
        near = sb("near", [P, 2, 2 * P])
        E = sb("E", [P, 2, T])
        A = [sb(f"A{p}", [P, T]) for p in range(2)]
        At = [sb(f"At{p}", [P, T]) for p in range(2)]
        mx = sb("mx", [P, 2, 2])
        negm = sb("negm", [P, 2])
        farb = sb("farb", [P, 2])
        ls = sb("ls", [P, 2, 2])
        lt = sb("lt", [P, 2])
        rl = sb("rl", [P, 2])
        c1 = sb("c1", [P, 1])
        X = [sb(f"X{p}", [P, TT]) for p in range(1, LEVELS)]
        KDM = sb("KDM", [NS, NB, P])
        AT = sb("AT", [P, NT, P])
        ATS = sb("ATS", [NS, NS])
        ST = sb("ST", [P, NT + 1, P])
        SIN = sb("SIN", [P, NB, P])
        SOUT = sb("SOUT", [P, NB, P])
        S = ps("S", [P, 2, T])
        trp = ps("trp", [P, 512])
        pvp = ps("pvp", [P, 512])
        rec = [ps(f"rec{p}", [P, 512]) for p in range(2)]

        early_in = [sem(f"early_in{p}") for p in range(2)]
        loaded = [sem(f"loaded{p}") for p in range(2)]
        states_in = sem("states_in")
        s_ready = sem("s_ready")
        small = sem("small")
        mx_ready = sem("mx_ready")
        e_ready = sem("e_ready")
        a_ready = sem("a_ready")
        t_ready = sem("t_ready")
        t_free = sem("t_free")
        pv_ready = sem("pv_ready")
        pv_free = sem("pv_free")
        d_ready = sem("d_ready")
        ex_ready = sem("ex_ready")
        x_ready = sem("x_ready")
        kdm_ready = sem("kdm_ready")
        zeroed = sem("zeroed")
        rec_ready = [sem(f"rec_ready{p}") for p in range(2)]
        rec_free = [sem(f"rec_free{p}") for p in range(2)]
        oa_stored = [sem(f"oa_stored{p}") for p in range(2)]
        or_stored = [sem(f"or_stored{p}") for p in range(2)]
        st_stored = sem("st_stored")
        so_stored = sem("so_stored")
        LOADS = 7 * 16
        SMALL = sum(9 if i > 1 else 6 for i in range(NT)) + (SLEVELS - 1) + 6

        def ready(h, u):
            return h * REC_PER[u % 2] + (REC_PER[u % 2] + u // 2 + 1)

        def ready_before(h, u):
            return h * REC_PER[u % 2] + (u // 2 + 1)

        freed = ready

        def each_head(eng, body):
            with eng.Fori(0, H // 2) as pair:
                for par in range(2):
                    body(pair * 2 + par, par, pair)

        clear_last(nc, keep)
        with nc.Block() as block:
            @block.sync
            def _(sp):
                for s in (t_free, pv_free, t_ready):
                    sp.sem_inc(s, 1)
                for b in range(2):
                    sp.sem_inc(rec_ready[b], REC_PER[b])
                    sp.sem_inc(rec_free[b], REC_PER[b])
                for s in (*oa_stored, *or_stored, st_stored, so_stored):
                    sp.sem_inc(s, 16)

                def load(h):
                    p = h % 2
                    for ready, copies in ((early_in, ((Q[p][0:HD, 0, :], io["q_d"][h, 0:HD, 0:T]), (Q[p][HD:P, 1, :], io["q_d"][h, HD:P, 0:T]), (K[p][:, :], io["k_d"][h, :, 0:T]),
                                                      (B[p][:, :], io["b_d"][h]), (KK[p][:, :], io["kk_d"][h]), (RQ[p][:, :], io["rq_d"][h]))),
                                          (loaded, ((V[p][:, :, :], io["v_prompt"].rearrange("(t p) h c -> h p t c", p=P)[h]),
                                                    (KDT[p][:, 0:NT, :], io["kd_d"][h, :, 0:NT, :]), (KDT[p][0:NS, NT, :], io["kd_d"][h, 0:NS, NT, :]),
                                                    (RI[p][:, 0:NT, :], io["ri_d"][h, :, 0:NT, :]), (RI[p][0:NS, NT, :], io["ri_d"][h, 0:NS, NT, :]),
                                                    (QD[p][:, :], io["qd_d"][h]), (ends[p][:, :], io["ends_d"][h])))):
                        for dst, src in copies:
                            sp.dma_start(dst, src).then_inc(ready[p], 16)

                def states(h):
                    sp.dma_start(SIN[:, :, :], io["state_hgrn"][0].rearrange("b h k v -> h k b v")[h]).then_inc(states_in, 16)

                load(0)
                states(0)
                load(1)
                for h in range(H):
                    p = h % 2
                    sp.wait_ge(rec_free[(U_USE + 1) % 2], freed(h, U_USE + 1))
                    sp.dma_start(io["hgrn_prompt"][h], ST[:, NT, :]).then_inc(st_stored, 16)
                    sp.wait_ge(rec_free[(SU_USE + 1) % 2], freed(h, SU_USE + 1))
                    sp.dma_start(io["hgrn_sample"].rearrange("b h k v -> h k b v")[h], SOUT[:, :, :]).then_inc(so_stored, 16)
                    sp.wait_ge(rec_free[SO_USE % 2], freed(h, SO_USE))
                    if h + 1 < H:
                        states(h + 1)
                    sp.wait_ge(rec_free[(O_USE + 1) % 2], freed(h, O_USE + 1))
                    sp.dma_start(io["o_d"][H + h], OR[p][:, :]).then_inc(or_stored[p], 16)
                    sp.wait_ge(pv_free, h * NT + NT + 1)
                    sp.dma_start(io["o_d"][h, :, 0:T], OA[p][:, :]).then_inc(oa_stored[p], 16)
                    if h + 2 < H:
                        load(h + 2)
                for p in range(2):
                    sp.wait_ge(oa_stored[p], 16 * 3)
                    sp.wait_ge(or_stored[p], 16 * 3)
                sp.wait_ge(st_stored, 16 * (H + 1))
                sp.wait_ge(so_stored, 16 * (H + 1))

            @block.gpsimd
            def _(pool):
                tt = nc.gpsimd.tensor_tensor

                def body(h, par, pair):
                    def tokens(l):
                        return TT if l < SLEVELS else T

                    def distances(l):
                        bl, xl = blocks_of(B[par], 2 ** l, tokens(l)), blocks_of(X[l - 1], 2 ** l, tokens(l))
                        w = 2 ** l // 2
                        mid = bl[:, :, 0, w - 1:w].broadcast_to([P, tokens(l) // (2 * w), w])
                        u = SG_USE if l < SLEVELS else L_USE[l]
                        pool.wait_ge(rec_ready[u % 2], ready_before(h, u))
                        tt(xl[:, :, 0, :], mid, bl[:, :, 0, :], ALU.subtract)
                        tt(xl[:, :, 1, :], bl[:, :, 1, :], mid, ALU.subtract).then_inc(d_ready, 1)

                    def weigh(l):
                        xl = blocks_of(X[l - 1], 2 ** l, tokens(l))
                        pool.wait_ge(ex_ready, h * (LEVELS - 1) + l)
                        tt(xl[:, :, 0, :], xl[:, :, 0, :], blocks_of(KK[par], 2 ** l, tokens(l))[:, :, 0, :], ALU.mult)
                        tt(xl[:, :, 1, :], xl[:, :, 1, :], blocks_of(RQ[par], 2 ** l, tokens(l))[:, :, 1, :], ALU.mult).then_inc(x_ready, 1)

                    pool.wait_ge(early_in[par], pair * 96 + 96)
                    distances(1), distances(2)
                    for l in range(1, LEVELS - 2):
                        weigh(l), distances(l + 2)
                    weigh(LEVELS - 2), weigh(LEVELS - 1)

                each_head(pool, body)

            @block.tensor
            def _(pe):
                mm = nc.tensor.matmul

                def body(h, par, pair):
                    def scores(i):
                        if i == 0:
                            pe.wait_ge(early_in[par], pair * 96 + 96)
                        n = (i + 1) * P
                        for m in range(2):
                            pe.wait_ge(e_ready, h * (2 * NT) + (2 * i + m + 1))
                            for c in range(0, n, 512):
                                w = min(512, n - c)
                                last = mm(S[:, m, c:c + w], Q[par][:, m, i * P:(i + 1) * P], K[par][:, c:c + w], start=True, stop=True)
                            last.then_inc(s_ready, 1)

                    def attend(i, uses):
                        uses = list(uses)

                        def between():
                            if uses:
                                recur(uses.pop(0))

                        def values(first, end):
                            pe.wait_ge(t_free, h * T_PER + (T_FIRST[i] + first // 4 + 2))
                            for j in range(first, end):
                                last = mm(pvp[:, 0:P], V[par][:, j, :], At[i % 2][:, j * P:(j + 1) * P], start=(j == 0), stop=(j == i))
                            return last

                        if i == 0:
                            pe.wait_ge(loaded[par], pair * LOADS + LOADS)
                        pe.wait_ge(a_ready, h * NT + (i + 1))
                        for g in range(T_GROUPS[i]):
                            pe.wait_ge(t_free, h * T_PER + (T_FIRST[i] + g + 1))
                            for j in range(4 * g, min(4 * g + 4, i + 1)):
                                last = nc.tensor.transpose(trp[:, (j % 4) * P:(j % 4 + 1) * P], A[i % 2][:, j * P:(j + 1) * P], keep["ident"][:, :])
                            last.then_inc(t_ready, 1)
                            between()
                        pe.wait_ge(pv_free, h * NT + (i + 1))
                        for j in range(0, i + 1, 4):
                            last = values(j, min(j + 4, i + 1))
                        last.then_inc(pv_ready, 1)
                        for u in uses:
                            recur(u)

                    def recur(u):
                        bank = rec[u % 2]
                        pe.wait_ge(rec_free[u % 2], freed(h, u) - 1)
                        if u in (L_USE[0], L_USE[0] + 1):
                            pe.wait_ge(early_in[par], pair * 96 + 96)
                            for j in range(4):
                                t = slice((4 * (u - L_USE[0]) + j) * P, (4 * (u - L_USE[0]) + j + 1) * P)
                                last = mm(bank[:, j * P:(j + 1) * P], KK[par][:, t], RQ[par][:, t], start=True, stop=True)
                        for l in range(1, LEVELS):
                            if u == L_USE[l]:
                                pe.wait_ge(x_ready, h * (LEVELS - 1) + l)
                                for t in range(NT):
                                    tile = X[l - 1][:, t * P:(t + 1) * P]
                                    last = mm(bank[:, t * HP:(t + 1) * HP], tile, blocks_of(tile, 2 ** l, P)[:, :, 1, :], start=True, stop=True)
                        if u == SG_USE:
                            for l in range(SLEVELS):
                                left, right = (KK[par], RQ[par]) if l == 0 else (X[l - 1],) * 2
                                last = mm(bank[0:NS, l * NS:(l + 1) * NS], left[:, T:TT], right[:, T:TT], start=True, stop=True)
                        if U_USE <= u < U_USE + 2:
                            for j in range(4):
                                t = 4 * (u - U_USE) + j
                                last = mm(bank[:, j * P:(j + 1) * P], KDT[par][:, t, :], RI[par][:, t, :], start=True, stop=True)
                        if SU_USE <= u < SU_USE + 2:
                            pe.wait_ge(kdm_ready, h + 1)
                            for j in range(4):
                                last = mm(bank[:, j * P:(j + 1) * P], KDM[:, 4 * (u - SU_USE) + j, :], RI[par][0:NS, NT, :], start=True, stop=True)
                        if O_USE <= u < O_USE + 2:
                            if u == O_USE:
                                pe.wait_ge(rec_free[(U_USE + 1) % 2], freed(h, U_USE + 1))
                            for j in range(4):
                                t = 4 * (u - O_USE) + j
                                out = bank[:, j * P:(j + 1) * P]
                                mm(out, RI[par][:, t, :], AT[:, t, :], start=True, stop=False)
                                last = mm(out, ST[:, t, :], QD[par][:, t * P:(t + 1) * P], start=False, stop=True)
                        if u == SO_USE:
                            pe.wait_ge(states_in, 16 * h + 16)
                            mm(bank[:, 0:NS], RI[par][0:NS, NT, :], ATS[:, :], start=True, stop=False)
                            for s in range(NB):
                                last = mm(bank[:, s * TS:(s + 1) * TS], SIN[:, s, :], QD[par][:, T + s * TS:T + (s + 1) * TS], start=False, stop=(s == NB - 1))
                        last.then_inc(rec_ready[u % 2], 1)

                    for i in range(NT):
                        scores(i)
                        if i:
                            attend(i - 1, REC_SLOT[i])
                        else:
                            for u in REC_SLOT[i]:
                                recur(u)
                    for u in REC_SLOT[NT]:
                        recur(u)
                    attend(NT - 1, ())

                pe.wait_ge(zeroed, 2)
                each_head(pe, body)

            @block.scalar
            def _(act):
                a = nc.scalar.activation
                act.sem_inc(e_ready, 2)

                def level(l, ahead=0, h=0):
                    n = TT if l < SLEVELS else T
                    act.wait_ge(d_ready, h * (LEVELS - 1) + (ahead * (LEVELS - 1) + l))
                    a(X[l - 1][:, 0:n], X[l - 1][:, 0:n], ACT.Exp).then_inc(ex_ready, 1)

                def body(h, par, pair, last=False):
                    def exponentials(i):
                        n0 = max(0, i - 1) * P
                        n1 = (i + 1) * P
                        for m in range(2):
                            act.wait_ge(mx_ready, h * (2 * NT) + (2 * i + m + 1))
                            if n0:
                                a(E[:, m, 0:n0], S[:, m, 0:n0], ACT.Exp, bias=farb[:, m:m + 1], accum_out=ls[:, m, 1:2])
                            a(E[:, m, n0:n1], near[:, m, 2 * P - (n1 - n0):2 * P], ACT.Exp, bias=negm[:, m:m + 1], accum_out=ls[:, m, 0:1]).then_inc(e_ready, 1)

                    def transposed(i):
                        for g in range(T_GROUPS[i]):
                            act.wait_ge(t_ready, h * T_PER + (T_FIRST[i] + g + 2))
                            w = min(4, i + 1 - 4 * g) * P
                            a(At[i % 2][:, 4 * g * P:4 * g * P + w], trp[:, 0:w], ACT.Copy).then_inc(t_free, 1)

                    def attended(i):
                        if i == 0:
                            act.wait_ge(oa_stored[par], pair * 16 + 16)
                        act.wait_ge(pv_ready, h * NT + (i + 1))
                        a(OA[par][:, i * P:(i + 1) * P], pvp[:, 0:P], ACT.Copy).then_inc(pv_free, 1)

                    def consume(u):
                        if u in range(O_USE, SO_USE + 1):
                            if u == O_USE:
                                act.wait_ge(or_stored[par], pair * 16 + 16)
                            act.wait_ge(rec_ready[u % 2], ready(h, u))
                            c, n = (u - O_USE) * 512, 512 if u < SO_USE else NS
                            a(OR[par][:, c:c + n], rec[u % 2][:, 0:n], ACT.Copy).then_inc(rec_free[u % 2], 1)

                    for i in range(NT):
                        if i:
                            transposed(i - 1)
                        exponentials(i)
                        if i:
                            attended(i - 1)
                        for u in REC_SLOT[i]:
                            consume(u)
                        for l in LEVEL_SLOT[i]:
                            level(l, 0, h)
                        if i == NT - 2 and not last:
                            for l in AHEAD:
                                level(l, 1, h)
                    for u in REC_SLOT[NT]:
                        consume(u)
                    transposed(NT - 1)
                    attended(NT - 1)

                for l in AHEAD:
                    level(l)
                with act.Fori(0, H // 2 - 1) as pair:
                    for par in range(2):
                        body(pair * 2 + par, par, pair)
                for par in range(2):
                    body(H - 2 + par, par, H // 2 - 1, last=(par == 1))

            @block.vector
            def _(dve):
                v = nc.vector
                for p in range(2):
                    v.memset(Q[p][HD:P, 0, :], 0.0)
                    v.memset(Q[p][0:HD, 1, :], 0.0).then_inc(zeroed, 1)
                v.memset(AT[:, :, :], 0.0)
                v.memset(ATS[:, :], 0.0)
                keep["dve_chain"].of(dve)(v.memset(ST[:, 0, :], 0.0))

                def body(h, par, pair):
                    count, gated = [0], [0]

                    def link(ins):
                        ins.then_inc(small, 1)
                        count[0] += 1
                        dve.wait_ge(small, h * SMALL + count[0])

                    def gate():
                        v.memset(gates[:, gated[0]:gated[0] + 1], 0.0)
                        gated[0] += 1

                    def maxima(i):
                        n0, n1 = max(0, i - 1) * P, (i + 1) * P
                        w = n1 - n0
                        bias = keep["bias"][:, bass.ds(h, 1), 2 * P - w:2 * P].rearrange("p o c -> p (o c)")
                        far = keep["far"][:, bass.ds(h, 1)]
                        for m in range(2):
                            neg, scores = negm[:, m:m + 1], near[:, m, 2 * P - w:2 * P]
                            dve.wait_ge(s_ready, h * (2 * NT) + (2 * i + m + 1))
                            link(v.tensor_tensor(scores, S[:, m, n0:n1], bias, ALU.add))
                            if not n0:
                                link(v.tensor_reduce(mx[:, 0, m:m + 1], scores, AX.X, ALU.max))
                                v.tensor_scalar(neg, mx[:, 0, m:m + 1], -1.0, None, ALU.mult).then_inc(mx_ready, 1)
                            else:
                                v.tensor_reduce(mx[:, 0, m:m + 1], scores, AX.X, ALU.max)
                                link(v.tensor_reduce(mx[:, 1, m:m + 1], S[:, m, 0:n0], AX.X, ALU.max))
                                link(v.scalar_tensor_tensor(mx[:, 0, m:m + 1], mx[:, 1, m:m + 1], far, mx[:, 0, m:m + 1], ALU.add, ALU.max))
                                v.tensor_scalar(neg, mx[:, 0, m:m + 1], -1.0, None, ALU.mult)
                                v.tensor_scalar(farb[:, m:m + 1], mx[:, 0, m:m + 1], -1.0, far, ALU.mult, ALU.add).then_inc(mx_ready, 1)

                    def combine(i):
                        n1 = (i + 1) * P
                        dve.wait_ge(e_ready, h * (2 * NT) + (2 * i + 4))
                        l = ls[:, :, 0]
                        if i > 1:
                            link(v.tensor_tensor(lt[:, :], ls[:, :, 0], ls[:, :, 1], ALU.add))
                            l = lt[:, :]
                        link(v.reciprocal(rl[:, :], l))
                        if i >= 2:
                            dve.wait_ge(t_ready, h * T_PER + (T_FIRST[i - 1] + 1))
                        else:
                            dve.wait_ge(t_ready, h * T_PER + 1)
                        v.tensor_scalar(c1[:, :], rl[:, 1:2], keep["lam"][:, 1:2], None, ALU.mult)
                        link(v.tensor_scalar(A[i % 2][:, 0:n1], E[:, 0, 0:n1], rl[:, 0:1], None, ALU.mult))
                        v.scalar_tensor_tensor(A[i % 2][:, 0:n1], E[:, 1, 0:n1], c1[:, 0:1], A[i % 2][:, 0:n1], ALU.mult, ALU.add).then_inc(a_ready, 1)

                    def consume(u):
                        bank = rec[u % 2]
                        if u in (L_USE[0], L_USE[0] + 1):
                            dve.wait_ge(rec_ready[u % 2], ready(h, u))
                            if u == L_USE[0]:
                                dve.wait_ge(rec_ready[(O_USE + 1) % 2], ready_before(h, O_USE + 1))
                            gate()
                            t = 4 * (u - L_USE[0])
                            v.copy_predicated(AT[:, t:t + 4, :], keep["lmask"][:, 0:P].rearrange("p (o c) -> p o c", o=1).broadcast_to([P, 4, P]),
                                              bank[:, :].rearrange("p (t c) -> p t c", t=4)).then_inc(rec_free[u % 2], 1)
                        for l in range(1, LEVELS):
                            if u == L_USE[l]:
                                dve.wait_ge(rec_ready[u % 2], ready(h, u))
                                dve.wait_ge(rec_free[(u - 1) % 2], freed(h, u - 1))
                                gate()
                                n, w = P // 2 ** l, 2 ** l // 2
                                mask = keep["lmask"][:, P + (l - 1) * HP:P + l * HP].rearrange("p (o n w) -> p o n w", o=1, w=w).broadcast_to([P, NT, n, w])
                                v.copy_predicated(AT[:, :, :].rearrange("p t (n s w) -> p t n s w", s=2, w=w)[:, :, :, 1, :], mask,
                                                  bank[:, :].rearrange("p (t n w) -> p t n w", t=NT, w=w)).then_inc(rec_free[u % 2], 1)
                        if u == SG_USE:
                            dve.wait_ge(rec_ready[u % 2], ready(h, u))
                            gate()
                            for l in range(SLEVELS):
                                last = v.copy_predicated(ATS[:, :], keep["slmask"][:, l, :], bank[0:NS, l * NS:(l + 1) * NS])
                                if l < SLEVELS - 1:
                                    link(last)
                                    gate()
                            last.then_inc(rec_free[u % 2], 1)
                        if U_USE <= u < U_USE + 2:
                            dve.wait_ge(rec_ready[u % 2], ready(h, u))
                            if u > U_USE:
                                dve.wait_ge(rec_free[(u - 1) % 2], freed(h, u - 1))
                                dve.wait_ge(st_stored, h * 16 + 16)
                            for j in range(4):
                                t = 4 * (u - U_USE) + j
                                last = v.scalar_tensor_tensor(ST[:, t + 1, :], ST[:, t, :], ends[par][:, t:t + 1], bank[:, j * P:(j + 1) * P], ALU.mult, ALU.add)
                                if j < 3:
                                    link(last)
                            last.then_inc(rec_free[u % 2], 1)
                        if SU_USE <= u < SU_USE + 2:
                            dve.wait_ge(rec_ready[u % 2], ready(h, u))
                            if u == SU_USE:
                                dve.wait_ge(states_in, 16 * h + 16)
                                dve.wait_ge(so_stored, h * 16 + 16)
                            for j in range(4):
                                s = 4 * (u - SU_USE) + j
                                last = v.scalar_tensor_tensor(SOUT[:, s, :], SIN[:, s, :], ends[par][:, NT + s:NT + s + 1], bank[:, j * P:(j + 1) * P], ALU.mult, ALU.add)
                            last.then_inc(rec_free[u % 2], 1)

                    for i in range(NT):
                        if i:
                            combine(i - 1)
                        maxima(i)
                        if i == KDM_SLOT:
                            dve.wait_ge(loaded[par], pair * LOADS + LOADS)
                            dve.wait_ge(rec_ready[(SU_USE + 1) % 2], ready_before(h, SU_USE + 1))
                            v.tensor_tensor(KDM[:, :, :], KDT[par][0:NS, NT:NT + 1, :].broadcast_to([NS, NB, P]),
                                            keep["rowmask"][:, :].rearrange("p (b o) -> p b o", o=1).broadcast_to([NS, NB, P]), ALU.mult).then_inc(kdm_ready, 1)
                        for u in REC_SLOT[i]:
                            consume(u)
                    combine(NT - 1)
                    for u in REC_SLOT[NT]:
                        consume(u)
                    assert count[0] == SMALL, (count, SMALL)

                each_head(dve, body)


def samples(nc, io, keep, O, hh, hl, acc):
    with ExitStack() as ctx:
        sb, ps, sem = open_memory(nc, ctx, keep["sems"])
        pt = sb("pt", [1, 2 * NB], I32)
        flat = acc[:, :, :].rearrange("p k t -> p (k t)")
        pages = [flat[:, 2 * FW * i:2 * FW * (i + 1)].rearrange("p (g c) -> p g c", g=2) for i in range(6)]
        kp, vp = pages[0:2], pages[2:6]
        rb = flat[:, 12 * FW:12 * FW + 2 * TT].rearrange("p (j t) -> p j t", j=2)
        V_ROOM = [vp[0], vp[1], vp[2], vp[3], kp[0], kp[1], vp[0], vp[1]]
        sq = sb("o_sq", [P, 2, TT])
        row_of_ones = sb("row_of_ones", [P, TT])
        rg = sb("o_rg", [P, 2, TT])
        KT = [sb(f"KT{p}", [P, H, PAST]) for p in range(2)]
        KN = sb("KN", [P, H, NS])
        QS = sb("QS", [P, H, NS])
        QZ = sb("QZ", [P, NB, H, 32])
        VN = sb("VN", [NS, FW])
        sc = sb("sc", [P, 2, NK])
        smx = sb("smx", [P, 2])
        snm = sb("snm", [P, 2])
        ssum = sb("ssum", [P, 2])
        srl = sb("srl", [P, 2])
        sfac = sb("sfac", [P, 3])
        PT = sb("PT", [P, 2, 2, P])
        PTN = sb("PTN", [NS, 2, P])
        OV = sb("OV", [P, 2, FW])
        trs = [ps(f"trs{p}", [P, 512]) for p in range(2)]
        Sg = [ps(f"Sg{g}", [P, 512]) for g in range(2)]
        ptp = ps("ptp", [P, 512])
        opv = [ps(f"opv{g}", [P, 512]) for g in range(2)]
        ms = opv + [ps("o_ms", [P, 512])]

        table_in = sem("table_in")
        news_in = sem("news_in")
        k_in = [sem(f"k_in{p}") for p in range(2)]
        v_in = [sem(f"v_in{s}") for s in range(NB)]
        o_in = [sem(f"o_in{j}") for j in range(H)]
        rg_in = [sem(f"rg_in{p}") for p in range(2)]
        sq_ready = sem("o_sq_ready")
        ms_ready = sem("o_ms_ready")
        ln_ready = sem("o_ln_ready")
        rb_ready = sem("o_rb_ready")
        on_ready = sem("on_ready")
        hi_ready = sem("o_hi_ready")
        o_clear = sem("o_clear")
        tr_ready = sem("str_ready")
        tr_free = [sem(f"str_free{p}") for p in range(2)]
        qz_ready = sem("qz_ready")
        sg_ready = sem("sg_ready")
        smx_ready = sem("smx_ready")
        sx_ready = sem("sx_ready")
        p_ready = sem("p_ready")
        pt_ready = sem("pt_ready")
        pt_free = sem("pt_free")
        pv_ready = sem("spv_ready")
        ov_ready = sem("ov_ready")
        ot_ready = sem("ot_ready")

        clear_last(nc, keep)
        with nc.Block() as block:
            @block.sync
            def _(sp):
                sp.dma_start(pt[:, :], io["page_table"].rearrange("(o b) n -> o (b n)", o=1)).then_inc(table_in, 16)
                sp.dma_start(QS[:, :, :], io["q_d"].rearrange("h p t -> p h t")[:, :, T:TT]).then_inc(news_in, 16)
                sp.dma_start(KN[:, :, :], io["k_d"].rearrange("h p t -> p h t")[:, :, T:TT]).then_inc(news_in, 16)
                sp.dma_start(VN[:, :], io["v_sample"].rearrange("t h c -> t (h c)")).then_inc(news_in, 16)
                sp.wait_ge(table_in, 16)
                for s in range(NB):
                    if s >= 2:
                        sp.wait_ge(tr_ready, 2 * (s - 2) + 2)
                    for g in range(2):
                        page = sp.value_load(pt[0:1, 2 * s + g:2 * s + g + 1], min_val=0, max_val=io["cache_k"].shape[1] - 1)
                        sp.dma_start(kp[s % 2][:, g, :], io["cache_k"][0].rearrange("n p h m d -> n p (h m d)")[bass.ds(page, 1)].rearrange("o p c -> p (o c)"))\
                          .then_inc(k_in[s % 2], 16)
                for s in range(NB):
                    if 4 <= s < 6:
                        sp.wait_ge(tr_ready, 2 * (s + 2) + 2)
                    if s >= 6:
                        sp.wait_ge(pv_ready, s - 5)
                    for g in range(2):
                        page = sp.value_load(pt[0:1, 2 * s + g:2 * s + g + 1], min_val=0, max_val=io["cache_v"].shape[1] - 1)
                        sp.dma_start(V_ROOM[s][:, g, :], io["cache_v"][0].rearrange("n p h c -> n p (h c)")[bass.ds(page, 1)].rearrange("o p c -> p (o c)"))\
                          .then_inc(v_in[s], 16)

            @block.gpsimd
            def _(pool):
                tt = nc.gpsimd.tensor_tensor

                def square(j):
                    pool.wait_ge(o_in[j // 2], 16)
                    if j >= 2:
                        pool.wait_ge(ms_ready, NPC * (j - 1))
                    tt(sq[:, j % 2, :], O[:, j, :], O[:, j, :], ALU.mult).then_inc(sq_ready, 1)

                def high(j):
                    pool.wait_ge(on_ready, j + 1)
                    tt(hh[:, j, :], O[:, j, :], row_of_ones[:, :], ALU.mult).then_inc(hi_ready, 1)

                pool.wait_ge(o_clear, 2)
                square(0), square(1)
                for j in range(0, 2 * H, 2):
                    if j + 2 < 2 * H:
                        square(j + 2), square(j + 3)
                    high(j), high(j + 1)

            @block.tensor
            def _(pe):
                mm = nc.tensor.matmul

                def sums(j):
                    pe.wait_ge(sq_ready, j + 1)
                    for n in range(NPC):
                        if j:
                            pe.wait_ge(ln_ready, (j - 1) * NPC + n + 1)
                        mm(ms[n][:, 0:PW], keep["ones"][:, :], sq[:, j % 2, piece(n)], start=True, stop=True).then_inc(ms_ready, 1)

                for s in range(NB):
                    pe.wait_ge(k_in[s % 2], 32 * (s // 2 + 1))
                    for g in range(2):
                        if s:
                            pe.wait_ge(tr_free[g], s)
                        for h in range(H):
                            last = nc.tensor.transpose(trs[g][:, h * P:(h + 1) * P], kp[s % 2][:, g, h * P:(h + 1) * P], keep["ident"][:, :])
                        last.then_inc(tr_ready, 1)
                    if s == 0:
                        pe.wait_ge(qz_ready, 1)
                        pe.wait_ge(news_in, 48)
                    for g in range(2):
                        pe.wait_ge(tr_free[g], s + 1)
                    rows = slice(32 * (s % 4), 32 * (s % 4) + 32)
                    for h in range(H):
                        mm(Sg[s // 4][rows, 0:PAST], QZ[:, s, h, :], KT[s % 2][:, h, :], start=(h == 0), stop=(h == H - 1), tile_position=(0, rows.start))
                    for h in range(H):
                        last = mm(Sg[s // 4][rows, PAST:NK], QZ[:, s, h, :], KN[:, h, :], start=(h == 0), stop=(h == H - 1), tile_position=(0, rows.start))
                    last.then_inc(sg_ready, 1)
                    if s:
                        sums(s - 1)
                sums(NB - 1)
                for g in range(2):
                    pe.wait_ge(p_ready, g + 1)
                    if g:
                        pe.wait_ge(pt_free, 1)
                    nc.tensor.transpose(ptp[:, 0:P], sc[:, g, 0:P], keep["ident"][:, :])
                    nc.tensor.transpose(ptp[:, P:2 * P], sc[:, g, P:2 * P], keep["ident"][:, :])
                    nc.tensor.transpose(ptp[0:NS, 2 * P:3 * P], sc[:, g, PAST:NK], keep["ident"][:, :]).then_inc(pt_ready, 1)
                for g in range(2):
                    pe.wait_ge(pt_free, g + 1)
                    pe.wait_ge(ln_ready, 2 * H * NPC)
                    mm(opv[g][:, :], PTN[:, g, :], VN[:, :], start=True, stop=False)
                    for s in range(4 * g, 4 * g + 4):
                        pe.wait_ge(v_in[s], 32)
                        rows = slice(32 * (s % 4), 32 * (s % 4) + 32)
                        for j in range(2):
                            last = mm(opv[g][rows, :], PT[:, g, j, rows], V_ROOM[s][:, j, :], start=False, stop=(j == 1), tile_position=(0, rows.start))
                        last.then_inc(pv_ready, 1)
                for g in range(2):
                    pe.wait_ge(ov_ready, g + 1)
                    for h in range(H):
                        last = nc.tensor.transpose(trs[g][:, h * P:(h + 1) * P], OV[:, g, h * P:(h + 1) * P], keep["ident"][:, :])
                    last.then_inc(ot_ready, 1)

            @block.scalar
            def _(act):
                a = nc.scalar.activation

                def keys(s):
                    act.wait_ge(tr_ready, 2 * s + 2)
                    if s >= 2:
                        act.wait_ge(sg_ready, s - 1)
                    a(KT[s % 2][:, :, P:2 * P], trs[1][:, :].rearrange("p (h c) -> p h c", h=H), ACT.Copy).then_inc(tr_free[1], 1)

                def log(j):
                    if j >= 2:
                        act.wait_ge(on_ready, j - 1)
                    for n in range(NPC):
                        act.wait_ge(ms_ready, j * NPC + n + 1)
                        a(rb[:, j % 2, piece(n)], ms[n][:, 0:PW], ACT.Ln, bias=keep["eps"][:, 0:1], scale=1.0 / P).then_inc(ln_ready, 1)

                def inverse(j):
                    act.wait_ge(ln_ready, NPC * (j + 1))
                    a(rb[:, j % 2, :], rb[:, j % 2, :], ACT.Exp, scale=-0.5).then_inc(rb_ready, 1)

                def load_outputs(j):
                    n = T if 2 * j < H else TT
                    act.dma_start(O[:, 2 * j:2 * j + 2, 0:n], io["o_d"][2 * j:2 * j + 2].rearrange("h p t -> p h t")[:, :, 0:n]).then_inc(o_in[j], 16)

                def load_gate(i):
                    if i >= 2:
                        act.wait_ge(on_ready, H + i - 1)
                    act.dma_start(rg[:, i % 2, :], io["rg_d"][i]).then_inc(rg_in[i % 2], 16)

                load_outputs(0)
                keys(0)
                load_outputs(1)
                keys(1)
                load_outputs(2), load_outputs(3), load_gate(0), load_gate(1)
                for s in range(2, NB, 2):
                    keys(s)
                    log(s - 2), log(s - 1), inverse(s - 2), inverse(s - 1)
                    keys(s + 1)
                load_gate(2), load_gate(3)
                log(2 * H - 2), log(2 * H - 1), inverse(2 * H - 2), inverse(2 * H - 1)
                for g in range(2):
                    act.wait_ge(smx_ready, g + 1)
                    a(sc[:, g, :], sc[:, g, :], ACT.Exp, bias=snm[:, g:g + 1], accum_out=ssum[:, g:g + 1]).then_inc(sx_ready, 1)

            @block.vector
            def _(dve):
                v = nc.vector
                link = keep["dve_chain"].of(dve)
                v.memset(row_of_ones[:, :], 1.0).then_inc(o_clear, 1)
                v.memset(O[:, 0:H, T:TT], 0.0).then_inc(o_clear, 1)
                link(v.memset(QZ[:, :, :, :], 0.0))
                dve.wait_ge(news_in, 48)
                for h in range(H):
                    for m in range(2):
                        rows, col = slice(m * HD, (m + 1) * HD), 8 * h + 4 * m
                        last = v.tensor_copy(QZ[rows, :, h, col:col + TS], QS[rows, h, :].rearrange("p (b t) -> p b t", t=TS))
                last.then_inc(qz_ready, 1)

                def keys(s):
                    dve.wait_ge(tr_ready, 2 * s + 1)
                    if s >= 2:
                        dve.wait_ge(sg_ready, s - 1)
                    v.tensor_copy(KT[s % 2][:, :, 0:P], trs[0][:, :].rearrange("p (h c) -> p h c", h=H)).then_inc(tr_free[0], 1)

                link(v.tensor_scalar(sfac[:, 0:1], keep["rowsel"][:, 1:2], keep["lam"][:, 1:2], None, ALU.mult))
                link(v.tensor_tensor(sfac[:, 0:1], sfac[:, 0:1], keep["rowsel"][:, 0:1], ALU.add))
                def norm(j):
                    dve.wait_ge(rb_ready, j + 1)
                    gain = vector(keep, "subln_g" if j < H else "hgrn_onorm_g")
                    ins = v.scalar_tensor_tensor(O[:, j, :], O[:, j, :], gain, rb[:, j % 2, :], ALU.mult, ALU.mult)
                    if j >= H:
                        link(ins)
                        dve.wait_ge(rg_in[j % 2], 16 * ((j - H) // 2 + 1))
                        ins = v.tensor_tensor(O[:, j, :], O[:, j, :], rg[:, j % 2, :], ALU.mult)
                    ins.then_inc(on_ready, 1)

                def low(j):
                    dve.wait_ge(hi_ready, j + 1)
                    return v.tensor_tensor(hl[:, j, :], O[:, j, :], hh[:, j, :].bitcast(F32), ALU.subtract)

                for s in range(3):
                    keys(s)
                for s in range(3, NB, 2):
                    j = s - 3
                    keys(s)
                    norm(j), norm(j + 1)
                    if s + 1 < NB:
                        keys(s + 1)
                    low(j), low(j + 1)
                for g in range(2):
                    dve.wait_ge(sg_ready, 4 * g + 4)
                    link(v.tensor_tensor(sc[:, g, :], Sg[g][:, 0:NK], keep["sbias"][:, g, :], ALU.add))
                    link(v.tensor_reduce(smx[:, g:g + 1], sc[:, g, :], AX.X, ALU.max))
                    v.tensor_scalar(snm[:, g:g + 1], smx[:, g:g + 1], -1.0, None, ALU.mult).then_inc(smx_ready, 1)
                norm(2 * H - 2), norm(2 * H - 1)
                for g in range(2):
                    dve.wait_ge(sx_ready, g + 1)
                    link(v.reciprocal(srl[:, g:g + 1], ssum[:, g:g + 1]))
                    link(v.tensor_tensor(sfac[:, 1 + g:2 + g], srl[:, g:g + 1], sfac[:, 0:1], ALU.mult))
                    v.tensor_scalar(sc[:, g, :], sc[:, g, :], sfac[:, 1 + g:2 + g], None, ALU.mult).then_inc(p_ready, 1)
                for g in range(2):
                    dve.wait_ge(pt_ready, g + 1)
                    v.tensor_copy(PT[:, g, :, :], ptp[:, 0:2 * P].rearrange("p (j c) -> p j c", j=2))
                    v.tensor_copy(PTN[:, g, :], ptp[0:NS, 2 * P:3 * P]).then_inc(pt_free, 1)
                for g in range(2):
                    dve.wait_ge(pv_ready, 4 * g + 4)
                    v.tensor_copy(OV[:, g, :], opv[g][:, :]).then_inc(ov_ready, 1)
                low(2 * H - 2)
                link(low(2 * H - 1))
                for g in range(2):
                    dve.wait_ge(ot_ready, g + 1)
                    both = trs[g][:, :].rearrange("p (v b h m t) -> p v h m b t", v=H, b=4, h=H, m=2)
                    for h in range(H):
                        out = O[:, h, T + 16 * g:T + 16 * g + 16].rearrange("p (b t) -> p b t", t=TS)
                        link(v.tensor_copy(out, both[:, h, h, 0]))
                        v.tensor_tensor(out, out, both[:, h, h, 1], ALU.add)


def mix(nc, io, keep, O, hh, hl, acc, total):
    with ExitStack() as ctx:
        sb, ps, sem = open_memory(nc, ctx, keep["sems"])
        raw = sb("m_raw", [P, 2, KC, P])
        whi = [sb(f"m_whi{s}", [P, KC, P], F32R) for s in range(2)]
        wlo = [sb(f"m_wlo{s}", [P, KC, P], F32R) for s in range(2)]
        sq = sb("m_sq", [P, TT])
        rb = sb("m_rb", [P, H, NS])
        zp = [ps(f"m_ps{n}", [P, 512]) for n in range(2 * NPC)]
        ms = ps("m_ms", [P, 512])

        x_back = sem("x_back")
        raw_in = [sem(f"m_raw_in{s}") for s in range(2)]
        w_ready = sem("m_w_ready")
        z_ready = sem("m_z_ready")
        z_free = sem("m_z_free")
        sq_ready = sem("m_sq_ready")
        ms_ready = sem("m_ms_ready")
        rb_ready = sem("m_rb_ready")
        on_ready = sem("m_on_ready")
        hi_ready = sem("m_hi_ready")
        lo_ready = sem("m_lo_ready")
        rsq_ready = sem("rsq_ready")
        total_ready = sem("total_ready")
        w_view = io["w_out"][0].rearrange("(k p) (d c) -> d p k c", p=P, c=P)
        new = slice(T, TT)

        clear_last(nc, keep)
        with nc.Block() as block:
            @block.sync
            def _(sp):
                for s, n in ((w_ready, 2), (z_ready, 2 * NPC), (z_free, 2 * NPC)):
                    sp.sem_inc(s, n)
                def load(d, s):
                    sp.dma_start(raw[:, s, :, :], w_view[d].rearrange("o p k c -> p (o k) c")).then_inc(raw_in[s], 16)

                load(slice(0, 1), 0)
                load(slice(1, 2), 1)
                sp.dma_start(acc[:, :, :], io["x_d"]).then_inc(x_back, 16)
                with sp.Fori(1, KC // 2) as pair:
                    for s in range(2):
                        sp.wait_ge(w_ready, pair * 2 + (s + 1))
                        load(bass.ds(pair * 2 + s, 1), s)

            @block.gpsimd
            def _(pool):
                link = keep["pool_chain"].of(pool)
                with link.loop(KC // 2, 2) as pair:
                    for s in range(2):
                        pool.wait_ge(raw_in[s], pair * 16 + 16)
                        pool.wait_ge(z_ready, pair * (2 * NPC) + NPC * (s + 1))
                        split_weights(nc, keep["ones"][:, :], raw[:, s, :, :], whi[s][:, :, :], wlo[s][:, :, :], link).then_inc(w_ready, 1)

            @block.tensor
            def _(pe):
                pe.wait_ge(sq_ready, 1)
                nc.tensor.matmul(ms[:, 0:H * NS], keep["ones"][:, :], sq[:, 0:H * NS], start=True, stop=True).then_inc(ms_ready, 1)
                with pe.Fori(0, KC // 2) as pair:
                    for s in range(2):
                        pe.wait_ge(w_ready, pair * 2 + (s + 3))
                        for n in range(NPC):
                            if n == NPC - 1:
                                pe.wait_ge(lo_ready, 1)
                            pe.wait_ge(z_free, pair * (2 * NPC) + (NPC * s + n + 1))
                            split_product(nc, zp[NPC * s + n][:, 0:PW], whi[s], wlo[s], hh[:, :, piece(n)], hl[:, :, piece(n)]).then_inc(z_ready, 1)

            @block.scalar
            def _(act):
                a = nc.scalar.activation
                link = keep["act_chain"].of(act)
                a(sq[:, 0:H * NS].rearrange("p (h t) -> p h t", h=H), O[:, 0:H, new], ACT.Square).then_inc(sq_ready, 1)
                act.wait_ge(ms_ready, 1)
                link(a(rb[:, :, :], ms[:, 0:H * NS].rearrange("p (h t) -> p h t", h=H), ACT.Ln, bias=keep["eps"][:, 0:1], scale=1.0 / P))
                a(rb[:, :, :], rb[:, :, :], ACT.Exp, scale=-0.5).then_inc(rb_ready, 1)
                act.wait_ge(on_ready, 1)
                a(hh[:, 0:H, new], O[:, 0:H, new], ACT.Copy).then_inc(hi_ready, 1)
                with act.Fori(0, KC) as d:
                    act.wait_ge(z_free, d * NPC + 3 * NPC)
                    act.wait_ge(total_ready, d + 1)
                    a(sq[:, :], acc[:, bass.ds(d, 1), :].rearrange("p o t -> p (o t)"), ACT.Square).then_inc(rsq_ready, 1)

            @block.vector
            def _(dve):
                v = nc.vector
                v.memset(total[:, :], 0.0).then_inc(total_ready, 1)
                dve.wait_ge(rb_ready, 1)
                v.scalar_tensor_tensor(O[:, 0:H, new], O[:, 0:H, new], vector(keep, "subln_g"), rb[:, :, :], ALU.mult, ALU.mult).then_inc(on_ready, 1)
                dve.wait_ge(hi_ready, 1)
                v.tensor_tensor(hl[:, 0:H, new], O[:, 0:H, new], hh[:, 0:H, new].bitcast(F32), ALU.subtract).then_inc(lo_ready, 1)
                dve.wait_ge(x_back, 16)
                with dve.Fori(0, KC // 2) as pair:
                    for s in range(2):
                        d = pair * 2 + s
                        for n in range(NPC):
                            dve.wait_ge(z_ready, pair * (2 * NPC) + (NPC * s + 2 * NPC + n + 1))
                            row = acc[:, bass.ds(d, 1), piece(n)].rearrange("p o t -> p (o t)")
                            v.tensor_tensor(row, row, zp[NPC * s + n][:, 0:PW], ALU.add).then_inc(z_free, 1)
                        dve.wait_ge(rsq_ready, pair * 2 + (s + 1))
                        dve.wait_ge(total_ready, pair * 2 + (s + 1))
                        v.tensor_tensor(total[:, :], total[:, :], sq[:, :], ALU.add).then_inc(total_ready, 1)


LAST = [("piece", 0), ("piece", 1), ("tile", 0), ("tile", 1), ("piece", 2)] + [("tile", t) for t in range(2, NT + 1)]
G2 = 2
GROUPS = FC // G2
DN_FIRST, DN_PER = 2, 2 + KC * NPC // 2


def mlp(nc, io, keep, acc, total):
    with ExitStack() as ctx:
        sb, ps, sem = open_memory(nc, ctx, keep["sems"])
        hh = sb("f_hi", [P, KC, TT], F32R)
        hl = sb("f_lo", [P, KC, TT], F32R)
        raw = sb("f_raw", [P, 3, KC, P])
        names = ("g0", "u0", "g1", "u1", "d0", "d1")
        whi = {n: sb(f"f_whi_{n}", [P, KC, P], F32R) for n in names}
        wlo = {n: sb(f"f_wlo_{n}", [P, KC, P], F32R) for n in names}
        ahi = [sb(f"f_ahi{c}", [P, TT], F32R) for c in range(G2)]
        alo = [sb(f"f_alo{c}", [P, TT], F32R) for c in range(G2)]
        cp = sb("f_cp", [P, 2, TT])
        conv, prod = cp[:, 0, :], cp[:, 1, :]
        gate = sb("f_gate", [P, TT + 2])
        gsm = sb("f_gsm", [P, NB, TS + 2])
        rb = total
        scr = sb("f_scr", [P, P])
        g18 = sb("f_g18", [P, 2 + 2 * NB])
        cout = sb("f_cout", [2 + 2 * NB, P])
        gp = [ps(f"f_gp{n}", [P, 512]) for n in range(NPC)]
        up = [ps(f"f_up{n}", [P, 512]) for n in range(NPC)]
        dn = [ps(f"f_dn{n}", [P, 512]) for n in range(2)]
        yp = [gp[0:2], up[0:2]]
        ybuf = [cp[:, p, 0:D] for p in range(2)] + [raw[:, p, :, :].rearrange("p k c -> p (k c)") for p in range(3)]

        ms_ready, rb_ready = sem("f_ms_ready"), sem("f_rb_ready")
        hf_ready, hi_ready, lo_ready = sem("f_hf_ready"), sem("f_hi_ready"), sem("f_lo_ready")
        raw_in = [sem(f"f_raw_in{s}") for s in range(3)]
        w_ready = sem("f_w_ready")
        scr_clear, scr_in = sem("scr_clear"), sem("scr_in")
        g_ready, g_free = sem("g_ready"), sem("g_free")
        gs_ready = sem("gs_ready")
        u_ready, u_free = sem("u_ready"), sem("u_free")
        c_ready, s_ready = sem("c_ready"), sem("f_s_ready")
        g18_ready = sem("g18_ready")
        dn_ready = [sem(f"dn_ready{b}") for b in range(2)]
        dn_free = [sem(f"dn_free{b}") for b in range(2)]
        ah_ready, al_ready = sem("ah_ready"), sem("al_ready")
        conv_stored = sem("conv_stored")
        y_ready = [sem(f"y_ready{b}") for b in range(2)]
        y_free = [sem(f"y_free{b}") for b in range(2)]
        y_stored = [sem(f"y_stored{p}") for p in range(5)]

        g_view = io["w_gate"][0].rearrange("(k p) (c f) -> c p k f", p=P, f=P)
        u_view = io["w_up"][0].rearrange("(k p) (c f) -> c p k f", p=P, f=P)
        d_view = io["w_down"][0].rearrange("(c p) (k f) -> c p k f", p=P, f=P)
        s_view = io["state_conv"][0].rearrange("b j (c f) -> c (b j) f", f=P)
        cp_view = io["conv_prompt"].rearrange("j (c f) -> c j f", f=P)
        cs_view = io["conv_sample"].rearrange("b j (c f) -> c (b j) f", f=P)
        W0 = 6

        def part(view, i):
            return view[bass.ds(i, 1)].rearrange("o p k f -> p (o k) f")

        def rows(view, i):
            return view[bass.ds(i, 1)].rearrange("o r f -> r (o f)")

        def dn_use(g, first, k):
            return k + 1 if first else g * DN_PER + (DN_FIRST - DN_PER + k + 1)

        clear_last(nc, keep)
        with nc.Block() as block:
            @block.sync
            def _(sp):
                for s, n in ((w_ready, W0), (dn_free[0], 1), (dn_free[1], 1), (g_free, NPC), (u_free, NPC), (g_ready, 2 * NPC),
                             (u_ready, 2 * NPC), (conv_stored, 32), (al_ready, 2), (c_ready, 1), (s_ready, 1), (gs_ready, 1), (g18_ready, 1)):
                    sp.sem_inc(s, n)
                sp.wait_ge(scr_clear, 1)
                with sp.Fori(0, GROUPS) as g:
                    for k, (n, view) in enumerate(zip(names, (g_view, u_view, g_view, u_view, d_view, d_view))):
                        c = g * G2 + (k // 2 if k < 4 else k - 4)
                        sp.wait_ge(w_ready, g * 6 + (k + W0 - 2))
                        sp.dma_start(raw[:, k % 3, :, :], part(view, c)).then_inc(raw_in[k % 3], 16)
                        if k in (0, 2):
                            sp.wait_ge(gs_ready, g * 2 + (k // 2 + 1))
                            sp.dma_start(scr[0:2 * NB, :], rows(s_view, c)).then_inc(scr_in, 16)

            @block.gpsimd
            def _(pool):
                link = keep["pool_chain"].of(pool)
                nc.gpsimd.memset(scr[:, :], 0.0).then_inc(scr_clear, 1)
                with link.loop(GROUPS, 6) as g:
                    for k, n in enumerate(names):
                        pool.wait_ge(raw_in[k % 3], g * 32 + 16 * (k // 3 + 1))
                        if n[0] == "g":
                            pool.wait_ge(g_ready, g * (2 * NPC) + NPC * (k // 2 + 1))
                        elif n[0] == "u":
                            pool.wait_ge(u_ready, g * (2 * NPC) + NPC * (k // 2 + 1))
                        elif n == "d0":
                            pool.wait_ge(g_ready, g * (2 * NPC) + (2 * NPC + NPC + 1))
                        split_weights(nc, keep["ones"][:, :], raw[:, k % 3, :, :], whi[n][:, :, :], wlo[n][:, :, :], link).then_inc(w_ready, 1)

            @block.tensor
            def _(pe):
                for n in range(NPC):
                    nc.tensor.matmul(gp[n][:, 0:PW], keep["ones"][:, :], total[:, piece(n)], start=True, stop=True).then_inc(ms_ready, 1)

                def group(g, first):
                    def branch(c, b):
                        banks, ready, free = ((gp, g_ready, g_free), (up, u_ready, u_free))[b]
                        n = names[2 * c + b]
                        pe.wait_ge(w_ready, g * 6 + (2 * c + b + 1 + W0))
                        for i in range(NPC):
                            if first and c == 0 and b == 0:
                                pe.wait_ge(lo_ready, KC * (i + 1))
                            pe.wait_ge(free, g * (2 * NPC) + (NPC * c + i + 1))
                            split_product(nc, banks[i][:, 0:PW], whi[n], wlo[n], hh[:, :, piece(i)], hl[:, :, piece(i)]).then_inc(ready, 1)

                    def old_gates(c):
                        k = 0 if c == 0 else (1 if first else 1 + KC * NPC // 2)
                        pe.wait_ge(scr_in, g * 32 + 16 * (c + 1))
                        pe.wait_ge(dn_free[0], dn_use(g, first, k))
                        nc.tensor.transpose(dn[0][:, 0:P], scr[:, :], keep["ident"][:, :]).then_inc(dn_ready[0], 1)

                    def last_gates(c):
                        k = 0 if c == 0 else (1 if first else 1 + KC * NPC // 2)
                        pe.wait_ge(g18_ready, g * 2 + (c + 2))
                        pe.wait_ge(dn_free[1], dn_use(g, first, k))
                        nc.tensor.transpose(dn[1][0:2 + 2 * NB, 0:P], g18[:, :], keep["ident"][:, :]).then_inc(dn_ready[1], 1)

                    old_gates(0)
                    branch(0, 0)
                    branch(0, 1)
                    last_gates(0)
                    if not first:
                        down(g)
                    old_gates(1)
                    branch(1, 0)
                    branch(1, 1)
                    last_gates(1)

                def down_unit(g, first, j, d, n):
                    b = j % 2
                    pe.wait_ge(dn_free[b], dn_use(g, False, first + j // 2))
                    out = dn[b][:, 0:PW]
                    for c in range(G2):
                        w = f"d{c}"
                        nc.tensor.matmul(out, whi[w][:, d, :], ahi[c][:, piece(n)], start=(c == 0), stop=False)
                        nc.tensor.matmul(out, whi[w][:, d, :], alo[c][:, piece(n)], start=False, stop=False)
                        last = nc.tensor.matmul(out, wlo[w][:, d, :], ahi[c][:, piece(n)], start=False, stop=(c == G2 - 1))
                    last.then_inc(dn_ready[b], 1)

                def down(g):
                    pe.wait_ge(w_ready, g * 6 + W0)
                    pe.wait_ge(al_ready, g * 2 + 2)
                    for j in range(KC * NPC):
                        down_unit(g, 1, j, *divmod(j, NPC))

                group(0, True)
                with pe.Fori(1, GROUPS) as g:
                    group(g, False)
                pe.wait_ge(w_ready, GROUPS * 6 + W0)
                pe.wait_ge(al_ready, GROUPS * 2 + 2)
                for kind, i in LAST:
                    if kind == "piece":
                        for d in range(KC):
                            down_unit(GROUPS, 0, i * KC + d, d, i)
                    else:
                        w = P if i < NT else NS
                        pieces = min(-(-(i + 1) * P // PW), NPC)
                        for b in range(2):
                            pe.wait_ge(dn_free[b], dn_use(GROUPS, False, pieces * KC // 2))
                        for b in range(2):
                            if i >= 2:
                                pe.wait_ge(y_free[b], i - 1)
                            for j in range(4):
                                last = nc.tensor.transpose(yp[i % 2][b][0:w, j * P:(j + 1) * P], acc[:, 4 * b + j, i * P:i * P + w], keep["ident"][:, :])
                            last.then_inc(y_ready[b], 1)

            @block.scalar
            def _(act):
                a = nc.scalar.activation
                link = keep["act_chain"].of(act)
                norm_inverse(nc, act, keep["eps"], gp, rb, ms_ready, rb_ready, link)
                norm_high(nc, act, gate[:, 0:TT].rearrange("p (s w) -> p s w", s=NPC), hh, hf_ready, hi_ready)

                def group(g, first):
                    def old_gates(c):
                        k = 0 if c == 0 else (1 if first else 1 + KC * NPC // 2)
                        act.wait_ge(c_ready, g * 2 + (c + 1))
                        act.wait_ge(g18_ready, g * 2 + (c + 1))
                        act.wait_ge(dn_ready[0], dn_use(g, first, k))
                        a(gsm[:, :, 0:2], dn[0][:, 0:2 * NB].rearrange("p (b j) -> p b j", j=2), ACT.Copy).then_inc(dn_free[0], 1)

                    def gates(c):
                        for i in range(NPC):
                            act.wait_ge(g_ready, g * (2 * NPC) + (2 * NPC + NPC * c + i + 1))
                            if first and c == 0 and i == 0:
                                act.wait_ge(lo_ready, KC * NPC)
                            lo, hi = i * PW, min((i + 1) * PW, T)
                            if i == NPC - 1:
                                a(gsm[:, :, 2:2 + TS], gp[i][:, hi - lo:PW].rearrange("p (b t) -> p b t", t=TS), ACT.Copy).then_inc(gs_ready, 1)
                            a(gate[:, 2 + lo:2 + hi], gp[i][:, 0:hi - lo], ACT.Copy).then_inc(g_free, 1)

                    def last_gates(c):
                        k = 0 if c == 0 else (1 if first else 1 + KC * NPC // 2)
                        act.wait_ge(dn_ready[1], dn_use(g, first, k))
                        act.wait_ge(conv_stored, g * 64 + 32 * (c + 1))
                        a(cout[:, :], dn[1][0:2 + 2 * NB, 0:P], ACT.Copy).then_inc(dn_free[1], 1)
                        act.wait_ge(dn_free[1], dn_use(g, first, k) + 1)
                        i = g * G2 + c
                        act.dma_start(rows(cp_view, i), cout[0:2, :]).then_inc(conv_stored, 16)
                        act.dma_start(rows(cs_view, i), cout[2:2 + 2 * NB, :]).then_inc(conv_stored, 16)

                    def silu(c):
                        act.wait_ge(c_ready, g * 2 + (c + 2))
                        a(conv, conv, ACT.Silu).then_inc(s_ready, 1)

                    def high(c):
                        act.wait_ge(u_free, g * (2 * NPC) + (NPC * c + 2 * NPC))
                        if c == 0 and not first:
                            act.wait_ge(g_ready, g * (2 * NPC) + (2 * NPC + NPC + 1))
                        a(ahi[c][:, :], prod, ACT.Copy).then_inc(ah_ready, 1)

                    old_gates(0), gates(0), silu(0), last_gates(0)
                    if first:
                        high(0), old_gates(1), gates(1)
                    else:
                        old_gates(1), high(0), gates(1)
                    silu(1), last_gates(1), high(1)

                group(0, True)
                with act.Fori(1, GROUPS) as g:
                    group(g, False)
                for t in range(NT + 1):
                    w = P if t < NT else NS
                    act.wait_ge(y_ready[1], t + 1)
                    if t == 0:
                        act.wait_ge(al_ready, 2 * GROUPS + 2)
                        act.wait_ge(w_ready, GROUPS * 6 + W0)
                    if t >= 5:
                        act.wait_ge(y_stored[t % 5], 16)
                    a(ybuf[t % 5][0:w, 4 * P:8 * P], yp[t % 2][1][0:w, :], ACT.Copy).then_inc(y_free[1], 1)
                    act.wait_ge(y_free[0], t + 1)
                    act.wait_ge(y_free[1], t + 1)
                    dst = io["y_prompt"][0, t * P:(t + 1) * P, :] if t < NT else io["y_sample"].rearrange("b t d -> (b t) d")
                    act.dma_start(dst, ybuf[t % 5][0:w, :]).then_inc(y_stored[t % 5], 16)
                for p in range(5):
                    act.wait_ge(y_stored[p], 32 if p < 4 else 16)
                act.wait_ge(conv_stored, 32 * (FC + 1))

            @block.vector
            def _(dve):
                v = nc.vector
                norm_low(nc, dve, acc, vector(keep, "norm2_g"), rb, gate[:, 0:TT].rearrange("p (s w) -> p s w", s=NPC), hh, hl, rb_ready, hf_ready, hi_ready, lo_ready)
                link = keep["dve_chain"].of(dve)
                dve.wait_ge(lo_ready, KC * NPC)
                link(v.memset(gate[:, 0:2], 0.0))

                def group(g, first, link):
                    def w(j, c):
                        return keep["vec"][:, bass.ds(g * G2 + (VECTORS["conv_w"][0] + j * FC + c), 1)]

                    def convolve(c):
                        bias = keep["vec"][:, bass.ds(g * G2 + (VECTORS["conv_b"][0] + c), 1)]
                        dve.wait_ge(g_free, g * (2 * NPC) + (NPC + NPC * c + NPC))
                        dve.wait_ge(dn_free[1], dn_use(g, first, 0 if c == 0 else (1 if first else 1 + KC * NPC // 2)))
                        v.tensor_copy(g18[:, 0:2], gate[:, T:T + 2])
                        v.tensor_copy(g18[:, 2:2 + 2 * NB].rearrange("p (b j) -> p b j", j=2), gsm[:, :, TS:TS + 2]).then_inc(g18_ready, 1)
                        old = conv[:, T:TT].rearrange("p (b t) -> p b t", t=TS)
                        if not (first and c == 0):
                            dve.wait_ge(ah_ready, g * 2 + c)
                        v.tensor_scalar(conv[:, 0:T], gate[:, 2:T + 2], w(2, c), bias, ALU.mult, ALU.add)
                        link(v.tensor_scalar(old, gsm[:, :, 2:2 + TS], w(2, c), bias, ALU.mult, ALU.add))
                        v.scalar_tensor_tensor(conv[:, 0:T], gate[:, 1:T + 1], w(1, c), conv[:, 0:T], ALU.mult, ALU.add)
                        link(v.scalar_tensor_tensor(old, gsm[:, :, 1:1 + TS], w(1, c), old, ALU.mult, ALU.add))
                        v.scalar_tensor_tensor(conv[:, 0:T], gate[:, 0:T], w(0, c), conv[:, 0:T], ALU.mult, ALU.add)
                        v.scalar_tensor_tensor(old, gsm[:, :, 0:TS], w(0, c), old, ALU.mult, ALU.add).then_inc(c_ready, 1)

                    def multiply(c):
                        dve.wait_ge(s_ready, g * 2 + (c + 2))
                        dve.wait_ge(al_ready, g * 2 + (c + 2))
                        for i in range(NPC):
                            dve.wait_ge(u_ready, g * (2 * NPC) + (2 * NPC + NPC * c + i + 1))
                            v.tensor_tensor(prod[:, piece(i)], conv[:, piece(i)], up[i][:, 0:PW], ALU.mult).then_inc(u_free, 1)

                    def low(c):
                        dve.wait_ge(ah_ready, g * 2 + (c + 1))
                        v.tensor_tensor(alo[c][:, :], prod, ahi[c][:, :].bitcast(F32), ALU.subtract).then_inc(al_ready, 1)

                    convolve(0), multiply(0)
                    if not first:
                        down(g)
                    low(0), convolve(1), multiply(1), low(1)

                def down_unit(g, first, j, d, n):
                    b = j % 2
                    dve.wait_ge(dn_ready[b], dn_use(g, False, first + j // 2))
                    v.tensor_tensor(acc[:, d, piece(n)], acc[:, d, piece(n)], dn[b][:, 0:PW], ALU.add).then_inc(dn_free[b], 1)

                def down(g):
                    for j in range(KC * NPC):
                        down_unit(g, 1, j, *divmod(j, NPC))

                group(0, True, link)
                with link.loop(GROUPS - 1, 4) as g1:
                    group(g1 + 1, False, link)
                for kind, i in LAST:
                    if kind == "piece":
                        for d in range(KC):
                            down_unit(GROUPS, 0, i * KC + d, d, i)
                    else:
                        w = P if i < NT else NS
                        dve.wait_ge(y_ready[0], i + 1)
                        if i == 0:
                            dve.wait_ge(w_ready, GROUPS * 6 + W0)
                        if i >= 5:
                            dve.wait_ge(y_stored[i % 5], 16)
                        v.tensor_copy(ybuf[i % 5][0:w, 0:4 * P], yp[i % 2][0][0:w, :]).then_inc(y_free[0], 1)


def rel_bucket(n):
    n = np.maximum(n, 0)
    exact = N_BUCKETS // 2
    nf = np.maximum(n, 1).astype(np.float32)
    large = exact + (np.log(nf / np.float32(exact)) / np.float32(math.log(MAX_DISTANCE / exact)) * np.float32(N_BUCKETS - exact)).astype(np.int32)
    return np.where(n < exact, n, np.minimum(large, N_BUCKETS - 1))


def one_hot(distance):
    out = np.zeros((N_BUCKETS + 1,) + distance.shape, np.float32)
    b = np.where(distance < 0, N_BUCKETS, rel_bucket(distance))
    for i in range(N_BUCKETS + 1):
        out[i] = b == i
    return out


def constants():
    c = {}
    c["c_ident"] = np.eye(P, dtype=np.float32)
    half = np.arange(P) // HD
    c["c_blk"] = (half[:, None] == half[None, :]).astype(np.float32)
    c["c_dist"] = one_hot(2 * P - 1 - np.arange(BW))
    q = np.arange(TS)[:, None]
    past = PAST + q - np.arange(PAST)[None, :]
    new = q - (np.arange(NS) % TS)[None, :]
    c["c_sdist"] = one_hot(np.concatenate([past, new], 1))
    row = np.arange(P) // 32
    m = np.zeros((P, 2, NK), np.float32)
    for g in range(2):
        other = (4 * g + row)[:, None] != (np.arange(NS) // TS)[None, :]
        m[:, g, PAST:] = np.where(other, np.float32(MASKED), 0)
    c["c_smask"] = m
    s, t = np.arange(P)[:, None], np.arange(P)[None, :]
    lm = np.zeros((P, LEVELS, P), np.int32)
    lm[:, 0] = s == t
    for l in range(1, LEVELS):
        w = 2 ** l
        lm[:, l] = (s // w == t // w) & (s % w < w // 2) & (t % w >= w // 2)
    c["c_slmask"] = np.ascontiguousarray(lm[0:NS, 0:SLEVELS, 0:NS])
    halves = [lm[:, l].reshape(P, P // 2 ** l, 2, 2 ** l // 2)[:, :, 1].reshape(P, P // 2) for l in range(1, LEVELS)]
    c["c_lmask"] = np.concatenate([lm[:, 0]] + halves, 1)
    c["c_rowmask"] = (np.arange(NS)[:, None] // TS == np.arange(NB)[None, :]).astype(np.float32)
    c["c_rowsel"] = (np.arange(P)[:, None] // TS % 2 == np.arange(2)[None, :]).astype(np.float32)
    return c


INPUTS = ["x_prompt", "x_sample", "cache_k", "cache_v", "page_table", "state_hgrn", "state_conv", "rel_bias",
          "norm1_g", "w_in", "qk_norm_g", "lambda_qk", "subln_g", "hgrn_lb", "hgrn_onorm_g", "w_out",
          "norm2_g", "w_gate", "w_up", "conv_w", "conv_b", "w_down"]
OUTPUTS = [("y_prompt", (1, T, D)), ("y_sample", (NB, TS, D)), ("k_prompt", (T, H, P)), ("v_prompt", (T, H, P)),
           ("hgrn_prompt", (H, P, P)), ("conv_prompt", (2, FF)), ("k_sample", (NS, H, P)), ("v_sample", (NS, H, P)),
           ("hgrn_sample", (NB, H, P, P)), ("conv_sample", (NB, 2, FF))]
SHAPES = [(1, T, D), (NB, TS, D), (1, 1, T, H, 2, HD), (1, 1, T, H, P), (1, 1, H, P, P), (1, 1, 2, FF),
          (1, NB, TS, H, 2, HD), (1, NB, TS, H, P), (1, NB, H, P, P), (1, NB, 2, FF)]
SCRATCH = [("skew", (H, P, BW)), ("x_d", (P, KC, TT)), ("q_d", (H, P, TT)), ("k_d", (H, P, TT)), ("rq_d", (H, P, TT)),
           ("kk_d", (H, P, TT)), ("b_d", (H, P, TT)), ("qd_d", (H, P, TT)), ("kd_d", (H, P, NT + 1, P)), ("ends_d", (H, P, NT + NB)),
           ("rg_d", (H, P, TT)), ("ri_d", (H, P, NT + 1, P)), ("o_d", (2 * H, P, TT))]


def program(nc, arrays):
    io = {}
    for name, a in arrays.items():
        io[name] = nc.dram_tensor(name, a.shape, mybir.dt.from_np(a.dtype), kind="ExternalInput").ap()
    for name, shape in OUTPUTS:
        io[name] = nc.dram_tensor(name, shape, F32, kind="ExternalOutput").ap()
    for name, shape in SCRATCH:
        io[name] = nc.dram_tensor(name, shape, F32, kind="Internal").ap()
    with ExitStack() as ctx:
        sb = open_memory(nc, ctx, [])[0]
        keep = {n: sb(n, shape, dt) for n, shape, dt in (
            ("ident", [P, P], F32), ("blk", [P, P], F32), ("ones", [P, P], F32), ("eps", [P, 1], F32),
            ("lmask", [P, P + (LEVELS - 1) * P // 2], I32), ("slmask", [NS, SLEVELS, NS], I32), ("rowmask", [NS, NB], F32), ("rowsel", [P, 2], F32), ("bias", [P, H, 2 * P], F32), ("far", [P, H], F32),
            ("sbias", [P, 2, NK], F32), ("lam", [P, 2], F32), ("lb0", [P, H], F32), ("lb1", [P, H], F32),
            ("vec", [P, NVEC], F32))}
        keep["sems"], keep["last"] = [], []
        for name in ("dve", "act", "pool"):
            keep[f"{name}_chain"] = Chain(ctx.enter_context(nc.semaphore(f"{name}_done")))
        keep["x_in"] = [ctx.enter_context(nc.semaphore(f"x_in{g}")) for g in range(3)]
        keep["late_in"] = ctx.enter_context(nc.semaphore("late_in"))
        keep["skewed"] = ctx.enter_context(nc.semaphore("skewed"))
        with ExitStack() as first:
            z_room = first.enter_context(nc.sbuf_tensor("z_room", [P, PARTS, TT], F32))
            tm = first.enter_context(nc.sbuf_tensor("tm", [P, 3, NT + 1, P], F32))
            flat = z_room[:, :, :].rearrange("p c t -> p (c t)")
            x = [flat[:, t * D:(t + 1) * D] for t in range(NT - 1)]
            x += [tm[:, t, 0:KC, :].rearrange("p k c -> p (k c)") for t in range(2)]
            prepare(nc, io, keep, x)
            project(nc, io, keep, x, z_room, tm)
        heads(nc, io, keep)
        acc = sb("residual", [P, KC, TT])
        total = sb("total", [P, TT])
        with ExitStack() as outputs:
            O = outputs.enter_context(nc.sbuf_tensor("O", [P, 2 * H, TT], F32))
            hh = outputs.enter_context(nc.sbuf_tensor("o_hi", [P, 2 * H, TT], F32R))
            hl = outputs.enter_context(nc.sbuf_tensor("o_lo", [P, 2 * H, TT], F32R))
            samples(nc, io, keep, O, hh, hl, acc)
            mix(nc, io, keep, O, hh, hl, acc, total)
        mlp(nc, io, keep, acc, total)


def kernel(**inputs):
    import concourse.bacc as bacc
    from concourse.bass_utils import run_bass_kernel_spmd

    nc = bacc.Bacc("TRN2", target_bir_lowering=False, num_devices=1)
    arrays = {n: np.ascontiguousarray(inputs[n]) for n in INPUTS}
    arrays.update(constants())
    program(nc, arrays)
    r = run_bass_kernel_spmd(nc, [arrays], core_ids=[0])
    return tuple(np.asarray(r.results[0][n]).reshape(s) for (n, _), s in zip(OUTPUTS, SHAPES))
```
